# Optimizing a Trainium2 kernel written in Bass

```python
import jax, jax.numpy as jnp
from jax import lax
import numpy as np

D_MODEL = 1024
BATCH = 1
SEQ = 4096
DEPTH = 1

CHUNK = 64
D_MIX = D_MODEL
ML_WIDTH = D_MIX // 2
ML_HEADS = 4
ML_HEAD_DIM = ML_WIDTH // ML_HEADS
SB_WIDTH = D_MIX - ML_WIDTH
SB_HEADS = 8
SB_HEAD_DIM = SB_WIDTH // SB_HEADS
CONV_K = 4
Q_BLOCK = 128
EPS = 1e-6
IN_SIZES = [2 * ML_WIDTH,
            ML_WIDTH,
            ML_WIDTH,
            ML_WIDTH,
            2 * ML_HEADS,
            SB_WIDTH,
            SB_WIDTH,
            SB_WIDTH,
            SB_WIDTH]
N_IN = sum(IN_SIZES)
IN_SPLITS = [int(s) for s in np.cumsum(IN_SIZES)[:-1]]

kernel_name = "hymba_mlstm_stickbreaking_layer"

def _rmsnorm(x, g):
    xf = x.astype(jnp.float32)
    r = lax.rsqrt(jnp.mean(xf * xf, axis=-1, keepdims=True) + EPS)
    return (xf * r).astype(x.dtype) * g

def _causal_conv(u, w, b):
    C = u.shape[-1]
    out = lax.conv_general_dilated(u, w[:, None, :].astype(u.dtype), window_strides=(1,),
                                   padding=[(CONV_K - 1, 0)],
                                   dimension_numbers=('NWC', 'WIO', 'NWC'),
                                   feature_group_count=C)
    return out + b

def _mlstm(q, k, v, i_pre, f_pre):
    B, S, H, d = q.shape
    nc = S // CHUNK
    L = CHUNK
    f32 = jnp.float32

    def chunked(t):
        t = t.reshape((B, nc, L) + t.shape[2:])
        return jnp.moveaxis(t, 3, 1)

    q = chunked(q).astype(f32)
    k = chunked(k).astype(f32) * (d ** -0.5)
    v = chunked(v).astype(f32)
    ig = chunked(i_pre).astype(f32)
    logf = jax.nn.log_sigmoid(chunked(f_pre).astype(f32))
    b = jnp.cumsum(logf, axis=-1)
    a = b[..., -1]

    g = a[..., None] - b + ig
    m_loc = jnp.max(g, axis=-1)
    w = jnp.exp(g - m_loc[..., None])
    wk = w[..., None] * k
    C_loc = jnp.einsum('bhcsk,bhcsv->bhckv', wk, v)
    n_loc = jnp.sum(wk, axis=-2)

    def step(carry, xs):
        C, n, m = carry
        a_c, m_l, C_l, n_l = xs
        m_new = jnp.maximum(a_c + m, m_l)
        s_old = jnp.exp(a_c + m - m_new)
        s_loc = jnp.exp(m_l - m_new)
        C_new = s_old[..., None, None] * C + s_loc[..., None, None] * C_l
        n_new = s_old[..., None] * n + s_loc[..., None] * n_l
        return (C_new, n_new, m_new), (C, n, m)

    init = (jnp.zeros((B, H, d, d), f32), jnp.zeros((B, H, d), f32), jnp.zeros((B, H), f32))
    xs = (jnp.moveaxis(a, 2, 0), jnp.moveaxis(m_loc, 2, 0),
          jnp.moveaxis(C_loc, 2, 0), jnp.moveaxis(n_loc, 2, 0))
    _, (C_prev, n_prev, m_prev) = lax.scan(step, init, xs)
    C_prev = jnp.moveaxis(C_prev, 0, 2)
    n_prev = jnp.moveaxis(n_prev, 0, 2)
    m_prev = jnp.moveaxis(m_prev, 0, 2)

    causal = jnp.tril(jnp.ones((L, L), dtype=bool))
    Dlog = b[..., :, None] - b[..., None, :] + ig[..., None, :]
    Dlog = jnp.where(causal, Dlog, -jnp.inf)
    inter_log = b + m_prev[..., None]
    m_t = jnp.maximum(inter_log, jnp.max(Dlog, axis=-1))
    Dw = jnp.exp(Dlog - m_t[..., None])
    inter_w = jnp.exp(inter_log - m_t)
    qk = jnp.einsum('bhctd,bhcsd->bhcts', q, k) * Dw
    num = (inter_w[..., None] * jnp.einsum('bhctk,bhckv->bhctv', q, C_prev)
           + jnp.einsum('bhcts,bhcsv->bhctv', qk, v))
    den = inter_w * jnp.einsum('bhctk,bhck->bhct', q, n_prev) + jnp.sum(qk, axis=-1)
    h = num / jnp.maximum(jnp.abs(den), jnp.exp(-m_t))[..., None]
    return jnp.moveaxis(h, 1, 3).reshape(B, S, H, d)

def _stick_breaking(q, k, v):
    B, S, H, d = q.shape
    f32 = jnp.float32
    q = q.astype(f32) * (d ** -0.5)
    k = k.astype(f32)
    v = v.astype(f32)
    outs = []
    for blk in range(S // Q_BLOCK):
        t0 = blk * Q_BLOCK
        t1 = t0 + Q_BLOCK
        qb = q[:, t0:t1]
        kb = k[:, :t1]
        vb = v[:, :t1]
        z = jnp.einsum('bthd,bshd->bhts', qb, kb)
        strict = jnp.arange(t1)[None, :] < jnp.arange(t0, t1)[:, None]
        log_beta = jax.nn.log_sigmoid(z)
        log_keep = jnp.where(strict, jax.nn.log_sigmoid(-z), 0.0)
        after = lax.cumsum(log_keep, axis=3, reverse=True) - log_keep
        A = jnp.where(strict, jnp.exp(log_beta + after), 0.0)
        outs.append(jnp.einsum('bhts,bshd->bthd', A, vb))
    return jnp.concatenate(outs, axis=1)

def setup_inputs(seed: int = 0) -> dict:
    key = jax.random.key(seed)
    ks = jax.random.split(key, 14)
    f32 = jnp.float32
    x = jax.random.normal(ks[0], (BATCH, SEQ, D_MODEL), f32)
    c = jax.random.normal(ks[1], (BATCH, D_MODEL), f32)
    w_ada = jax.random.normal(ks[2], (D_MODEL, 3 * D_MODEL), f32) * (0.5 * D_MODEL ** -0.5)
    b_ada = 0.02 * jax.random.normal(ks[3], (3 * D_MODEL,), f32)
    g_pre = 1.0 + 0.02 * jax.random.normal(ks[4], (D_MODEL,), f32)
    w_in = jax.random.normal(ks[5], (D_MODEL, N_IN), f32) * (D_MODEL ** -0.5)
    b_igate = 0.1 * jax.random.normal(ks[6], (ML_HEADS,), f32)
    b_fgate = jnp.linspace(3.0, 6.0, ML_HEADS, dtype=f32) + 0.02 * jax.random.normal(ks[7], (ML_HEADS,), f32)
    conv_w = jax.random.normal(ks[8], (CONV_K, 2 * ML_WIDTH), f32) * (CONV_K ** -0.5)
    conv_b = 0.02 * jax.random.normal(ks[9], (2 * ML_WIDTH,), f32)
    g_ml_head = 1.0 + 0.02 * jax.random.normal(ks[10], (ML_HEADS, ML_HEAD_DIM), f32)
    w_out = jax.random.normal(ks[11], (D_MIX, D_MODEL), f32) * (D_MIX ** -0.5)
    g_post = 1.0 + 0.02 * jax.random.normal(ks[12], (D_MODEL,), f32)
    return {"x": x, "c": c, "w_ada": w_ada, "b_ada": b_ada, "g_pre": g_pre,
            "w_in": w_in, "b_igate": b_igate, "b_fgate": b_fgate,
            "conv_w": conv_w, "conv_b": conv_b, "g_ml_head": g_ml_head,
            "w_out": w_out, "g_post": g_post}

def reference(x, c, w_ada, b_ada, g_pre, w_in, b_igate, b_fgate, conv_w, conv_b,
              g_ml_head, w_out, g_post):
    B, S, _ = x.shape
    for _layer in range(DEPTH):
        mod = jax.nn.silu(c) @ w_ada + b_ada
        shift, scale, gate = jnp.split(mod, 3, axis=-1)
        h = _rmsnorm(x, g_pre) * (1.0 + scale[:, None, :]) + shift[:, None, :]

        proj = h @ w_in
        (ml_qk, ml_v, ml_o, ml_z, ml_gates,
         sb_q, sb_k, sb_v, sb_z) = jnp.split(proj, IN_SPLITS, axis=-1)

        ml_qk = jax.nn.silu(_causal_conv(ml_qk, conv_w, conv_b))
        ml_q, ml_k = jnp.split(ml_qk, 2, axis=-1)
        i_pre = ml_gates[..., :ML_HEADS] + b_igate
        f_pre = ml_gates[..., ML_HEADS:] + b_fgate
        hs = (B, S, ML_HEADS, ML_HEAD_DIM)
        h_ml = _mlstm(ml_q.reshape(hs), ml_k.reshape(hs), ml_v.reshape(hs), i_pre, f_pre)
        h_ml = jax.nn.sigmoid(ml_o.reshape(hs).astype(jnp.float32)) * h_ml
        h_ml = _rmsnorm(h_ml, g_ml_head).reshape(B, S, ML_WIDTH)
        h_ml = h_ml.astype(x.dtype) * jax.nn.silu(ml_z)

        ss = (B, S, SB_HEADS, SB_HEAD_DIM)
        h_sb = _stick_breaking(sb_q.reshape(ss), sb_k.reshape(ss), sb_v.reshape(ss))
        h_sb = h_sb.reshape(B, S, SB_WIDTH).astype(x.dtype) * jax.nn.silu(sb_z)

        y = jnp.concatenate([h_ml, h_sb], axis=-1) @ w_out
        x = x + gate[:, None, :] * _rmsnorm(y, g_post)
    return x


_drawn_inputs = setup_inputs


def setup_inputs(seed=0):
    import zlib

    import numpy as np

    out = dict(_drawn_inputs(seed))
    spreads = {}
    factors = {'g_pre': 6.729, 'b_igate': 200.0, 'conv_b': 172.073, 'g_ml_head': 94.355, 'g_post': 77.918}
    for name, (base, spread) in spreads.items():
        noise = np.random.default_rng([zlib.crc32(name.encode()), seed]).standard_normal(out[name].shape)
        drawn = base * np.exp(spread * noise) if base else spread * noise
        out[name] = __import__('jax').numpy.asarray(drawn.astype(out[name].dtype))
    for name, factor in factors.items():
        out[name] = (out[name] * factor).astype(out[name].dtype)
    return out
```

```python
import concourse.bass as bass
from concourse import mybir
from contextlib import ExitStack

F32 = mybir.dt.float32
F32R = mybir.dt.float32r
BF16 = mybir.dt.bfloat16
ALU = mybir.AluOpType
ACT = mybir.ActivationFunctionType

P = 128
D = 1024
S = 4096
KT = D // P
CH = 512
NCH = S // CH
TPC = CH // P
NT = S // P
MH, MD = 4, 128
SH, SD = 8, 64
EPS = 1e-6
K_SCALE = float(MD) ** -0.5
Z_SCALE = float(SD) ** -0.5
BIG = 1.0e30

C_QK, C_V, C_O, C_Z, C_G = 0, 1024, 1536, 2048, 2560
C_SQ, C_SK, C_SV, C_SZ = 2568, 3080, 3592, 4104


class Count:

    def __init__(self, start=0):
        self.now, self.reg, self.per = start, None, 0

    def enter(self, reg, per):
        self.first, self.reg, self.per = self.now, reg, per

    def leave(self, trips):
        assert self.now - self.first == self.per, (self.now - self.first, self.per)
        self.now, self.reg = self.first + self.per * trips, None

    def value(self, more=0):
        if self.reg is None or not self.per:
            return self.now + more
        return self.reg * self.per + (self.now + more)

    def up(self, k=1):
        self.now += k
        return self.value()


def identity(pool, tile, sem, n):
    pool.memset(tile, 0.0).then_inc(sem, 1)
    pool.wait_ge(sem, n + 1)
    pool.affine_select(out=tile, in_=tile, compare_op=ALU.not_equal, fill=1.0, base=0,
                       pattern=[[-1, P]], channel_multiplier=1).then_inc(sem, 1)


def stage_norm(nc, x, c, w_ada, b_ada, g_pre, g_post, hT_d, gg_d):
    NB = 3 * D // CH
    with ExitStack() as ctx:
        sb = lambda n, s, d=F32: ctx.enter_context(nc.sbuf_tensor("n_" + n, s, d))
        ps = lambda n, s, d=F32: ctx.enter_context(nc.psum_tensor("n_" + n, s, d))
        sem = lambda n: ctx.enter_context(nc.semaphore("n_" + n))
        wada = sb("wada", [P, NB, KT, CH])
        ccol, csig, csil = sb("ccol", [P, KT]), sb("csig", [P, KT]), sb("csil", [P, KT])
        gcol, acol, shcol = sb("gcol", [P, KT]), sb("acol", [P, KT]), sb("shcol", [P, KT])
        brow, mrow = sb("brow", [1, 3 * D]), sb("mrow", [1, 3 * D])
        gprow, ggrow, one = sb("gprow", [1, D]), sb("ggrow", [1, D]), sb("one", [1, 1])
        ident = sb("ident", [P, P])
        xt = sb("xt", [P, 2, TPC, D])
        xn = sb("xn", [P, TPC, D])
        sq = sb("sq", [P, TPC, D], BF16)
        ss, var, rt, r0, r1, r2, rr = (sb(n, [P, TPC]) for n in ("ss", "var", "rt", "r0", "r1", "r2", "rr"))
        hout = sb("hout", [P, KT, CH])
        bank = [ps(f"bank{k}", [P, CH]) for k in range(8)]

        x_in = [sem("x_in0"), sem("x_in1")]
        small_in, w_in = sem("small_in"), [sem(f"w_in{b}") for b in range(NB)]
        id_ready, csig_ready, csil_ready = sem("id_ready"), sem("csig_ready"), sem("csil_ready")
        row_done, mrow_ready, col_done, col_ready = sem("row_done"), sem("mrow_ready"), sem("col_done"), sem("col_ready")
        gg_ready, gg_out = sem("gg_ready"), sem("gg_out")
        ss_ready, var_ready, rt_ready, r_step, xn_ready = sem("ss_ready"), sem("var_ready"), sem("rt_ready"), sem("r_step"), sem("xn_ready")
        tr_done, a_evac, v_evac, h_out = sem("tr_done"), sem("a_evac"), sem("v_evac"), sem("h_out")
        block = ctx.enter_context(nc.Block())
        x_v = x.rearrange("b (n i p) d -> (b n) p i d", i=TPC, p=P)

        @block.sync
        def _(sp):
            sp.dma_start(ccol[:], c.rearrange("b (k p) -> p (b k)", p=P), allow_slow_non_contiguous=True).then_inc(small_in, 16)
            sp.dma_start(gcol[:], g_pre.rearrange("(k p) -> p k", p=P), allow_slow_non_contiguous=True).then_inc(small_in, 16)
            sp.dma_start(brow[:], b_ada.rearrange("(a n) -> a n", a=1)).then_inc(small_in, 16)
            sp.dma_start(gprow[:], g_post.rearrange("(a n) -> a n", a=1)).then_inc(small_in, 16)
            for p in range(2):
                sp.dma_start(xt[:, p], x_v[p]).then_inc(x_in[p], 16)
            for b in range(NB):
                sp.dma_start(wada[:, b], w_ada[:, b * CH:(b + 1) * CH].rearrange("(k p) n -> p k n", p=P)).then_inc(w_in[b], 16)
            def pair(i, ahead):
                for p in range(2):
                    if ahead:
                        sp.wait_ge(xn_ready, 2 * TPC * i + TPC * (p + 1))
                        sp.dma_start(xt[:, p], x_v[2 * i + (2 + p)]).then_inc(x_in[p], 16)
                    sp.wait_ge(a_evac, KT * i + KT // 2 * (p + 2))
                    sp.wait_ge(v_evac, KT * i + KT // 2 * (p + 2))
                    sp.dma_start(hT_d[2 * i + p], hout[:]).then_inc(h_out, 16)

            with sp.Fori(0, NCH // 2 - 1) as i:
                pair(i, True)
            pair(NCH // 2 - 1, False)
            sp.wait_ge(h_out, 16 * NCH + 16)
            sp.dma_start(hT_d[NCH], hT_d[0]).then_inc(h_out, 16)
            sp.wait_ge(gg_ready, 1)
            sp.dma_start(gg_d, ggrow[:]).then_inc(gg_out, 16)
            sp.wait_ge(gg_out, 16)
            sp.wait_ge(h_out, 16 * NCH + 32)

        @block.gpsimd
        def _(pool):
            identity(pool, ident[:], id_ready, 0)
            pool.memset(one[:], 1.0).then_inc(id_ready, 1)

        @block.scalar
        def _(act):
            act.sem_inc(a_evac, KT // 2)
            act.wait_ge(small_in, 64)
            act.activation(csig[:], ccol[:], ACT.Sigmoid).then_inc(csig_ready, 1)
            with act.Fori(0, NCH // 2) as i:
                for p in range(2):
                    act.wait_ge(x_in[p], 16 * i + 16)
                    for t in range(TPC):
                        act.activation(sq[:, t], xt[:, p, t], ACT.Square, accum_out=ss[:, t:t + 1]).then_inc(ss_ready, 1)
                    act.wait_ge(var_ready, 2 * i + p + 1)
                    act.activation(rt[:], var[:], ACT.Sqrt).then_inc(rt_ready, 1)
                    act.wait_ge(col_ready, 2)
                    for k in range(0, KT, 2):
                        act.wait_ge(tr_done, 2 * KT * i + KT * (p + 1) + k + 1)
                        if k == 0:
                            act.wait_ge(h_out, 32 * i + 16 * p + 16)
                        act.activation(hout[:, k], bank[k][:], ACT.Identity, bias=shcol[:, k:k + 1],
                                       scale=acol[:, k:k + 1]).then_inc(a_evac, 1)

        @block.vector
        def _(dve):
            dve.sem_inc(h_out, 16)
            dve.sem_inc(v_evac, KT // 2)
            dve.wait_ge(small_in, 64)
            dve.wait_ge(csig_ready, 1)
            dve.tensor_tensor(csil[:], csig[:], ccol[:], ALU.mult).then_inc(csil_ready, 1)
            for b in range(NB):
                dve.wait_ge(row_done, b + 1)
                dve.tensor_tensor(mrow[0:1, b * CH:(b + 1) * CH], bank[b][0:1, :], brow[0:1, b * CH:(b + 1) * CH],
                                  ALU.add).then_inc(mrow_ready, 1)
            dve.wait_ge(mrow_ready, NB)
            dve.tensor_tensor(ggrow[:], mrow[0:1, 2 * D:3 * D], gprow[:], ALU.mult).then_inc(gg_ready, 1)
            dve.wait_ge(col_done, 1)
            dve.tensor_copy(shcol[:], bank[6][:, 0:KT]).then_inc(col_ready, 1)
            dve.scalar_tensor_tensor(out=acol[:], in0=bank[6][:, KT:2 * KT], scalar=1.0, in1=gcol[:],
                                     op0=ALU.add, op1=ALU.mult).then_inc(col_ready, 1)
            with dve.Fori(0, NCH // 2) as i:
                for p in range(2):
                    dve.wait_ge(ss_ready, 2 * TPC * i + TPC * (p + 1))
                    dve.tensor_scalar(var[:], ss[:], 1.0 / D, EPS, ALU.mult, ALU.add).then_inc(var_ready, 1)
                    dve.wait_ge(rt_ready, 2 * i + p + 1)
                    n = Count()
                    n.enter(i, 10)
                    n.now = 5 * p
                    dve.reciprocal(r0[:], rt[:]).then_inc(r_step, 1)
                    dve.wait_ge(r_step, n.up())
                    dve.tensor_tensor(r1[:], r0[:], r0[:], ALU.mult).then_inc(r_step, 1)
                    dve.wait_ge(r_step, n.up())
                    dve.tensor_tensor(r2[:], r1[:], var[:], ALU.mult).then_inc(r_step, 1)
                    dve.wait_ge(r_step, n.up())
                    dve.tensor_scalar(r1[:], r2[:], -0.5, 1.5, ALU.mult, ALU.add).then_inc(r_step, 1)
                    dve.wait_ge(r_step, n.up())
                    dve.tensor_tensor(rr[:], r0[:], r1[:], ALU.mult).then_inc(r_step, 1)
                    dve.wait_ge(r_step, n.up())
                    dve.wait_ge(tr_done, 2 * KT * i + KT * (p + 1))
                    for t in range(TPC):
                        dve.tensor_scalar(xn[:, t], xt[:, p, t], rr[:, t:t + 1], None, ALU.mult).then_inc(xn_ready, 1)
                    for k in range(1, KT, 2):
                        dve.wait_ge(tr_done, 2 * KT * i + KT * (p + 1) + k + 1)
                        if k == 1:
                            dve.wait_ge(h_out, 32 * i + 16 * p + 16)
                        dve.tensor_scalar(hout[:, k], bank[k][:], acol[:, k:k + 1], shcol[:, k:k + 1],
                                          ALU.mult, ALU.add).then_inc(v_evac, 1)

        @block.tensor
        def _(pe):
            pe.wait_ge(id_ready, 3)
            pe.wait_ge(csil_ready, 1)
            for b in range(NB):
                pe.wait_ge(w_in[b], 16)
                for k in range(KT):
                    last = pe.matmul(bank[b][0:1, :], csil[:, k:k + 1], wada[:, b, k], start=(k == 0), stop=(k == KT - 1))
                last.then_inc(row_done, 1)
            pe.wait_ge(mrow_ready, NB)
            for k in range(2 * KT):
                last = pe.matmul(bank[6][:, k:k + 1], mrow[0:1, k * P:(k + 1) * P], one[:], start=True, stop=True)
            last.then_inc(col_done, 1)
            pe.wait_ge(col_ready, 2)
            pe.sem_inc(tr_done, KT)
            with pe.Fori(0, NCH // 2) as i:
                for p in range(2):
                    pe.wait_ge(xn_ready, 2 * TPC * i + TPC * (p + 1))
                    for k in range(KT):
                        pe.wait_ge(a_evac if k % 2 == 0 else v_evac, KT * i + KT // 2 * p + k // 2 + 1)
                        for t in range(TPC):
                            last = pe.transpose(bank[k][:, t * P:(t + 1) * P], xn[:, t, k * P:(k + 1) * P], ident[:])
                        last.then_inc(tr_done, 1)


CONV, SPLIT, VO, ZV, GATED = range(5)
GROUPS = [
    (CONV, [(C_QK, 1024)]),
    (ZV, [(C_Z, 512), (C_SV, 512)]),
    (SPLIT, [(C_SQ, 1024)]),
    (VO, [(C_V, 1024)]),
    (GATED, [(C_SZ, 512), (C_G, 8)]),
]


def stage_project(nc, w_in, b_igate, b_fgate, conv_w, conv_b, g_ml, hT_d, out):
    NG = len(GROUPS)
    W = 1024
    with ExitStack() as ctx:
        sb = lambda n, s, d=F32: ctx.enter_context(nc.sbuf_tensor("p_" + n, s, d))
        ps = lambda n, s, d=F32: ctx.enter_context(nc.psum_tensor("p_" + n, s, d))
        sem = lambda n: ctx.enter_context(nc.semaphore("p_" + n))
        wraw = sb("wraw", [P, KT, W])
        whi, wlo = sb("whi", [P, KT, W], F32R), sb("wlo", [P, KT, W], F32R)
        hraw = sb("hraw", [P, KT, CH])
        hhi, hlo = sb("hhi", [P, 2, KT, CH], F32R), sb("hlo", [P, 2, KT, CH], F32R)
        oa, ob = sb("oa", [P, 4, CH]), sb("ob", [P, 4, CH])
        u, y = sb("u", [P, 2, CH + 3]), sb("y", [P, 2, CH])
        tail = sb("tail", [P, 8, 3])
        cw, cb = sb("cw", [P, 4, 8]), sb("cb", [P, 8])
        gml = sb("gml", [P, CH])
        gbias = sb("gbias", [8, 1])
        bank = [ps(f"bank{k}", [P, CH]) for k in range(8)]

        small_in, h_in, w_ld = sem("small_in"), sem("h_in"), sem("w_ld")
        h_hi, h_lo, w_hi, w_lo = sem("h_hi"), sem("h_lo"), sem("w_hi"), sem("w_lo")
        full = [sem(f"full{b}") for b in range(8)]
        free = [sem(f"free{b}") for b in range(8)]
        ready = [sem(f"ready{s}") for s in range(4)]
        st_a, st_b = [sem(f"st_a{s}") for s in range(4)], [sem(f"st_b{s}") for s in range(4)]
        sig_step, conv_step, u_ready, conv_done = sem("sig_step"), sem("conv_step"), sem("u_ready"), sem("conv_done")
        zero_ready, zero_out = sem("zero_ready"), sem("zero_out")
        dv_in, dv_step, dv_out = sem("dv_in"), sem("dv_step"), sem("dv_out")
        pool_held = sem("pool_held")
        va, vb, vh = (sb(n, [P, CH // 2]) for n in ("va", "vb", "vh"))
        block = ctx.enter_context(nc.Block())

        def banks(kind):
            return 5 if kind == GATED else 8

        def uses(kind, s):
            return sum(b % 4 == s for b in range(banks(kind)))

        def by_ready(kind, b):
            return kind in (CONV, SPLIT) or (kind == ZV and b % 2 == 0)

        def ready_uses(kind, s):
            return sum(b % 4 == s and by_ready(kind, b) for b in range(banks(kind)))

        def low_uses(kind, s):
            return uses(kind, s) if kind == SPLIT else 0

        def enter(cs, i, pers):
            for c, per in zip(cs, pers):
                c.enter(i, per)

        def leave(cs):
            for c in cs:
                c.leave(NCH // 2)

        @block.sync
        def _(sp):
            sp.dma_start(cw[:], conv_w.rearrange("j (m p) -> p j m", p=P), allow_slow_non_contiguous=True).then_inc(small_in, 16)
            sp.dma_start(cb[:], conv_b.rearrange("(m p) -> p m", p=P), allow_slow_non_contiguous=True).then_inc(small_in, 16)
            sp.dma_start(gbias[0:4], b_igate.rearrange("(p a) -> p a", a=1), allow_slow_non_contiguous=True).then_inc(small_in, 16)
            sp.dma_start(gbias[4:8], b_fgate.rearrange("(p a) -> p a", a=1), allow_slow_non_contiguous=True).then_inc(small_in, 16)
            sp.dma_start(gml[:], g_ml.rearrange("(a h) d -> a (h d)", a=1).to_broadcast([P, CH])).then_inc(small_in, 16)
            h_v = hT_d.rearrange("n p (k t) -> n p k t", k=KT)

            def load_w(cols):
                at = 0
                for c0, w in cols:
                    sp.dma_start(wraw[:, :, at:at + w], w_in[:, c0:c0 + w].rearrange("(k p) n -> p k n", p=P)).then_inc(w_ld, 16)
                    at += w

            qk_v = [out[k].rearrange("(n j) p h t -> n p j h t", j=TPC) for k in ("mlq", "mlk")]
            nat_v = {k: out[k].rearrange("(n i p) d -> n i p d", i=TPC, p=P) for k in ("v", "so", "szg")}
            nat_v["sbv"] = out["sbv"][1:S + 1, :].rearrange("(n i p) d -> n i p d", i=TPC, p=P)
            ch_v = {k: out[k].rearrange("(m p) (n t) -> n m p t", p=P, t=CH) for k in ("sqh", "sql", "skh", "skl", "sbz")}
            g_v = out["gates"].rearrange("g (n t) -> n g t", t=CH)

            def place(kind, b, n, low=False):
                if kind == CONV:
                    return qk_v[b // 4][n, :, :, b % 4, :]
                if kind == SPLIT:
                    return ch_v[("sq", "sk")[b // 4] + ("l" if low else "h")][n, b % 4]
                if kind in (VO, ZV):
                    return nat_v[(("v", "so") if kind == VO else ("szg", "sbv"))[b % 2]][n, b // 2]
                return ch_v["sbz"][n, b] if b < 4 else g_v[n]

            sp.dma_start(hraw[:], h_v[0]).then_inc(h_in, 16)
            load_w(GROUPS[0][1])
            rdy, freed, stored, stored_low = ([Count() for _ in range(4)], [Count(1) for _ in range(8)],
                                              [Count(1) for _ in range(4)], [Count(1) for _ in range(4)])
            h_split = Count()
            for g, (kind, _) in enumerate(GROUPS):
                if g + 1 < NG:
                    sp.wait_ge(w_hi, KT * (g + 1))
                    sp.wait_ge(w_lo, KT * (g + 1))
                    load_w(GROUPS[g + 1][1])
                with sp.Fori(0, NCH // 2) as i:
                    enter(rdy, i, [2 * ready_uses(kind, s) for s in range(4)])
                    enter(freed, i, [2 * (b < banks(kind)) for b in range(8)])
                    enter(stored, i, [2 * uses(kind, s) for s in range(4)])
                    enter(stored_low, i, [2 * low_uses(kind, s) for s in range(4)])
                    h_split.enter(i, 2)
                    for p in range(2):
                        sp.wait_ge(h_lo, h_split.up())
                        sp.dma_start(hraw[:], h_v[2 * i + (p + 1)]).then_inc(h_in, 16)
                        for b in range(banks(kind)):
                            s = b % 4
                            rows = 8 if b >= 4 and kind == GATED else P
                            tile = oa[0:rows, s]
                            if kind == CONV:
                                tile = tile.rearrange("p (j t) -> p j t", j=TPC)
                            stored[s].up()
                            freed[b].up()
                            if by_ready(kind, b):
                                sp.wait_ge(ready[s], rdy[s].up())
                            else:
                                sp.wait_ge(free[b], freed[b].value())
                            sp.dma_start(place(kind, b, 2 * i + p), tile).then_inc(st_a[s], 16)
                            if kind == SPLIT:
                                stored_low[s].up()
                                sp.wait_ge(free[b], freed[b].value())
                                sp.dma_start(place(kind, b, 2 * i + p, True), ob[:, s]).then_inc(st_b[s], 16)
                    leave(rdy + freed + stored + stored_low + [h_split])
            for s in range(4):
                sp.wait_ge(st_a[s], 16 * stored[s].now)
                sp.wait_ge(st_b[s], 16 * stored_low[s].now)

        @block.tensor
        def _(pe):
            for b in range(8):
                pe.sem_inc(full[b], 1)
            got = Count()
            bank_free = [Count() for _ in range(8)]
            for g, (kind, _) in enumerate(GROUPS):
                pe.wait_ge(w_hi, KT * (g + 1))
                pe.wait_ge(w_lo, KT * (g + 1))
                with pe.Fori(0, NCH // 2) as i:
                    got.enter(i, 2)
                    enter(bank_free, i, [2 * (b < banks(kind)) for b in range(8)])
                    for p in range(2):
                        n = got.up()
                        pe.wait_ge(h_hi, n)
                        pe.wait_ge(h_lo, n)
                        for b in range(banks(kind)):
                            pe.wait_ge(free[b], bank_free[b].up())
                            for k in range(KT):
                                if kind in (VO, ZV):
                                    t, c = slice((b // 2) * P, (b // 2 + 1) * P), slice((b % 2) * CH, (b % 2 + 1) * CH)
                                    dst = bank[b][:]
                                    hl = [(hhi[:, p, k, t], whi[:, k, c]), (hhi[:, p, k, t], wlo[:, k, c]), (hlo[:, p, k, t], whi[:, k, c])]
                                else:
                                    m = 8 if b >= 4 and kind == GATED else P
                                    c = slice(b * P, b * P + m)
                                    dst = bank[b][0:m, :]
                                    hl = [(whi[:, k, c], hhi[:, p, k]), (whi[:, k, c], hlo[:, p, k]), (wlo[:, k, c], hhi[:, p, k])]
                                for q, (stationary, moving) in enumerate(hl):
                                    last = pe.matmul(dst, stationary, moving, start=(k == 0 and q == 0), stop=(k == KT - 1 and q == 2))
                            last.then_inc(full[b], 1)
                    leave(bank_free + [got])

        @block.gpsimd
        def _(pool):
            pool.memset(vh[:], 0.0).then_inc(zero_ready, 1)
            pool.wait_ge(zero_ready, 1)
            for q in range(2):
                pool.dma_start(out["sbv"][0:1, q * 256:(q + 1) * 256], vh[0:1, :]).then_inc(zero_out, 16)
            pool.wait_ge(zero_out, 32)
            pool.wait_ge(h_hi, 1)
            pool.tensor_tensor(hlo[:, 0], hraw[:], hhi[:, 0].bitcast(F32), ALU.subtract).then_inc(h_lo, 1)
            got, vin, vstep, vout = Count(1), Count(), Count(), Count()

            def hold(semaphore, value):
                pool.wait_ge(semaphore, value)
                pool.sem_inc(pool_held, 1)

            for g, (kind, _) in enumerate(GROUPS):
                dv = g in (2, 3)
                if g == 2:
                    for s in range(4):
                        pool.wait_ge(st_a[s], 16 * (2 * 2 * NCH + 1))
                with pool.Fori(0, NCH // 2) as i:
                    enter([got, vin, vstep, vout], i, [2, 256 * dv, 24 * dv, 256 * dv])
                    for p in range(2):
                        pool.wait_ge(h_hi, got.up())
                        pool.tensor_tensor(hlo[:, 1 - p], hraw[:], hhi[:, 1 - p].bitcast(F32), ALU.subtract).then_inc(h_lo, 1)
                        if not dv:
                            continue
                        for e in range(2):
                            row = 16 * P * (g - 2) + (4 * i + (2 * p + e)) * P
                            for q in range(2):
                                cols = slice(q * 256, (q + 1) * 256)
                                pool.dma_start(va[:], out["sbv"][bass.ds(row, P), cols]).then_inc(dv_in, 16)
                                pool.dma_start(vb[:], out["sbv"][bass.ds(row + 1, P), cols]).then_inc(dv_in, 16)
                                pool.wait_ge(dv_in, vin.up(32))
                                pool.tensor_tensor(va[:], va[:], vb[:], ALU.subtract).then_inc(dv_step, 1)
                                hold(dv_step, vstep.up())
                                pool.tensor_copy(vh[:].bitcast(F32R), va[:]).then_inc(dv_step, 1)
                                pool.wait_ge(dv_step, vstep.up())
                                pool.tensor_tensor(vb[:].bitcast(F32R), va[:], vh[:], ALU.subtract).then_inc(dv_step, 1)
                                hold(dv_step, vstep.up())
                                dst = out["dw"][4 * q:4 * q + 4, 4 * (g - 2) + i, :, 2 * p + e, :].rearrange("h p e -> p h e")
                                pool.dma_start(dst[:, :, 0:SD], vh[:].rearrange("p (h e) -> p h e", h=4)).then_inc(dv_out, 16)
                                pool.dma_start(dst[:, :, SD:P], vb[:].rearrange("p (h e) -> p h e", h=4)).then_inc(dv_out, 16)
                                hold(dv_out, vout.up(32))
                    leave([got, vin, vstep, vout])
            pool.wait_ge(dv_out, vout.now)

        @block.scalar
        def _(act):
            act.wait_ge(h_in, 16)
            act.copy(hhi[:, 0], hraw[:]).then_inc(h_hi, 1)
            for b in range(8):
                act.sem_inc(free[b], 1)
            got, wl = Count(1), Count()
            fulls, slot = [Count(1) for _ in range(8)], [Count() for _ in range(4)]
            cdone, freed = Count(), [Count(1) for _ in range(8)]
            for g, (kind, cols) in enumerate(GROUPS):
                width = sum(w for _, w in cols)
                act.wait_ge(w_ld, wl.up(16 * len(cols)))
                if g:
                    last_bank = banks(GROUPS[g - 1][0]) - 1
                    act.wait_ge(full[last_bank], fulls[last_bank].value())
                for k in range(KT):
                    act.copy(whi[:, k, 0:width], wraw[:, k, 0:width]).then_inc(w_hi, 1)
                with act.Fori(0, NCH // 2) as i:
                    conv = kind == CONV
                    enter([got, cdone], i, [2, 16 * conv])
                    enter(fulls, i, [2 * (b < banks(kind)) for b in range(8)])
                    enter(slot, i, [2 * uses(kind, s) for s in range(4)])
                    enter(freed, i, [2 * (b < banks(kind)) for b in range(8)])
                    for p in range(2):
                        n = got.up()
                        act.wait_ge(h_in, 16 * n)
                        last_bank = banks(kind) - 1
                        act.wait_ge(full[last_bank], fulls[last_bank].value())
                        act.copy(hhi[:, 1 - p], hraw[:]).then_inc(h_hi, 1)

                        def conv_gate(b):
                            act.wait_ge(conv_done, cdone.up())
                            act.activation(ob[:, b % 4], y[:, b % 2], ACT.Sigmoid).then_inc(sig_step, 1)

                        for b in range(banks(kind)):
                            s = b % 4
                            act.wait_ge(full[b], fulls[b].up())
                            if kind == CONV:
                                act.copy(u[:, b % 2, 3:], bank[b][:]).then_inc(u_ready, 1)
                                if b:
                                    conv_gate(b - 1)
                            elif kind == SPLIT:
                                other = (b + 4) % 8
                                act.wait_ge(free[other], freed[other].value())
                                act.wait_ge(st_a[s], 16 * slot[s].up())
                                act.copy(oa[:, s].bitcast(F32R), bank[b][:]).then_inc(ready[s], 1)
                            elif kind == VO and b % 2:
                                act.wait_ge(st_a[s], 16 * slot[s].up())
                                act.activation(oa[:, s], bank[b][:], ACT.Sigmoid).then_inc(free[b], 1)
                            elif (kind == ZV and b % 2 == 0) or (kind == GATED and b < 4):
                                act.wait_ge(st_a[s], 16 * slot[s].up())
                                act.activation(ob[:, s], bank[b][:], ACT.Sigmoid).then_inc(sig_step, 1)
                            else:
                                slot[s].up()
                            freed[b].up()
                        if kind == CONV:
                            conv_gate(7)
                            for b in range(8):
                                slot[b % 4].up()
                    leave([got, cdone] + fulls + slot + freed)

        @block.vector
        def _(dve):
            for s in range(4):
                dve.sem_inc(st_a[s], 16)
                dve.sem_inc(st_b[s], 16)
            dve.memset(tail[:], 0.0).then_inc(conv_step, 1)
            dve.wait_ge(conv_step, 1)
            dve.wait_ge(small_in, 80)
            fulls, slot, slot_b = [Count(1) for _ in range(8)], [Count() for _ in range(4)], [Count() for _ in range(4)]
            rdy, freed, ur, cs, sg = [Count() for _ in range(4)], [Count(1) for _ in range(8)], Count(), Count(1), Count()
            for g, (kind, cols) in enumerate(GROUPS):
                width = sum(w for _, w in cols)
                for k in range(KT):
                    dve.wait_ge(w_hi, KT * g + k + 1)
                    dve.tensor_tensor(wlo[:, k, 0:width], wraw[:, k, 0:width], whi[:, k, 0:width].bitcast(F32),
                                      ALU.subtract).then_inc(w_lo, 1)
                with dve.Fori(0, NCH // 2) as i:
                    conv = kind == CONV
                    gated = {CONV: 8, ZV: 4, GATED: 4}.get(kind, 0)
                    enter([ur, cs, sg], i, [16 * conv, 64 * conv, 2 * gated])
                    enter(freed, i, [2 * (b < banks(kind)) for b in range(8)])
                    enter(fulls, i, [2 * (b < banks(kind)) for b in range(8)])
                    enter(slot, i, [2 * uses(kind, s) for s in range(4)])
                    enter(slot_b, i, [2 * low_uses(kind, s) for s in range(4)])
                    enter(rdy, i, [2 * ready_uses(kind, s) for s in range(4)])
                    for p in range(2):
                        def conv_out(b):
                            s = b % 4
                            dve.wait_ge(sig_step, sg.up())
                            dve.wait_ge(st_a[s], 16 * slot[s].up())
                            dve.scalar_tensor_tensor(out=oa[:, s], in0=y[:, b % 2], scalar=1.0 if b < 4 else K_SCALE,
                                                     in1=ob[:, s], op0=ALU.mult, op1=ALU.mult).then_inc(ready[s], 1)

                        for b in range(banks(kind)):
                            s = b % 4
                            if kind == CONV:
                                fulls[b].up()
                                rdy[s].up()
                                uu, yy = u[:, b % 2], y[:, b % 2]
                                dve.wait_ge(u_ready, ur.up())
                                dve.wait_ge(free[b], freed[b].value())
                                dve.tensor_copy(uu[:, 0:3], tail[:, b]).then_inc(conv_step, 1)
                                dve.wait_ge(conv_step, cs.up())
                                dve.tensor_copy(tail[:, b], uu[:, CH:CH + 3]).then_inc(free[b], 1)
                                freed[b].up()
                                dve.tensor_scalar(yy, uu[:, 0:CH], cw[:, 0, b:b + 1], cb[:, b:b + 1], ALU.mult, ALU.add).then_inc(conv_step, 1)
                                for j in range(1, 4):
                                    dve.wait_ge(conv_step, cs.up())
                                    dve.scalar_tensor_tensor(out=yy, in0=uu[:, j:j + CH], scalar=cw[:, j, b:b + 1], in1=yy,
                                                             op0=ALU.mult, op1=ALU.add).then_inc(conv_step if j < 3 else conv_done, 1)
                                if b:
                                    conv_out(b - 1)
                                continue
                            dve.wait_ge(full[b], fulls[b].up())
                            freed[b].up()
                            if by_ready(kind, b):
                                rdy[s].up()
                            if kind == SPLIT:
                                slot[s].up()
                                dve.wait_ge(ready[s], rdy[s].value())
                                dve.wait_ge(st_b[s], 16 * slot_b[s].up())
                                dve.tensor_tensor(ob[:, s].bitcast(F32R), bank[b][:], oa[:, s], ALU.subtract).then_inc(free[b], 1)
                            elif (kind == ZV and b % 2 == 0) or (kind == GATED and b < 4):
                                dve.wait_ge(sig_step, sg.up())
                                dve.wait_ge(st_a[s], 16 * slot[s].up())
                                if kind == ZV:
                                    dve.wait_ge(ready[(s + 2) % 4], rdy[(s + 2) % 4].value())
                                    dve.tensor_tensor(y[:, 0], bank[b][:], ob[:, s], ALU.mult).then_inc(free[b], 1)
                                    dve.wait_ge(free[b], freed[b].value())
                                    dve.tensor_tensor(oa[:, s], y[:, 0], gml[:], ALU.mult).then_inc(ready[s], 1)
                                else:
                                    dve.tensor_tensor(oa[:, s], bank[b][:], ob[:, s], ALU.mult).then_inc(free[b], 1)
                            elif kind == GATED:
                                dve.wait_ge(st_a[s], 16 * slot[s].up())
                                dve.tensor_scalar(oa[0:8, s], bank[b][0:8, :], gbias[:], None, ALU.add).then_inc(free[b], 1)
                            elif kind == VO and b % 2:
                                slot[s].up()
                            else:
                                dve.wait_ge(st_a[s], 16 * slot[s].up())
                                dve.tensor_copy(oa[:, s], bank[b][:]).then_inc(free[b], 1)
                        if kind == CONV:
                            conv_out(7)
                    leave([ur, cs, sg] + fulls + freed + slot + slot_b + rdy)


def stage_gates(nc, d, cols):
    with ExitStack() as ctx:
        sb = lambda n, s, dt=F32: ctx.enter_context(nc.sbuf_tensor("g_" + n, s, dt))
        ps = lambda n, s, dt=F32: ctx.enter_context(nc.psum_tensor("g_" + n, s, dt))
        sem = lambda n: ctx.enter_context(nc.semaphore("g_" + n))
        ig, fg, soft, logf, b, u, m, carry, keep = (sb(n, [MH, S]) for n in
            ("ig", "fg", "soft", "logf", "b", "u", "m", "carry", "keep"))
        ends = sb("ends", [MH, 2, NT])
        mprev, mlast = cols["mprev"], sb("mlast", [P, MH, NT])
        xw, xs, xe = (sb(n, [P, NT, MH]) for n in ("xw", "xs", "xe"))
        mcol = sb("mcol", [P, NT, MH])
        ident = sb("ident", [P, P])
        tr = [ps(f"tr{k}", [P, NT, MH]) for k in range(3)]
        g_in, const, act_step, dve_step, tr_done, ends_out, ends_in = (sem(n) for n in
            ("g_in", "const", "act_step", "dve_step", "tr_done", "ends_out", "ends_in"))
        block = ctx.enter_context(nc.Block())

        @block.sync
        def _(sp):
            sp.dma_start(fg[:], d["gates"][MH:2 * MH, :]).then_inc(g_in, 16)
            sp.dma_start(ig[:], d["gates"][0:MH, :]).then_inc(g_in, 16)
            sp.wait_ge(dve_step, 7)
            sp.dma_start(d["mb"].rearrange("a h c -> h a c"), ends[:]).then_inc(ends_out, 16)
            sp.wait_ge(ends_out, 16)
            sp.dma_start(mprev[:], d["mb"][0:1].to_broadcast([P, MH, NT])).then_inc(ends_in, 16)
            sp.dma_start(mlast[:], d["mb"][1:2].to_broadcast([P, MH, NT])).then_inc(ends_in, 16)
            sp.dma_start(d["m"], m[:]).then_inc(ends_out, 16)
            sp.wait_ge(ends_in, 32)
            sp.wait_ge(ends_out, 32)

        @block.gpsimd
        def _(pool):
            identity(pool, ident[:], const, 0)
            pool.memset(keep[:], 1.0).then_inc(const, 1)
            pool.memset(carry[:], 0.0).then_inc(const, 1)
            pool.memset(ends[:], 0.0).then_inc(const, 1)
            pool.wait_ge(const, 5)
            pool.memset(keep[:, 0:S:P], 0.0).then_inc(const, 1)

        @block.scalar
        def _(act):
            act.wait_ge(g_in, 32)
            act.activation(soft[:], fg[:], ACT.Abs).then_inc(act_step, 1)
            act.wait_ge(act_step, 1)
            act.activation(soft[:], soft[:], ACT.Exp, scale=-1.0).then_inc(act_step, 1)
            act.wait_ge(act_step, 2)
            act.activation(soft[:], soft[:], ACT.Ln, bias=1.0).then_inc(act_step, 1)
            act.wait_ge(dve_step, 12)
            act.activation(cols["wk"][:], xw[:], ACT.Exp).then_inc(act_step, 1)
            act.activation(cols["decay"][:], xs[:], ACT.Exp).then_inc(act_step, 1)
            act.activation(cols["floor"][:], xe[:], ACT.Exp, scale=-1.0).then_inc(act_step, 1)

        @block.vector
        def _(dve):
            dve.wait_ge(act_step, 3)
            dve.scalar_tensor_tensor(out=logf[:], in0=fg[:], scalar=0.0, in1=soft[:],
                                     op0=ALU.min, op1=ALU.subtract).then_inc(dve_step, 1)
            dve.wait_ge(dve_step, 1)
            dve.wait_ge(const, 6)
            dve.tensor_tensor_scan(b[:], keep[:], logf[:], 0.0, ALU.mult, ALU.add).then_inc(dve_step, 1)
            dve.wait_ge(dve_step, 2)
            dve.tensor_tensor(u[:], ig[:], b[:], ALU.subtract).then_inc(dve_step, 1)
            dve.tensor_copy(carry[:, P:S:P], b[:, P - 1:S - P:P]).then_inc(dve_step, 1)
            dve.wait_ge(dve_step, 4)
            dve.tensor_tensor_scan(m[:], carry[:], u[:], 0.0, ALU.add, ALU.max).then_inc(dve_step, 1)
            dve.wait_ge(dve_step, 5)
            dve.tensor_tensor(ends[:, 0, 1:NT], b[:, P - 1:S - P:P], m[:, P - 1:S - P:P], ALU.add).then_inc(dve_step, 1)
            dve.tensor_copy(ends[:, 1, :], m[:, P - 1:S:P]).then_inc(dve_step, 1)
            dve.wait_ge(tr_done, 3)
            dve.tensor_copy(cols["u"][:], tr[0][:]).then_inc(dve_step, 1)
            dve.tensor_copy(mcol[:], tr[1][:]).then_inc(dve_step, 1)
            dve.wait_ge(dve_step, 9)
            dve.wait_ge(ends_in, 32)
            dve.tensor_tensor(xw[:], tr[0][:], mlast[:].rearrange("p h c -> p c h"), ALU.subtract).then_inc(dve_step, 1)
            dve.tensor_tensor(xs[:].rearrange("p c h -> p h c"), mprev[:], mlast[:], ALU.subtract).then_inc(dve_step, 1)
            dve.tensor_tensor(xe[:], tr[2][:], mcol[:], ALU.add).then_inc(dve_step, 1)

        @block.tensor
        def _(pe):
            pe.wait_ge(const, 2)
            pe.wait_ge(dve_step, 5)
            for q, rows in enumerate((u, m, b)):
                for c in range(NT):
                    last = pe.transpose(tr[q][:, c, :], rows[:, c * P:(c + 1) * P], ident[0:MH, 0:MH])
                last.then_inc(tr_done, 1)


def stage_attend(nc, d):
    STEPS = []
    n = 0
    for r in range(NCH):
        for j in range(NCH - 1 - r, -1, -1):
            STEPS += [(n, r, NCH - 1 - r, j, q) for q in range(TPC)]
            n += 1
    N = len(STEPS)
    row_last = {r: max(k for k, s in enumerate(STEPS) if s[1] == r) for r in range(NCH)}
    ZB, RB = 3, 3
    with ExitStack() as ctx:
        sb = lambda n, s, dt=F32: ctx.enter_context(nc.sbuf_tensor("a_" + n, s, dt))
        ps = lambda n, s, dt=F32: ctx.enter_context(nc.psum_tensor("a_" + n, s, dt))
        sem = lambda n: ctx.enter_context(nc.semaphore("a_" + n))
        q_sb = sb("q", [P, S], F32R)
        khi, klo = sb("khi", [P, S], F32R), sb("klo", [P, S], F32R)
        dw = sb("dw", [P, NT, P], F32R)
        keep = sb("keep", [P, 3, CH])
        prod = sb("prod", [P, 2, TPC, CH])
        hi, lo = sb("hi", [P, 4, CH], F32R), sb("lo", [P, 4, CH], F32R)
        zeros = sb("zeros", [P, CH])
        ident, identb, maskb = sb("ident", [P, P]), sb("identb", [P, P], BF16), sb("maskb", [P, P], BF16)
        lowsum, osum, gate = sb("lowsum", [SD, 2, CH]), sb("osum", [SD, 2, CH]), sb("gate", [SD, 2, CH])
        vrow, v_e = sb("vrow", [NT, SH * SD]), sb("v_e", [SD, SH * NT])
        z = [ps(f"z{k}", [P, CH]) for k in range(ZB)]
        rt = [ps(f"rt{k}", [P, CH]) for k in range(RB)]
        acc = [ps(f"acc{k}", [P, CH]) for k in range(2)]

        const, v_in, ve_tr, ve_done = sem("const"), sem("v_in"), sem("ve_tr"), sem("ve_done")
        chunk_in = [sem(f"chunk_in{k}") for k in range(NCH)]
        z_done, keep_done, scan_done = sem("z_done"), sem("keep_done"), sem("scan_done")
        rt_done, hi_done, lo_done, av_done = sem("rt_done"), sem("hi_done"), sem("lo_done"), sem("av_done")
        low_done, sum_done, add_done, gated = sem("low_done"), sem("sum_done"), sem("add_done"), sem("gated")
        gate_in, o_st = [sem("gate_in0"), sem("gate_in1")], [sem("o_st0"), sem("o_st1")]
        held, held_sp = sem("held"), sem("held_sp")
        block = ctx.enter_context(nc.Block())
        KEEP0, SCAN0, RT0, LO0, AV0, SUM0 = ZB, 3, 8, RB, 4, 2

        def lo_col(k):
            _, _, c, j, q = STEPS[k]
            return q * P if c == j else 0

        def width(k):
            _, _, c, j, q = STEPS[k]
            return (q + 1) * P if c == j else CH

        @block.sync
        def _(sp):
            def load_chunk(k, h):
                t, hh = slice(k * CH, (k + 1) * CH), (slice(h * SD, (h + 1) * SD) if isinstance(h, int) else bass.ds(h * SD, SD))
                for tile, part, src in ((q_sb, 0, "sqh"), (q_sb, 1, "sql"), (khi, 0, "skh"), (khi, 1, "skh"), (klo, 0, "skl"), (klo, 1, "skl")):
                    sp.dma_start(tile[part * SD:(part + 1) * SD, t].bitcast(F32), d[src][hh, t]).then_inc(chunk_in[k], 16)
                sp.dma_start(dw[:, k * TPC:(k + 1) * TPC, :].bitcast(F32), d["dw"][h, k]).then_inc(chunk_in[k], 16)

            def load_gate(r, h):
                c, hh = NCH - 1 - r, (slice(h * SD, (h + 1) * SD) if isinstance(h, int) else bass.ds(h * SD, SD))
                sp.dma_start(gate[:, r % 2], d["sbz"][hh, c * CH:(c + 1) * CH]).then_inc(gate_in[r % 2], 16)

            sp.dma_start(vrow[:], d["sbv"][1:S + 1, :].rearrange("(b r) e -> r b e", r=P)[P - 1]).then_inc(v_in, 16)
            load_chunk(NCH - 1, 0)
            load_gate(0, 0)
            load_gate(1, 0)
            for k in range(NCH - 2, -1, -1):
                load_chunk(k, 0)

            def head(h, last):
                for r in range(NCH):
                    c = NCH - 1 - r
                    if not last:
                        sp.wait_ge(sum_done, NCH * h + (r + 1 + SUM0))
                        sp.sem_inc(held_sp, 1)
                        load_chunk(c, h + 1)
                    sp.wait_ge(gated, NCH * h + (r + 1))
                    sp.sem_inc(held_sp, 1)
                    hh = slice(h * SD, (h + 1) * SD) if isinstance(h, int) else bass.ds(h * SD, SD)
                    sp.dma_start(d["hsb"][c * TPC:(c + 1) * TPC, hh, :].rearrange("j e t -> e j t"),
                                 osum[:, r % 2].rearrange("e (j t) -> e j t", j=TPC)).then_inc(o_st[r % 2], 16)
                    if r + 2 < NCH:
                        load_gate(r + 2, h)
                    elif not last:
                        load_gate(r + 2 - NCH, h + 1)

            with sp.Fori(0, SH - 1) as h:
                head(h, False)
            head(SH - 1, True)
            for p in range(2):
                sp.wait_ge(o_st[p], 16 * (SH * NCH // 2 + 1))

        @block.gpsimd
        def _(pool):
            identity(pool, ident[:], const, 0)
            pool.memset(zeros[:], 0.0).then_inc(const, 1)
            pool.memset(maskb[:], 0.0).then_inc(const, 1)
            pool.wait_ge(const, 4)
            pool.affine_select(out=maskb[:], in_=maskb[:], compare_op=ALU.is_gt, fill=-BIG, base=0,
                               pattern=[[-1, P]], channel_multiplier=1).then_inc(const, 1)
            pool.tensor_copy(identb[:], ident[:]).then_inc(const, 1)
            pool.wait_ge(ve_done, 1)
            with pool.Fori(0, SH) as h:
                for r in range(NCH):
                    c = NCH - 1 - r
                    o = osum[:, r % 2].rearrange("e (j t) -> e j t", j=TPC)
                    pool.wait_ge(sum_done, NCH * h + (r + 1 + SUM0))
                    pool.sem_inc(held, 1)
                    pool.tensor_tensor(o, o, v_e[:, bass.ds(h * NT + c * TPC, TPC)].unsqueeze(2).to_broadcast([SD, TPC, P]),
                                       ALU.add).then_inc(add_done, 1)
                    pool.wait_ge(add_done, NCH * h + (r + 1))
                    pool.sem_inc(held, 1)
                    pool.wait_ge(gate_in[r % 2], h * (16 * NCH // 2) + 16 * (r // 2 + 1))
                    pool.tensor_tensor(osum[:, r % 2], osum[:, r % 2], gate[:, r % 2], ALU.mult).then_inc(gated, 1)

        @block.tensor
        def _(pe):
            pe.wait_ge(const, 6)
            pe.wait_ge(v_in, 16)
            for h in range(SH):
                last = pe.transpose(z[0][0:SD, h * NT:(h + 1) * NT], vrow[:, h * SD:(h + 1) * SD], ident[0:NT, 0:NT])
            last.then_inc(ve_tr, 1)
            pe.wait_ge(ve_done, 1)
            pe.sem_inc(rt_done, RT0)
            pe.sem_inc(av_done, AV0)
            with pe.Fori(0, SH) as h:
                def scores(k):
                    n, r, c, j, q = STEPS[k]
                    if q == 0:
                        pe.wait_ge(chunk_in[j], h * 112 + 112)
                    pe.wait_ge(keep_done, N * h + (k + 1))
                    w, bank = width(k), z[k % ZB]
                    t, s = c * CH + q * P, slice(j * CH, j * CH + w)
                    pe.matmul(bank[:, 0:w], q_sb[:, t:t + P], khi[:, s], start=True, stop=False)
                    last = pe.matmul(bank[:, 0:w], q_sb[:, t:t + P], klo[:, s], start=False, stop=c != j)
                    if c == j:
                        last = pe.matmul(bank[:, q * P:w], identb[:], maskb[:], start=False, stop=True)
                    last.then_inc(z_done, 1)

                def turn(k):
                    n, r, c, j, q = STEPS[k]
                    if q == 0:
                        pe.wait_ge(scan_done, N * h + (4 * n + 4 + SCAN0))
                    pe.wait_ge(lo_done, N * h + (k + 1))
                    for i in range(q if c == j else 0, TPC):
                        last = pe.transpose(rt[k % RB][:, i * P:(i + 1) * P], prod[:, n % 2, i, q * P:(q + 1) * P], ident[:])
                    last.then_inc(rt_done, 1)

                def weigh(k):
                    n, r, c, j, q = STEPS[k]
                    if c == j and q == 0:
                        pe.wait_ge(sum_done, NCH * h + (r + 1))
                    pe.wait_ge(lo_done, N * h + (k + 1 + LO0))
                    t = lo_col(k)
                    w = dw[:, j * TPC + q, :]
                    pe.matmul(acc[r % 2][:, t:], w, hi[:, k % 4, t:], start=(c == j and q == 0), stop=False)
                    pe.matmul(acc[r % 2][:, t:], w, lo[:, k % 4, t:], start=False, stop=k == row_last[r]).then_inc(av_done, 1)

                for k in range(4):
                    scores(k)
                for k in range(N + 2):
                    if k + 4 < N:
                        scores(k + 4)
                    if k < N:
                        turn(k)
                    if k >= 2:
                        weigh(k - 2)

        @block.scalar
        def _(act):
            act.sem_inc(keep_done, KEEP0)
            act.wait_ge(ve_tr, 1)
            act.copy(v_e[:], z[0][0:SD, 0:SH * NT]).then_inc(ve_done, 1)
            with act.Fori(0, SH) as h:
                def gate_of(k):
                    w = width(k)
                    act.wait_ge(z_done, N * h + (k + 1))
                    act.wait_ge(scan_done, N * h + (k + 1))
                    act.activation(keep[:, k % 3, 0:w], z[k % ZB][:, 0:w], ACT.Sigmoid, scale=-Z_SCALE).then_inc(keep_done, 1)

                def row_out(r):
                    act.wait_ge(av_done, N * h + (row_last[r] + 1 + AV0))
                    act.wait_ge(sum_done, NCH * h + (r + 1))
                    act.copy(lowsum[:, r % 2], acc[r % 2][SD:P, :]).then_inc(low_done, 1)

                for k in range(4):
                    gate_of(k)
                for k in range(N):
                    if k + 4 < N:
                        gate_of(k + 4)
                    t = lo_col(k)
                    act.wait_ge(rt_done, N * h + (k + 1 + RT0))
                    act.wait_ge(av_done, N * h + (k + 1))
                    act.copy(hi[:, k % 4, t:], rt[k % RB][:, t:]).then_inc(hi_done, 1)
                    for r in range(NCH):
                        if row_last[r] + 3 == k:
                            row_out(r)
                row_out(NCH - 1)

        @block.vector
        def _(dve):
            dve.sem_inc(scan_done, SCAN0)
            dve.sem_inc(lo_done, LO0)
            dve.sem_inc(sum_done, SUM0)
            for p in range(2):
                dve.sem_inc(o_st[p], 16)
            dve.wait_ge(const, 6)
            with dve.Fori(0, SH) as h:
                def scan(k):
                    n, r, c, j, q = STEPS[k]
                    w = width(k)
                    dve.wait_ge(keep_done, N * h + (k + 1 + KEEP0))
                    dve.wait_ge(rt_done, N * h + (4 * (n - 1) + RT0))
                    first = 1.0
                    if c != j:
                        dve.wait_ge(scan_done, N * h + (k - 4 + 1 + SCAN0))
                        first = prod[:, (n - 1) % 2, q, 0:1]
                    dve.tensor_tensor_scan(prod[:, n % 2, q, 0:w][:, ::-1], keep[:, k % 3, 0:w][:, ::-1], zeros[:, 0:w],
                                           first, ALU.mult, ALU.add).then_inc(scan_done, 1)

                def row_out(r):
                    dve.wait_ge(low_done, NCH * h + (r + 1))
                    dve.wait_ge(o_st[r % 2], h * (16 * NCH // 2) + 16 * (r // 2 + 1))
                    dve.tensor_tensor(osum[:, r % 2], acc[r % 2][0:SD, :], lowsum[:, r % 2], ALU.add).then_inc(sum_done, 1)

                for k in range(4):
                    scan(k)
                for k in range(N):
                    if k + 4 < N:
                        scan(k + 4)
                    t = lo_col(k)
                    dve.wait_ge(hi_done, N * h + (k + 1))
                    dve.tensor_tensor(lo[:, k % 4, t:], rt[k % RB][:, t:], hi[:, k % 4, t:].bitcast(F32), ALU.subtract).then_inc(lo_done, 1)
                    for r in range(NCH):
                        if row_last[r] + 3 == k:
                            row_out(r)
                row_out(NCH - 1)


def stage_mix(nc, d, cols, x, w_out, gg_d, y):
    VW = MD + 1
    with ExitStack() as ctx:
        sb = lambda n, s, dt=F32: ctx.enter_context(nc.sbuf_tensor("m_" + n, s, dt))
        ps = lambda n, s, dt=F32: ctx.enter_context(nc.psum_tensor("mp_" + n, s, dt))
        sem = lambda n: ctx.enter_context(nc.semaphore("m_" + n))
        wraw = sb("wraw", [P, KT, D])
        whi, wlo = sb("whi", [P, KT, D], F32R), sb("wlo", [P, KT, D], F32R)
        ggb = sb("ggb", [P, D])
        ident, maskb = sb("ident", [P, P]), sb("maskb", [P, P])
        qT, kT, mb = (sb(n, [P, 2, MH, P]) for n in ("qT", "kT", "mb"))
        v = sb("v", [P, 2, MH, VW])
        so, szg = sb("so", [P, 2, MH, MD]), sb("szg", [P, 2, MH, MD])
        sbt, xt, ot = sb("sbt", [P, 2, MH, P]), sb("xt", [P, 2, D]), sb("ot", [P, 2, D])
        gap, dwt = sb("gap", [P, MH, P]), sb("dwt", [P, MH, P])
        wq, qs, pm, kn = (sb(n, [P, MH, P]) for n in ("wq", "qs", "pm", "kn"))
        state = sb("state", [P, MH, VW])
        dneg, den, rden = (sb(n, [P, MH]) for n in ("dneg", "den", "rden"))
        hp, hf = sb("hp", [P, MH, MD]), sb("hf", [P, MH, MD])
        sq, sqy = sb("sq", [P, MH, MD], BF16), sb("sqy", [P, 2, CH], BF16)
        ss, sv, sl, s0, s1, s2, s3 = (sb(n, [P, MH]) for n in ("ss", "sv", "sl", "s0", "s1", "s2", "s3"))
        ys, yv, yl, y0, y1, y2, y3 = (sb(n, [P, 2]) for n in ("ys", "yv", "yl", "y0", "y1", "y2", "y3"))
        shi, slo = sb("shi", [P, 2, MH, P], F32R), sb("slo", [P, 2, MH, P], F32R)
        mhi, mlo = sb("mhi", [P, MH, P], F32R), sb("mlo", [P, MH, P], F32R)
        t_ps, s_ps = ps("t", [P, MH, P]), ps("s", [P, MH, P])
        n_ps = [ps(f"n{k}", [P, 2, VW]) for k in range(2)]
        u_ps = [ps(f"u{k}", [P, 2, VW]) for k in range(2)]
        y_ps = [ps(f"y{k}", [P, CH]) for k in range(2)]

        names = ("const w_in c_in w_hi w_lo k_tr s_done gap_done dwt_done wq_done qs_done pm_done kn_done n_done u_done "
                 "state_done den_step hp_done sq_done sv_done sr_done s_step hf_done h_tr mhi_done mlo_done shi_done slo_done "
                 "held y_done ysq_done yv_done yr_done y_step o_done fin_done").split()
        e = {n: sem(n) for n in names}
        ch_in, x_in, out_st = ([sem(f"{n}{p}") for p in range(2)] for n in ("ch_in", "x_in", "out_st"))
        act_held = sem("act_held")
        block = ctx.enter_context(nc.Block())

        def after(eng, semaphore, value):
            if not isinstance(value, int) or value > 0:
                eng.wait_ge(semaphore, value)

        def over_chunks(eng, body, ahead):
            body(0, 0, 0)
            body(1, 0, 1)
            pairs = (NT - 2 - ahead) // 2
            with eng.Fori(0, pairs) as i:
                for p in range(2):
                    body(2 * i + (2 + p), i + 1, p)
            for c in range(2 + 2 * pairs, NT):
                body(c, c // 2, c % 2)

        @block.sync
        def _(sp):
            def load(c, p):
                dst = [(qT, d["mlq"][c]), (kT, d["mlk"][c])]
                for tile, src in dst:
                    sp.dma_start(tile[:, p], src).then_inc(ch_in[p], 16)
                rows = slice(c * P, (c + 1) * P) if isinstance(c, int) else bass.ds(c * P, P)
                sp.dma_start(v[:, p, :, 0:MD], d["v"][rows, :].rearrange("t (h e) -> t h e", h=MH)).then_inc(ch_in[p], 16)
                sp.dma_start(so[:, p], d["so"][rows, :].rearrange("t (h e) -> t h e", h=MH)).then_inc(ch_in[p], 16)
                sp.dma_start(szg[:, p], d["szg"][rows, :].rearrange("t (h e) -> t h e", h=MH)).then_inc(ch_in[p], 16)
                sp.dma_start(mb[:, p], d["m"][:, rows].unsqueeze(0).to_broadcast([P, MH, P])).then_inc(ch_in[p], 16)
                sp.dma_start(sbt[:, p], d["hsb"][c].rearrange("(k p) t -> p k t", p=P)).then_inc(ch_in[p], 16)

            def load_x(c, p):
                rows = slice(c * P, (c + 1) * P) if isinstance(c, int) else bass.ds(c * P, P)
                sp.dma_start(xt[:, p], x[0, rows, :]).then_inc(x_in[p], 16)

            sp.dma_start(wraw[:], w_out.rearrange("(k p) n -> p k n", p=P)).then_inc(e["w_in"], 16)
            load(0, 0)
            load_x(0, 0)
            sp.dma_start(ggb[:], gg_d.to_broadcast([P, D])).then_inc(e["c_in"], 16)

            def store(c, p):
                after(sp, e["fin_done"], c + 1)
                rows = slice(c * P, (c + 1) * P) if isinstance(c, int) else bass.ds(c * P, P)
                sp.sem_inc(e["held"], 1)
                sp.dma_start(y[0, rows, :], ot[:, p]).then_inc(out_st[p], 16)

            def body(c, half, p):
                first, last = isinstance(c, int) and c == 0, isinstance(c, int) and c == NT - 1
                if not last:
                    after(sp, e["hf_done"], MH * c)
                    after(sp, e["slo_done"], c)
                    after(sp, e["state_done"], MH * (c + 1))
                    sp.sem_inc(e["held"], 1)
                    load(c + 1, 1 - p)
                if not first:
                    store(c - 1, 1 - p)
                if not last:
                    load_x(c + 1, 1 - p)

            over_chunks(sp, body, 2)
            store(NT - 1, (NT - 1) % 2)
            for p in range(2):
                sp.wait_ge(out_st[p], 16 * (NT // 2 + 1))

        @block.gpsimd
        def _(pool):
            identity(pool, ident[:], e["const"], 0)
            pool.memset(maskb[:], 0.0).then_inc(e["const"], 1)
            pool.wait_ge(e["const"], 3)
            pool.affine_select(out=maskb[:], in_=maskb[:], compare_op=ALU.is_ge, fill=BIG, base=0,
                               pattern=[[1, P]], channel_multiplier=-1).then_inc(e["const"], 1)
            pool.memset(v[:, :, :, MD:VW], 1.0).then_inc(e["const"], 1)
            pool.memset(state[:], 0.0).then_inc(e["state_done"], MH)

            def body(c, half, p):
                after(pool, ch_in[p], 112 * half + 112)
                after(pool, e["wq_done"], MH * (c + 1))
                after(pool, e["n_done"], c)
                pool.tensor_tensor(qs[:], qT[:, p], wq[:], ALU.mult).then_inc(e["qs_done"], 1)
                after(pool, e["shi_done"], c + 1)
                pool.tensor_tensor(slo[:, p], sbt[:, p], shi[:, p].bitcast(F32), ALU.subtract).then_inc(e["slo_done"], 1)
                if not (isinstance(c, int) and c == 0):
                    pool.wait_ge(x_in[1 - p], 16 * (half + p))
                    pool.wait_ge(e["o_done"], 2 * c)
                    pool.tensor_tensor(ot[:, 1 - p], ot[:, 1 - p], xt[:, 1 - p], ALU.add).then_inc(e["fin_done"], 1)

            over_chunks(pool, body, 0)
            pool.wait_ge(x_in[1], 16 * (NT // 2))
            pool.wait_ge(e["o_done"], 2 * NT)
            pool.tensor_tensor(ot[:, 1], ot[:, 1], xt[:, 1], ALU.add).then_inc(e["fin_done"], 1)

        @block.tensor
        def _(pe):
            pe.wait_ge(e["const"], 5)

            def turn_and_score(c, half, p):
                after(pe, ch_in[p], 112 * half + 112)
                after(pe, e["mlo_done"], c - 1)
                for h in range(MH):
                    last = pe.transpose(t_ps[:, h], kT[:, p, h], ident[:])
                last.then_inc(e["k_tr"], 1)
                after(pe, e["pm_done"], c)
                for h in range(MH):
                    last = pe.matmul(s_ps[:, h], kT[:, p, h], qT[:, p, h], start=True, stop=True)
                last.then_inc(e["s_done"], 1)

            def project(c, p, ks, parts):
                for nb in range(2):
                    for k in ks:
                        hi, lo = parts[0][:, k % MH], parts[1][:, k % MH]
                        cc = slice(nb * CH, (nb + 1) * CH)
                        for q, (a, b) in enumerate(((hi, whi), (hi, wlo), (lo, whi))):
                            last = pe.matmul(y_ps[nb][:], a, b[:, k, cc], start=(k == MH and q == 0), stop=(k == MH - 1 and q == 2))
                return last

            def project_sb(c, p):
                after(pe, e["o_done"], 2 * c)
                after(pe, e["slo_done"], c + 1)
                project(c, p, range(MH, KT), (shi[:, p], slo[:, p]))

            def turn_h(c):
                after(pe, e["hf_done"], MH * (c + 1))
                after(pe, e["kn_done"], MH * (c + 2 if not (isinstance(c, int) and c == NT - 1) else c + 1))
                for h in range(MH):
                    last = pe.transpose(t_ps[:, h], hf[:, h], ident[:])
                last.then_inc(e["h_tr"], 1)

            def project_ml(c, p):
                after(pe, e["mlo_done"], c + 1)
                project(c, p, range(MH), (mhi, mlo)).then_inc(e["y_done"], 1)

            def recur(c, p):
                after(pe, e["pm_done"], c + 1)
                after(pe, e["qs_done"], c + 1)
                after(pe, e["state_done"], MH * (c + 1))
                after(pe, e["hp_done"], MH * c)
                for h in range(MH):
                    dst = n_ps[h // 2][:, h % 2]
                    pe.matmul(dst, pm[:, h], v[:, p, h], start=(h % 2 == 0), stop=False, skip_group_check=True)
                    last = pe.matmul(dst, qs[:, h], state[:, h], start=False, stop=(h % 2 == 1), skip_group_check=True)
                last.then_inc(e["n_done"], 1)
                after(pe, e["kn_done"], MH * (c + 1))
                for h in range(MH):
                    last = pe.matmul(u_ps[h // 2][:, h % 2], kn[:, h], v[:, p, h], start=True, stop=True)
                last.then_inc(e["u_done"], 1)

            def body(c, half, p):
                turn_and_score(c, half, p)
                first = isinstance(c, int) and c == 0
                if not first:
                    project_sb(c - 1, 1 - p)
                    turn_h(c - 1)
                recur(c, p)
                if not first:
                    project_ml(c - 1, 1 - p)

            body(0, 0, 0)
            pe.wait_ge(e["w_hi"], KT)
            pe.wait_ge(e["w_lo"], KT)
            body(1, 0, 1)
            with pe.Fori(0, NT // 2 - 1) as i:
                for p in range(2):
                    body(2 * i + (2 + p), i + 1, p)
            project_sb(NT - 1, 1)
            turn_h(NT - 1)
            project_ml(NT - 1, 1)

        @block.scalar
        def _(act):
            def split_w():
                act.wait_ge(e["w_in"], 16)
                for k in range(KT):
                    act.copy(whi[:, k], wraw[:, k]).then_inc(e["w_hi"], 1)

            def split_h(c):
                after(act, e["h_tr"], c + 1)
                after(act, e["y_done"], c)
                act.copy(mhi[:], t_ps[:]).then_inc(e["mhi_done"], 1)

            def norm_y(c):
                after(act, e["y_done"], c + 1)
                after(act, e["yv_done"], c)
                for nb in range(2):
                    act.activation(sqy[:, nb], y_ps[nb][:], ACT.Square, accum_out=ys[:, nb:nb + 1]).then_inc(e["ysq_done"], 1)
                after(act, e["yv_done"], c + 1)
                act.activation(yl[:, 0:1], yv[:, 0:1], ACT.Ln).then_inc(e["yr_done"], 1)
                after(act, e["yr_done"], 2 * c + 1)
                act.activation(y0[:, 0:1], yl[:, 0:1], ACT.Exp, scale=-0.5).then_inc(e["yr_done"], 1)

            def body(c, half, p):
                dyn = (lambda t, h: t[:, c, h:h + 1]) if isinstance(c, int) else (lambda t, h: t[:, bass.ds(c, 1), h])
                dynm = (lambda t, h: t[:, h, c:c + 1]) if isinstance(c, int) else (lambda t, h: t[:, h, bass.ds(c, 1)])
                after(act, ch_in[p], 112 * half + 112)
                after(act, e["qs_done"], c)
                act.sem_inc(act_held, 1)
                for h in range(MH):
                    act.activation(wq[:, h], mb[:, p, h], ACT.Exp, scale=-1.0, bias=dynm(cols["mprev"], h)).then_inc(e["wq_done"], 1)
                after(act, e["gap_done"], MH * (c + 1))
                after(act, e["pm_done"], c)
                act.activation(dwt[:], gap[:], ACT.Exp, scale=-1.0).then_inc(e["dwt_done"], 1)
                after(act, e["k_tr"], c + 1)
                after(act, e["u_done"], c)
                act.sem_inc(act_held, 1)
                for h in range(MH):
                    act.activation(kn[:, h], t_ps[:, h], ACT.Copy, scale=dyn(cols["wk"], h)).then_inc(e["kn_done"], 1)
                after(act, e["y_done"], c - 1)
                act.copy(shi[:, p], sbt[:, p]).then_inc(e["shi_done"], 1)
                first = isinstance(c, int) and c == 0
                if not first:
                    split_h(c - 1)
                after(act, e["hp_done"], MH * (c + 1))
                after(act, e["sv_done"], c)
                for h in range(MH):
                    act.activation(sq[:, h], hp[:, h], ACT.Square, accum_out=ss[:, h:h + 1]).then_inc(e["sq_done"], 1)
                after(act, e["sv_done"], c + 1)
                act.activation(sl[:], sv[:], ACT.Ln).then_inc(e["sr_done"], 1)
                after(act, e["sr_done"], 2 * c + 1)
                act.activation(s0[:], sl[:], ACT.Exp, scale=-0.5).then_inc(e["sr_done"], 1)
                if not first:
                    norm_y(c - 1)

            body(0, 0, 0)
            split_w()
            body(1, 0, 1)
            with act.Fori(0, NT // 2 - 1) as i:
                for p in range(2):
                    body(2 * i + (2 + p), i + 1, p)
            split_h(NT - 1)
            norm_y(NT - 1)

        @block.vector
        def _(dve):
            for p in range(2):
                dve.sem_inc(out_st[p], 16)
            dve.wait_ge(e["c_in"], 16)
            dve.wait_ge(e["const"], 4)

            def newton(step, base, r0, var, t1, t2, r, n):
                dve.tensor_tensor(t1[:, 0:n], r0[:, 0:n], r0[:, 0:n], ALU.mult).then_inc(step, 1)
                dve.wait_ge(step, base + 1)
                dve.tensor_tensor(t2[:, 0:n], t1[:, 0:n], var[:, 0:n], ALU.mult).then_inc(step, 1)
                dve.wait_ge(step, base + 2)
                dve.tensor_scalar(t1[:, 0:n], t2[:, 0:n], -0.5, 1.5, ALU.mult, ALU.add).then_inc(step, 1)
                dve.wait_ge(step, base + 3)
                dve.tensor_tensor(r[:, 0:n], r0[:, 0:n], t1[:, 0:n], ALU.mult).then_inc(step, 1)
                dve.wait_ge(step, base + 4)

            def low_h(c):
                after(dve, e["mhi_done"], c + 1)
                dve.tensor_tensor(mlo[:], t_ps[:], mhi[:].bitcast(F32), ALU.subtract).then_inc(e["mlo_done"], 1)

            def norm_y(c, p, stored):
                after(dve, e["ysq_done"], 2 * c + 2)
                dve.tensor_tensor(y1[:, 0:1], ys[:, 0:1], ys[:, 1:2], ALU.add).then_inc(e["y_step"], 1)
                dve.wait_ge(e["y_step"], 5 * c + 1)
                dve.tensor_scalar(yv[:, 0:1], y1[:, 0:1], 1.0 / D, EPS, ALU.mult, ALU.add).then_inc(e["yv_done"], 1)
                after(dve, e["yr_done"], 2 * c + 2)
                newton(e["y_step"], 5 * c + 1, y0, yv, y1, y2, y3, 1)
                after(dve, out_st[p], stored)
                for nb in range(2):
                    cc = slice(nb * CH, (nb + 1) * CH)
                    dve.scalar_tensor_tensor(out=ot[:, p, cc], in0=y_ps[nb][:], scalar=y3[:, 0:1], in1=ggb[:, cc],
                                             op0=ALU.mult, op1=ALU.mult).then_inc(e["o_done"], 1)

            def body(c, half, p):
                dyn = (lambda t, h: t[:, c, h:h + 1]) if isinstance(c, int) else (lambda t, h: t[:, bass.ds(c, 1), h])
                first = isinstance(c, int) and c == 0
                after(dve, ch_in[p], 112 * half + 112)
                after(dve, e["dwt_done"], c)
                for h in range(MH):
                    dve.scalar_tensor_tensor(out=gap[:, h], in0=mb[:, p, h], scalar=dyn(cols["u"], h), in1=maskb[:],
                                             op0=ALU.subtract, op1=ALU.max).then_inc(e["gap_done"], 1)
                after(dve, e["dwt_done"], c + 1)
                after(dve, e["s_done"], c + 1)
                after(dve, e["n_done"], c)
                dve.tensor_tensor(pm[:], s_ps[:], dwt[:], ALU.mult).then_inc(e["pm_done"], 1)
                if not first:
                    low_h(c - 1)
                after(dve, e["n_done"], c + 1)
                for b in range(2):
                    fl = cols["floor"][:, c, 2 * b:2 * b + 2] if isinstance(c, int) else cols["floor"][:, bass.ds(c, 1), 2 * b:2 * b + 2].rearrange("p a h -> p (a h)")
                    dve.scalar_tensor_tensor(out=dneg[:, 2 * b:2 * b + 2], in0=n_ps[b][:, :, MD], scalar=-1.0, in1=fl,
                                             op0=ALU.mult, op1=ALU.max).then_inc(e["den_step"], 1)
                dve.wait_ge(e["den_step"], 5 * c + 2)
                for b in range(2):
                    dve.tensor_tensor(den[:, 2 * b:2 * b + 2], n_ps[b][:, :, MD], dneg[:, 2 * b:2 * b + 2],
                                      ALU.max).then_inc(e["den_step"], 1)
                dve.wait_ge(e["den_step"], 5 * c + 4)
                dve.reciprocal(rden[:], den[:]).then_inc(e["den_step"], 1)
                dve.wait_ge(e["den_step"], 5 * c + 5)
                for h in range(MH):
                    dve.scalar_tensor_tensor(out=hp[:, h], in0=n_ps[h // 2][:, h % 2, 0:MD], scalar=rden[:, h:h + 1], in1=so[:, p, h],
                                             op0=ALU.mult, op1=ALU.mult).then_inc(e["hp_done"], 1)
                after(dve, e["u_done"], c + 1)
                for h in range(MH):
                    dve.scalar_tensor_tensor(out=state[:, h], in0=state[:, h], scalar=dyn(cols["decay"], h), in1=u_ps[h // 2][:, h % 2],
                                             op0=ALU.mult, op1=ALU.add).then_inc(e["state_done"], 1)
                after(dve, e["sq_done"], MH * (c + 1))
                dve.tensor_scalar(sv[:], ss[:], 1.0 / MD, EPS, ALU.mult, ALU.add).then_inc(e["sv_done"], 1)
                after(dve, e["sr_done"], 2 * c + 2)
                newton(e["s_step"], 4 * c, s0, sv, s1, s2, s3, MH)
                after(dve, e["h_tr"], c)
                for h in range(MH):
                    dve.scalar_tensor_tensor(out=hf[:, h], in0=hp[:, h], scalar=s3[:, h:h + 1], in1=szg[:, p, h],
                                             op0=ALU.mult, op1=ALU.mult).then_inc(e["hf_done"], 1)
                if not first:
                    norm_y(c - 1, 1 - p, 16 * half + 16 * p)

            body(0, 0, 0)
            for k in range(KT):
                dve.wait_ge(e["w_hi"], k + 1)
                dve.tensor_tensor(wlo[:, k], wraw[:, k], whi[:, k].bitcast(F32), ALU.subtract).then_inc(e["w_lo"], 1)
            body(1, 0, 1)
            with dve.Fori(0, NT // 2 - 1) as i:
                for p in range(2):
                    body(2 * i + (2 + p), i + 1, p)
            low_h(NT - 1)
            norm_y(NT - 1, 1, 16 * NT // 2)


def program(nc, x, c, w_ada, b_ada, g_pre, w_in, b_igate, b_fgate, conv_w, conv_b, g_ml_head, w_out, g_post, y):
    def scratch(name, *shape):
        return nc.dram_tensor("scratch_" + name, shape, F32, kind="Internal").ap()

    hT_d = scratch("hT", NCH + 1, P, KT * CH)
    gg_d = scratch("gg", 1, D)
    d = dict(mlq=scratch("mlq", NT, P, MH, P), mlk=scratch("mlk", NT, P, MH, P),
             v=scratch("v", S, 512), so=scratch("so", S, 512), szg=scratch("szg", S, 512),
             sbv=scratch("sbv", S + 1, 512), sbz=scratch("sbz", 512, S), gates=scratch("gates", 8, S),
             sqh=scratch("sqh", 512, S), sql=scratch("sql", 512, S), skh=scratch("skh", 512, S), skl=scratch("skl", 512, S),
             dw=scratch("dw", SH, NCH, P, TPC, P), hsb=scratch("hsb", NT, 512, P),
             m=scratch("m", MH, S), mb=scratch("mb", 2, MH, NT))
    stage_norm(nc, x, c, w_ada, b_ada, g_pre, g_post, hT_d, gg_d)
    stage_project(nc, w_in, b_igate, b_fgate, conv_w, conv_b, g_ml_head, hT_d, d)
    with ExitStack() as ctx:
        cols = {k: ctx.enter_context(nc.sbuf_tensor("c_" + k, [P, NT, MH], F32)) for k in ("u", "wk", "decay", "floor")}
        cols["mprev"] = ctx.enter_context(nc.sbuf_tensor("c_mprev", [P, MH, NT], F32))
        stage_gates(nc, d, cols)
        stage_attend(nc, d)
        stage_mix(nc, d, cols, x, w_out, gg_d, y)


def kernel(x, c, w_ada, b_ada, g_pre, w_in, b_igate, b_fgate, conv_w, conv_b, g_ml_head, w_out, g_post):
    import numpy as np
    import concourse.bacc as bacc
    from concourse.bass_utils import run_bass_kernel_spmd as run

    nc = bacc.Bacc("TRN2", target_bir_lowering=False, num_devices=1)
    given = dict(x=x, c=c, w_ada=w_ada, b_ada=b_ada, g_pre=g_pre, w_in=w_in, b_igate=b_igate, b_fgate=b_fgate,
                 conv_w=conv_w, conv_b=conv_b, g_ml_head=g_ml_head, w_out=w_out, g_post=g_post)
    arrays = {"in_" + k: np.ascontiguousarray(a) for k, a in given.items()}
    aps = [nc.dram_tensor(k, a.shape, F32, kind="ExternalInput").ap() for k, a in arrays.items()]
    y = nc.dram_tensor("out_y", (1, S, D), F32, kind="ExternalOutput").ap()
    program(nc, *aps, y)
    return run(nc, [arrays], core_ids=[0]).results[0]["out_y"]
```

```python
import concourse.bass as bass
from concourse import mybir
from contextlib import ExitStack

F32 = mybir.dt.float32
F32R = mybir.dt.float32r
BF16 = mybir.dt.bfloat16
ALU = mybir.AluOpType
ACT = mybir.ActivationFunctionType

P = 128
D = 1024
S = 4096
KT = D // P
CH = 512
NCH = S // CH
TPC = CH // P
NT = S // P
MH, MD = 4, 128
SH, SD = 8, 64
EPS = 1e-6
K_SCALE = float(MD) ** -0.5
Z_SCALE = float(SD) ** -0.5
BIG = 1.0e30

C_QK, C_V, C_O, C_Z, C_G = 0, 1024, 1536, 2048, 2560
C_SQ, C_SK, C_SV, C_SZ = 2568, 3080, 3592, 4104


class Count:

    def __init__(self, start=0):
        self.now, self.reg, self.per = start, None, 0

    def enter(self, reg, per):
        self.first, self.reg, self.per = self.now, reg, per

    def leave(self, trips):
        assert self.now - self.first == self.per, (self.now - self.first, self.per)
        self.now, self.reg = self.first + self.per * trips, None

    def value(self, more=0):
        if self.reg is None or not self.per:
            return self.now + more
        return self.reg * self.per + (self.now + more)

    def up(self, k=1):
        self.now += k
        return self.value()


def identity(pool, tile, sem, n):
    pool.memset(tile, 0.0).then_inc(sem, 1)
    pool.wait_ge(sem, n + 1)
    pool.affine_select(out=tile, in_=tile, compare_op=ALU.not_equal, fill=1.0, base=0,
                       pattern=[[-1, P]], channel_multiplier=1).then_inc(sem, 1)


def stage_norm(nc, x, c, w_ada, b_ada, g_pre, g_post, hT_d, gg_d):
    NB = 3 * D // CH
    with ExitStack() as ctx:
        sb = lambda n, s, d=F32: ctx.enter_context(nc.sbuf_tensor("n_" + n, s, d))
        ps = lambda n, s, d=F32: ctx.enter_context(nc.psum_tensor("n_" + n, s, d))
        sem = lambda n: ctx.enter_context(nc.semaphore("n_" + n))
        wada = sb("wada", [P, NB, KT, CH])
        ccol, csig, csil = sb("ccol", [P, KT]), sb("csig", [P, KT]), sb("csil", [P, KT])
        gcol, acol, shcol = sb("gcol", [P, KT]), sb("acol", [P, KT]), sb("shcol", [P, KT])
        brow, mrow = sb("brow", [1, 3 * D]), sb("mrow", [1, 3 * D])
        gprow, ggrow, one = sb("gprow", [1, D]), sb("ggrow", [1, D]), sb("one", [1, 1])
        ident = sb("ident", [P, P])
        xt = sb("xt", [P, 2, TPC, D])
        xn = sb("xn", [P, TPC, D])
        sq = sb("sq", [P, TPC, D], BF16)
        ss, var, rt, r0, r1, r2, rr = (sb(n, [P, TPC]) for n in ("ss", "var", "rt", "r0", "r1", "r2", "rr"))
        hout = sb("hout", [P, KT, CH])
        bank = [ps(f"bank{k}", [P, CH]) for k in range(8)]

        x_in = [sem("x_in0"), sem("x_in1")]
        small_in, w_in = sem("small_in"), [sem(f"w_in{b}") for b in range(NB)]
        id_ready, csig_ready, csil_ready = sem("id_ready"), sem("csig_ready"), sem("csil_ready")
        row_done, mrow_ready, col_done, col_ready = sem("row_done"), sem("mrow_ready"), sem("col_done"), sem("col_ready")
        gg_ready, gg_out = sem("gg_ready"), sem("gg_out")
        ss_ready, var_ready, rt_ready, r_step, xn_ready = sem("ss_ready"), sem("var_ready"), sem("rt_ready"), sem("r_step"), sem("xn_ready")
        tr_done, a_evac, v_evac, h_out = sem("tr_done"), sem("a_evac"), sem("v_evac"), sem("h_out")
        block = ctx.enter_context(nc.Block())
        x_v = x.rearrange("b (n i p) d -> (b n) p i d", i=TPC, p=P)

        @block.sync
        def _(sp):
            sp.dma_start(ccol[:], c.rearrange("b (k p) -> p (b k)", p=P), allow_slow_non_contiguous=True).then_inc(small_in, 16)
            sp.dma_start(gcol[:], g_pre.rearrange("(k p) -> p k", p=P), allow_slow_non_contiguous=True).then_inc(small_in, 16)
            sp.dma_start(brow[:], b_ada.rearrange("(a n) -> a n", a=1)).then_inc(small_in, 16)
            sp.dma_start(gprow[:], g_post.rearrange("(a n) -> a n", a=1)).then_inc(small_in, 16)
            for p in range(2):
                sp.dma_start(xt[:, p], x_v[p]).then_inc(x_in[p], 16)
            for b in range(NB):
                sp.dma_start(wada[:, b], w_ada[:, b * CH:(b + 1) * CH].rearrange("(k p) n -> p k n", p=P)).then_inc(w_in[b], 16)
            def pair(i, ahead):
                for p in range(2):
                    if ahead:
                        sp.wait_ge(xn_ready, 2 * TPC * i + TPC * (p + 1))
                        sp.dma_start(xt[:, p], x_v[2 * i + (2 + p)]).then_inc(x_in[p], 16)
                    sp.wait_ge(a_evac, KT * i + KT // 2 * (p + 2))
                    sp.wait_ge(v_evac, KT * i + KT // 2 * (p + 2))
                    sp.dma_start(hT_d[2 * i + p], hout[:]).then_inc(h_out, 16)

            with sp.Fori(0, NCH // 2 - 1) as i:
                pair(i, True)
            pair(NCH // 2 - 1, False)
            sp.wait_ge(h_out, 16 * NCH + 16)
            sp.dma_start(hT_d[NCH:NCH + 2], hT_d[0:2]).then_inc(h_out, 16)
            sp.wait_ge(gg_ready, 1)
            sp.dma_start(gg_d, ggrow[:]).then_inc(gg_out, 16)
            sp.wait_ge(gg_out, 16)
            sp.wait_ge(h_out, 16 * NCH + 32)

        @block.gpsimd
        def _(pool):
            identity(pool, ident[:], id_ready, 0)
            pool.memset(one[:], 1.0).then_inc(id_ready, 1)

        @block.scalar
        def _(act):
            act.sem_inc(a_evac, KT // 2)
            act.wait_ge(small_in, 64)
            act.activation(csig[:], ccol[:], ACT.Sigmoid).then_inc(csig_ready, 1)
            with act.Fori(0, NCH // 2) as i:
                for p in range(2):
                    act.wait_ge(x_in[p], 16 * i + 16)
                    for t in range(TPC):
                        act.activation(sq[:, t], xt[:, p, t], ACT.Square, accum_out=ss[:, t:t + 1]).then_inc(ss_ready, 1)
                    act.wait_ge(var_ready, 2 * i + p + 1)
                    act.activation(rt[:], var[:], ACT.Sqrt).then_inc(rt_ready, 1)
                    act.wait_ge(col_ready, 2)
                    for k in range(0, KT, 2):
                        act.wait_ge(tr_done, 2 * KT * i + KT * (p + 1) + k + 1)
                        if k == 0:
                            act.wait_ge(h_out, 32 * i + 16 * p + 16)
                        act.activation(hout[:, k], bank[k][:], ACT.Identity, bias=shcol[:, k:k + 1],
                                       scale=acol[:, k:k + 1]).then_inc(a_evac, 1)

        @block.vector
        def _(dve):
            dve.sem_inc(h_out, 16)
            dve.sem_inc(v_evac, KT // 2)
            dve.wait_ge(small_in, 64)
            dve.wait_ge(csig_ready, 1)
            dve.tensor_tensor(csil[:], csig[:], ccol[:], ALU.mult).then_inc(csil_ready, 1)
            for b in range(NB):
                dve.wait_ge(row_done, b + 1)
                dve.tensor_tensor(mrow[0:1, b * CH:(b + 1) * CH], bank[b][0:1, :], brow[0:1, b * CH:(b + 1) * CH],
                                  ALU.add).then_inc(mrow_ready, 1)
            dve.wait_ge(mrow_ready, NB)
            dve.tensor_tensor(ggrow[:], mrow[0:1, 2 * D:3 * D], gprow[:], ALU.mult).then_inc(gg_ready, 1)
            dve.wait_ge(col_done, 1)
            dve.tensor_copy(shcol[:], bank[6][:, 0:KT]).then_inc(col_ready, 1)
            dve.scalar_tensor_tensor(out=acol[:], in0=bank[6][:, KT:2 * KT], scalar=1.0, in1=gcol[:],
                                     op0=ALU.add, op1=ALU.mult).then_inc(col_ready, 1)
            with dve.Fori(0, NCH // 2) as i:
                for p in range(2):
                    dve.wait_ge(ss_ready, 2 * TPC * i + TPC * (p + 1))
                    dve.tensor_scalar(var[:], ss[:], 1.0 / D, EPS, ALU.mult, ALU.add).then_inc(var_ready, 1)
                    dve.wait_ge(rt_ready, 2 * i + p + 1)
                    n = Count()
                    n.enter(i, 10)
                    n.now = 5 * p
                    dve.reciprocal(r0[:], rt[:]).then_inc(r_step, 1)
                    dve.wait_ge(r_step, n.up())
                    dve.tensor_tensor(r1[:], r0[:], r0[:], ALU.mult).then_inc(r_step, 1)
                    dve.wait_ge(r_step, n.up())
                    dve.tensor_tensor(r2[:], r1[:], var[:], ALU.mult).then_inc(r_step, 1)
                    dve.wait_ge(r_step, n.up())
                    dve.tensor_scalar(r1[:], r2[:], -0.5, 1.5, ALU.mult, ALU.add).then_inc(r_step, 1)
                    dve.wait_ge(r_step, n.up())
                    dve.tensor_tensor(rr[:], r0[:], r1[:], ALU.mult).then_inc(r_step, 1)
                    dve.wait_ge(r_step, n.up())
                    dve.wait_ge(tr_done, 2 * KT * i + KT * (p + 1))
                    for t in range(TPC):
                        dve.tensor_scalar(xn[:, t], xt[:, p, t], rr[:, t:t + 1], None, ALU.mult).then_inc(xn_ready, 1)
                    for k in range(1, KT, 2):
                        dve.wait_ge(tr_done, 2 * KT * i + KT * (p + 1) + k + 1)
                        if k == 1:
                            dve.wait_ge(h_out, 32 * i + 16 * p + 16)
                        dve.tensor_scalar(hout[:, k], bank[k][:], acol[:, k:k + 1], shcol[:, k:k + 1],
                                          ALU.mult, ALU.add).then_inc(v_evac, 1)

        @block.tensor
        def _(pe):
            pe.wait_ge(id_ready, 3)
            pe.wait_ge(csil_ready, 1)
            for b in range(NB):
                pe.wait_ge(w_in[b], 16)
                for k in range(KT):
                    last = pe.matmul(bank[b][0:1, :], csil[:, k:k + 1], wada[:, b, k], start=(k == 0), stop=(k == KT - 1))
                last.then_inc(row_done, 1)
            pe.wait_ge(mrow_ready, NB)
            for k in range(2 * KT):
                last = pe.matmul(bank[6][:, k:k + 1], mrow[0:1, k * P:(k + 1) * P], one[:], start=True, stop=True)
            last.then_inc(col_done, 1)
            pe.wait_ge(col_ready, 2)
            pe.sem_inc(tr_done, KT)
            with pe.Fori(0, NCH // 2) as i:
                for p in range(2):
                    pe.wait_ge(xn_ready, 2 * TPC * i + TPC * (p + 1))
                    for k in range(KT):
                        pe.wait_ge(a_evac if k % 2 == 0 else v_evac, KT * i + KT // 2 * p + k // 2 + 1)
                        for t in range(TPC):
                            last = pe.transpose(bank[k][:, t * P:(t + 1) * P], xn[:, t, k * P:(k + 1) * P], ident[:])
                        last.then_inc(tr_done, 1)


CONV, SPLIT, VO, ZV, GATED = range(5)
GROUPS = [
    (CONV, [(C_QK, 1024)]),
    (ZV, [(C_Z, 512), (C_SV, 512)]),
    (SPLIT, [(C_SQ, 1024)]),
    (VO, [(C_V, 1024)]),
    (GATED, [(C_SZ, 512), (C_G, 8)]),
]


def stage_project(nc, w_in, b_igate, b_fgate, conv_w, conv_b, g_ml, hT_d, out):
    NG = len(GROUPS)
    W = 1024
    with ExitStack() as ctx:
        sb = lambda n, s, d=F32: ctx.enter_context(nc.sbuf_tensor("p_" + n, s, d))
        ps = lambda n, s, d=F32: ctx.enter_context(nc.psum_tensor("p_" + n, s, d))
        sem = lambda n: ctx.enter_context(nc.semaphore("p_" + n))
        wraw = sb("wraw", [P, KT, W])
        whi, wlo = sb("whi", [P, KT, W], F32R), sb("wlo", [P, KT, W], F32R)
        hraw = sb("hraw", [P, KT, CH])
        hhi, hlo = sb("hhi", [P, 2, KT, CH], F32R), sb("hlo", [P, 2, KT, CH], F32R)
        oa, ob = sb("oa", [P, 4, CH]), sb("ob", [P, 4, CH])
        u, y = sb("u", [P, 2, CH + 3]), sb("y", [P, 2, CH])
        tail = sb("tail", [P, 8, 3])
        cw, cb = sb("cw", [P, 4, 8]), sb("cb", [P, 8])
        gml = sb("gml", [P, CH])
        gbias = sb("gbias", [8, 1])
        bank = [ps(f"bank{k}", [P, CH]) for k in range(8)]

        small_in, h_in, w_ld = sem("small_in"), sem("h_in"), sem("w_ld")
        h_hi, h_lo, w_hi, w_lo = sem("h_hi"), sem("h_lo"), sem("w_hi"), sem("w_lo")
        full = [sem(f"full{b}") for b in range(8)]
        free = [sem(f"free{b}") for b in range(8)]
        ready = [sem(f"ready{s}") for s in range(4)]
        st_a, st_b = [sem(f"st_a{s}") for s in range(4)], [sem(f"st_b{s}") for s in range(4)]
        sig_step, conv_step, u_ready, conv_done = sem("sig_step"), sem("conv_step"), sem("u_ready"), sem("conv_done")
        zero_ready, zero_out = sem("zero_ready"), sem("zero_out")
        dv_in, dv_step, dv_out = sem("dv_in"), sem("dv_step"), sem("dv_out")
        pool_held = sem("pool_held")
        va, vb, vh = (sb(n, [P, CH // 2]) for n in ("va", "vb", "vh"))
        block = ctx.enter_context(nc.Block())

        def banks(kind):
            return 5 if kind == GATED else 8

        def uses(kind, s):
            return sum(b % 4 == s for b in range(banks(kind)))

        def by_ready(kind, b):
            return kind in (CONV, SPLIT) or (kind == ZV and b % 2 == 0)

        def ready_uses(kind, s):
            return sum(b % 4 == s and by_ready(kind, b) for b in range(banks(kind)))

        def split_after(kind):
            return {CONV: 2, GATED: 0}.get(kind, 1)

        def low_uses(kind, s):
            return uses(kind, s) if kind == SPLIT else 0

        def enter(cs, i, pers):
            for c, per in zip(cs, pers):
                c.enter(i, per)

        def leave(cs):
            for c in cs:
                c.leave(NCH // 2)

        @block.sync
        def _(sp):
            sp.dma_start(cw[:], conv_w.rearrange("j (m p) -> p j m", p=P), allow_slow_non_contiguous=True).then_inc(small_in, 16)
            sp.dma_start(cb[:], conv_b.rearrange("(m p) -> p m", p=P), allow_slow_non_contiguous=True).then_inc(small_in, 16)
            sp.dma_start(gbias[0:4], b_igate.rearrange("(p a) -> p a", a=1), allow_slow_non_contiguous=True).then_inc(small_in, 16)
            sp.dma_start(gbias[4:8], b_fgate.rearrange("(p a) -> p a", a=1), allow_slow_non_contiguous=True).then_inc(small_in, 16)
            sp.dma_start(gml[:], g_ml.rearrange("(a h) d -> a (h d)", a=1).to_broadcast([P, CH])).then_inc(small_in, 16)
            h_v = hT_d.rearrange("n p (k t) -> n p k t", k=KT)

            def load_w(cols):
                at = 0
                for c0, w in cols:
                    sp.dma_start(wraw[:, :, at:at + w], w_in[:, c0:c0 + w].rearrange("(k p) n -> p k n", p=P)).then_inc(w_ld, 16)
                    at += w

            qk_v = [out[k].rearrange("(n j) p h t -> n p j h t", j=TPC) for k in ("mlq", "mlk")]
            nat_v = {k: out[k].rearrange("(n i p) d -> n i p d", i=TPC, p=P) for k in ("v", "so", "szg")}
            nat_v["sbv"] = out["sbv"][1:S + 1, :].rearrange("(n i p) d -> n i p d", i=TPC, p=P)
            ch_v = {k: out[k].rearrange("(m p) (n t) -> n m p t", p=P, t=CH) for k in ("sqh", "sql", "skh", "skl", "sbz")}
            g_v = out["gates"].rearrange("g (n t) -> n g t", t=CH)

            def place(kind, b, n, low=False):
                if kind == CONV:
                    return qk_v[b // 4][n, :, :, b % 4, :]
                if kind == SPLIT:
                    return ch_v[("sq", "sk")[b // 4] + ("l" if low else "h")][n, b % 4]
                if kind in (VO, ZV):
                    return nat_v[(("v", "so") if kind == VO else ("szg", "sbv"))[b % 2]][n, b // 2]
                return ch_v["sbz"][n, b] if b < 4 else g_v[n]

            sp.dma_start(hraw[:], h_v[0]).then_inc(h_in, 16)
            load_w(GROUPS[0][1])
            sp.wait_ge(h_lo, 1)
            sp.dma_start(hraw[:], h_v[1]).then_inc(h_in, 16)
            rdy, freed, stored, stored_low = ([Count() for _ in range(4)], [Count(1) for _ in range(8)],
                                              [Count(1) for _ in range(4)], [Count(1) for _ in range(4)])
            h_split = Count(1)
            for g, (kind, _) in enumerate(GROUPS):
                if g + 1 < NG:
                    sp.wait_ge(w_hi, KT * (g + 1))
                    sp.wait_ge(w_lo, KT * (g + 1))
                    load_w(GROUPS[g + 1][1])
                with sp.Fori(0, NCH // 2) as i:
                    enter(rdy, i, [2 * ready_uses(kind, s) for s in range(4)])
                    enter(freed, i, [2 * (b < banks(kind)) for b in range(8)])
                    enter(stored, i, [2 * uses(kind, s) for s in range(4)])
                    enter(stored_low, i, [2 * low_uses(kind, s) for s in range(4)])
                    h_split.enter(i, 2)
                    for p in range(2):
                        for b in range(banks(kind)):
                            s = b % 4
                            rows = 8 if b >= 4 and kind == GATED else P
                            tile = oa[0:rows, s]
                            if kind == CONV:
                                tile = tile.rearrange("p (j t) -> p j t", j=TPC)
                            stored[s].up()
                            freed[b].up()
                            if by_ready(kind, b):
                                sp.wait_ge(ready[s], rdy[s].up())
                            else:
                                sp.wait_ge(free[b], freed[b].value())
                            sp.dma_start(place(kind, b, 2 * i + p), tile).then_inc(st_a[s], 16)
                            if kind == SPLIT:
                                stored_low[s].up()
                                sp.wait_ge(free[b], freed[b].value())
                                sp.dma_start(place(kind, b, 2 * i + p, True), ob[:, s]).then_inc(st_b[s], 16)
                        sp.wait_ge(h_lo, h_split.up())
                        sp.dma_start(hraw[:], h_v[2 * i + (p + 2)]).then_inc(h_in, 16)
                    leave(rdy + freed + stored + stored_low + [h_split])
            sp.wait_ge(h_in, 16 * (NCH * NG + 2))
            for s in range(4):
                sp.wait_ge(st_a[s], 16 * stored[s].now)
                sp.wait_ge(st_b[s], 16 * stored_low[s].now)

        @block.tensor
        def _(pe):
            for b in range(8):
                pe.sem_inc(full[b], 1)
            got = Count()
            bank_free = [Count() for _ in range(8)]
            for g, (kind, _) in enumerate(GROUPS):
                with pe.Fori(0, NCH // 2) as i:
                    got.enter(i, 2)
                    enter(bank_free, i, [2 * (b < banks(kind)) for b in range(8)])
                    for p in range(2):
                        n = got.up()
                        pe.wait_ge(h_hi, n)
                        pe.wait_ge(h_lo, n)
                        for b in range(banks(kind)):
                            pe.wait_ge(free[b], bank_free[b].up())
                            for k in range(KT):
                                if p == 0 and b == 0:
                                    pe.wait_ge(w_hi, KT * g + k + 1)
                                    pe.wait_ge(w_lo, KT * g + k + 1)
                                if kind in (VO, ZV):
                                    t, c = slice((b // 2) * P, (b // 2 + 1) * P), slice((b % 2) * CH, (b % 2 + 1) * CH)
                                    dst = bank[b][:]
                                    hl = [(hhi[:, p, k, t], whi[:, k, c]), (hhi[:, p, k, t], wlo[:, k, c]), (hlo[:, p, k, t], whi[:, k, c])]
                                else:
                                    m = 8 if b >= 4 and kind == GATED else P
                                    c = slice(b * P, b * P + m)
                                    dst = bank[b][0:m, :]
                                    hl = [(whi[:, k, c], hhi[:, p, k]), (whi[:, k, c], hlo[:, p, k]), (wlo[:, k, c], hhi[:, p, k])]
                                for q, (stationary, moving) in enumerate(hl):
                                    last = pe.matmul(dst, stationary, moving, start=(k == 0 and q == 0), stop=(k == KT - 1 and q == 2))
                            last.then_inc(full[b], 1)
                    leave(bank_free + [got])

        @block.gpsimd
        def _(pool):
            pool.memset(vh[:], 0.0).then_inc(zero_ready, 1)
            pool.wait_ge(zero_ready, 1)
            for q in range(2):
                pool.dma_start(out["sbv"][0:1, q * 256:(q + 1) * 256], vh[0:1, :]).then_inc(zero_out, 16)
            pool.wait_ge(zero_out, 32)
            pool.wait_ge(h_hi, 1)
            pool.tensor_tensor(hlo[:, 0], hraw[:], hhi[:, 0].bitcast(F32), ALU.subtract).then_inc(h_lo, 1)
            got, vin, vstep, vout = Count(1), Count(), Count(), Count()

            def hold(semaphore, value):
                pool.wait_ge(semaphore, value)
                pool.sem_inc(pool_held, 1)

            for g, (kind, _) in enumerate(GROUPS):
                dv = g in (2, 3)
                if g == 2:
                    for s in range(4):
                        pool.wait_ge(st_a[s], 16 * (2 * 2 * NCH + 1))
                with pool.Fori(0, NCH // 2) as i:
                    enter([got, vin, vstep, vout], i, [2 * (g == 0), 256 * dv, 24 * dv, 256 * dv])
                    for p in range(2):
                        if g == 0:
                            pool.wait_ge(h_hi, got.up())
                            pool.tensor_tensor(hlo[:, 1 - p], hraw[:], hhi[:, 1 - p].bitcast(F32), ALU.subtract).then_inc(h_lo, 1)
                        if not dv:
                            continue
                        for e in range(2):
                            row = 16 * P * (g - 2) + (4 * i + (2 * p + e)) * P
                            for q in range(2):
                                cols = slice(q * 256, (q + 1) * 256)
                                pool.dma_start(va[:], out["sbv"][bass.ds(row, P), cols]).then_inc(dv_in, 16)
                                pool.dma_start(vb[:], out["sbv"][bass.ds(row + 1, P), cols]).then_inc(dv_in, 16)
                                pool.wait_ge(dv_in, vin.up(32))
                                pool.tensor_tensor(va[:], va[:], vb[:], ALU.subtract).then_inc(dv_step, 1)
                                hold(dv_step, vstep.up())
                                pool.tensor_copy(vh[:].bitcast(F32R), va[:]).then_inc(dv_step, 1)
                                pool.wait_ge(dv_step, vstep.up())
                                pool.tensor_tensor(vb[:].bitcast(F32R), va[:], vh[:], ALU.subtract).then_inc(dv_step, 1)
                                hold(dv_step, vstep.up())
                                dst = out["dw"][4 * q:4 * q + 4, 4 * (g - 2) + i, :, 2 * p + e, :].rearrange("h p e -> p h e")
                                pool.dma_start(dst[:, :, 0:SD], vh[:].rearrange("p (h e) -> p h e", h=4)).then_inc(dv_out, 16)
                                pool.dma_start(dst[:, :, SD:P], vb[:].rearrange("p (h e) -> p h e", h=4)).then_inc(dv_out, 16)
                                hold(dv_out, vout.up(32))
                    leave([got, vin, vstep, vout])
            pool.wait_ge(dv_out, vout.now)

        @block.scalar
        def _(act):
            act.wait_ge(h_in, 16)
            act.copy(hhi[:, 0], hraw[:]).then_inc(h_hi, 1)
            for b in range(8):
                act.sem_inc(free[b], 1)
            got, wl = Count(1), Count()
            fulls, slot = [Count(1) for _ in range(8)], [Count() for _ in range(4)]
            cdone, freed = Count(), [Count(1) for _ in range(8)]
            for g, (kind, cols) in enumerate(GROUPS):
                width = sum(w for _, w in cols)
                act.wait_ge(w_ld, wl.up(16 * len(cols)))
                if g:
                    last_bank = banks(GROUPS[g - 1][0]) - 1
                    act.wait_ge(full[last_bank], fulls[last_bank].value())
                for k in range(KT):
                    act.copy(whi[:, k, 0:width], wraw[:, k, 0:width]).then_inc(w_hi, 1)
                with act.Fori(0, NCH // 2) as i:
                    conv = kind == CONV
                    enter([got, cdone], i, [2, 16 * conv])
                    enter(fulls, i, [2 * (b < banks(kind)) for b in range(8)])
                    enter(slot, i, [2 * uses(kind, s) for s in range(4)])
                    enter(freed, i, [2 * (b < banks(kind)) for b in range(8)])
                    for p in range(2):
                        def high_h():
                            act.wait_ge(h_in, 16 * got.up())
                            last_bank = banks(kind) - 1
                            act.wait_ge(full[last_bank], fulls[last_bank].value())
                            act.copy(hhi[:, 1 - p], hraw[:]).then_inc(h_hi, 1)

                        def conv_gate(b):
                            act.wait_ge(conv_done, cdone.up())
                            act.activation(ob[:, b % 4], y[:, b % 2], ACT.Sigmoid).then_inc(sig_step, 1)

                        for b in range(banks(kind)):
                            s = b % 4
                            act.wait_ge(full[b], fulls[b].up())
                            if kind == CONV:
                                act.copy(u[:, b % 2, 3:], bank[b][:]).then_inc(u_ready, 1)
                                if b:
                                    conv_gate(b - 1)
                            elif kind == SPLIT:
                                other = (b + 4) % 8
                                act.wait_ge(free[other], freed[other].value())
                                act.wait_ge(st_a[s], 16 * slot[s].up())
                                act.copy(oa[:, s].bitcast(F32R), bank[b][:]).then_inc(ready[s], 1)
                            elif kind == VO and b % 2:
                                act.wait_ge(st_a[s], 16 * slot[s].up())
                                act.activation(oa[:, s], bank[b][:], ACT.Sigmoid).then_inc(free[b], 1)
                            elif (kind == ZV and b % 2 == 0) or (kind == GATED and b < 4):
                                act.wait_ge(st_a[s], 16 * slot[s].up())
                                act.activation(ob[:, s], bank[b][:], ACT.Sigmoid).then_inc(sig_step, 1)
                            else:
                                slot[s].up()
                            freed[b].up()
                            if b == split_after(kind):
                                high_h()
                        if kind == CONV:
                            conv_gate(7)
                            for b in range(8):
                                slot[b % 4].up()
                    leave([got, cdone] + fulls + slot + freed)

        @block.vector
        def _(dve):
            for s in range(4):
                dve.sem_inc(st_a[s], 16)
                dve.sem_inc(st_b[s], 16)
            dve.memset(tail[:], 0.0).then_inc(conv_step, 1)
            dve.wait_ge(conv_step, 1)
            dve.wait_ge(small_in, 80)
            fulls, slot, slot_b = [Count(1) for _ in range(8)], [Count() for _ in range(4)], [Count() for _ in range(4)]
            got, rdy, freed, ur, cs, sg = Count(1 + NCH), [Count() for _ in range(4)], [Count(1) for _ in range(8)], Count(), Count(1), Count()
            for g, (kind, cols) in enumerate(GROUPS):
                width = sum(w for _, w in cols)
                for k in range(KT):
                    dve.wait_ge(w_hi, KT * g + k + 1)
                    dve.tensor_tensor(wlo[:, k, 0:width], wraw[:, k, 0:width], whi[:, k, 0:width].bitcast(F32),
                                      ALU.subtract).then_inc(w_lo, 1)
                with dve.Fori(0, NCH // 2) as i:
                    conv = kind == CONV
                    gated = {CONV: 8, ZV: 4, GATED: 4}.get(kind, 0)
                    enter([got, ur, cs, sg], i, [2 * (not conv), 16 * conv, 64 * conv, 2 * gated])
                    enter(freed, i, [2 * (b < banks(kind)) for b in range(8)])
                    enter(fulls, i, [2 * (b < banks(kind)) for b in range(8)])
                    enter(slot, i, [2 * uses(kind, s) for s in range(4)])
                    enter(slot_b, i, [2 * low_uses(kind, s) for s in range(4)])
                    enter(rdy, i, [2 * ready_uses(kind, s) for s in range(4)])
                    for p in range(2):
                        def conv_out(b):
                            s = b % 4
                            dve.wait_ge(sig_step, sg.up())
                            dve.wait_ge(st_a[s], 16 * slot[s].up())
                            dve.scalar_tensor_tensor(out=oa[:, s], in0=y[:, b % 2], scalar=1.0 if b < 4 else K_SCALE,
                                                     in1=ob[:, s], op0=ALU.mult, op1=ALU.mult).then_inc(ready[s], 1)

                        for b in range(banks(kind)):
                            s = b % 4
                            if kind == CONV:
                                fulls[b].up()
                                rdy[s].up()
                                uu, yy = u[:, b % 2], y[:, b % 2]
                                dve.wait_ge(u_ready, ur.up())
                                dve.wait_ge(free[b], freed[b].value())
                                dve.tensor_copy(uu[:, 0:3], tail[:, b]).then_inc(conv_step, 1)
                                dve.wait_ge(conv_step, cs.up())
                                dve.tensor_copy(tail[:, b], uu[:, CH:CH + 3]).then_inc(free[b], 1)
                                freed[b].up()
                                dve.tensor_scalar(yy, uu[:, 0:CH], cw[:, 0, b:b + 1], cb[:, b:b + 1], ALU.mult, ALU.add).then_inc(conv_step, 1)
                                for j in range(1, 4):
                                    dve.wait_ge(conv_step, cs.up())
                                    dve.scalar_tensor_tensor(out=yy, in0=uu[:, j:j + CH], scalar=cw[:, j, b:b + 1], in1=yy,
                                                             op0=ALU.mult, op1=ALU.add).then_inc(conv_step if j < 3 else conv_done, 1)
                                if b:
                                    conv_out(b - 1)
                                continue
                            dve.wait_ge(full[b], fulls[b].up())
                            freed[b].up()
                            if by_ready(kind, b):
                                rdy[s].up()
                            if kind == SPLIT:
                                slot[s].up()
                                dve.wait_ge(ready[s], rdy[s].value())
                                dve.wait_ge(st_b[s], 16 * slot_b[s].up())
                                dve.tensor_tensor(ob[:, s].bitcast(F32R), bank[b][:], oa[:, s], ALU.subtract).then_inc(free[b], 1)
                            elif (kind == ZV and b % 2 == 0) or (kind == GATED and b < 4):
                                dve.wait_ge(sig_step, sg.up())
                                dve.wait_ge(st_a[s], 16 * slot[s].up())
                                if kind == ZV:
                                    dve.wait_ge(ready[(s + 2) % 4], rdy[(s + 2) % 4].value())
                                    dve.tensor_tensor(y[:, 0], bank[b][:], ob[:, s], ALU.mult).then_inc(free[b], 1)
                                    dve.wait_ge(free[b], freed[b].value())
                                    dve.tensor_tensor(oa[:, s], y[:, 0], gml[:], ALU.mult).then_inc(ready[s], 1)
                                else:
                                    dve.tensor_tensor(oa[:, s], bank[b][:], ob[:, s], ALU.mult).then_inc(free[b], 1)
                            elif kind == GATED:
                                dve.wait_ge(st_a[s], 16 * slot[s].up())
                                dve.tensor_scalar(oa[0:8, s], bank[b][0:8, :], gbias[:], None, ALU.add).then_inc(free[b], 1)
                            elif kind == VO and b % 2:
                                slot[s].up()
                            else:
                                dve.wait_ge(st_a[s], 16 * slot[s].up())
                                dve.tensor_copy(oa[:, s], bank[b][:]).then_inc(free[b], 1)
                            if b == split_after(kind):
                                dve.wait_ge(h_hi, got.up())
                                dve.tensor_tensor(hlo[:, 1 - p], hraw[:], hhi[:, 1 - p].bitcast(F32), ALU.subtract).then_inc(h_lo, 1)
                        if kind == CONV:
                            conv_out(7)
                    leave([got, ur, cs, sg] + fulls + freed + slot + slot_b + rdy)


def stage_attend(nc, d, cols, wout_hi, wout_lo, w_out):
    STEPS = []
    n = 0
    for r in range(NCH):
        for j in range(NCH - 1 - r, -1, -1):
            STEPS += [(n, r, NCH - 1 - r, j, q) for q in range(TPC)]
            n += 1
    N = len(STEPS)
    row_last = {r: max(k for k, s in enumerate(STEPS) if s[1] == r) for r in range(NCH)}
    ZB, RB = 3, 3
    KB, PB = 3, 3
    LEAD = 6
    with ExitStack() as ctx:
        sb = lambda n, s, dt=F32: ctx.enter_context(nc.sbuf_tensor("a_" + n, s, dt))
        ps = lambda n, s, dt=F32: ctx.enter_context(nc.psum_tensor("a_" + n, s, dt))
        sem = lambda n: ctx.enter_context(nc.semaphore("a_" + n))
        q_sb = sb("q", [P, S], F32R)
        khi, klo = sb("khi", [P, S], F32R), sb("klo", [P, S], F32R)
        dw = sb("dw", [P, NT, P], F32R)
        keep = sb("keep", [P, KB, CH])
        prod = sb("prod", [P, PB, TPC, CH])
        hi, lo = sb("hi", [P, 4, CH], F32R), sb("lo", [P, 4, CH], F32R)
        tile = sb("tile", [P, CH])
        zeros = sb("zeros", [P, CH])
        ident, identb, maskb = sb("ident", [P, P]), sb("identb", [P, P], BF16), sb("maskb", [P, P], BF16)
        lowsum, osum, gate = sb("lowsum", [SD, CH]), sb("osum", [SD, 2, CH]), sb("gate", [SD, 2, CH])
        vrow, v_e = sb("vrow", [NT, SH * SD]), sb("v_e", [SD, SH * NT])
        ig, fg, soft, b, u, top, m = (sb(n, [P, P]) for n in ("ig", "fg", "soft", "b", "u", "top", "m"))
        ones, mcol_in = sb("ones", [P, P]), sb("mcol_in", [P, 1])
        b_before, tops, mlast_row, mprev_row = (sb(n, [1, MH, NT]) for n in ("b_before", "tops", "mlast_row", "mprev_row"))
        mlast, (xw, xs, xe, mcol) = sb("mlast", [P, MH, NT]), (sb(n, [P, NT, MH]) for n in ("xw", "xs", "xe", "mcol"))
        wout_raw = sb("wout_raw", [P, D])
        z = [ps(f"z{k}", [P, CH]) for k in range(ZB)]
        rt = [ps(f"rt{k}", [P, CH]) for k in range(RB)]
        acc = [ps(f"acc{k}", [P, CH]) for k in range(2)]

        const, v_in, ve_tr, ve_done = sem("const"), sem("v_in"), sem("ve_tr"), sem("ve_done")
        chunk_in = [sem(f"chunk_in{k}") for k in range(NCH)]
        z_done, keep_done, scan_done = sem("z_done"), sem("keep_done"), sem("scan_done")
        rt_done, hi_done, lo_done, av_done = sem("rt_done"), sem("hi_done"), sem("lo_done"), sem("av_done")
        tile_done, pool_lo_done = sem("tile_done"), sem("pool_lo_done")
        low_done, sum_done, add_done, gated = sem("low_done"), sem("sum_done"), sem("add_done"), sem("gated")
        gate_in, o_st = [sem("gate_in0"), sem("gate_in1")], [sem("o_st0"), sem("o_st1")]
        held, held_sp = sem("held"), sem("held_sp")
        g_in, g_const, g_act, g_dve, g_pe, m_out = (sem(n) for n in ("g_in", "g_const", "g_act", "g_dve", "g_pe", "m_out"))
        wout_in, wout_step = sem("wout_in"), sem("wout_step")
        block = ctx.enter_context(nc.Block())
        KEEP0, SCAN0, RT0, LO0, AV0, SUM0, TILE0 = ZB, KB, TPC * PB, RB - 1, 4, 2, 1

        def by_pool(k):
            return k % 4 == 2

        def pool_lows(k):
            return (k + 1) // 4

        def dve_lows(k):
            return k - pool_lows(k)

        NP, ND = pool_lows(N), dve_lows(N)

        def lo_col(k):
            _, _, c, j, q = STEPS[k]
            return q * P if c == j else 0

        def width(k):
            _, _, c, j, q = STEPS[k]
            return (q + 1) * P if c == j else CH

        @block.sync
        def _(sp):
            def load_chunk(k, h):
                t, hh = slice(k * CH, (k + 1) * CH), (slice(h * SD, (h + 1) * SD) if isinstance(h, int) else bass.ds(h * SD, SD))
                for tile, part, src in ((q_sb, 0, "sqh"), (q_sb, 1, "sql"), (khi, 0, "skh"), (khi, 1, "skh"), (klo, 0, "skl"), (klo, 1, "skl")):
                    sp.dma_start(tile[part * SD:(part + 1) * SD, t].bitcast(F32), d[src][hh, t]).then_inc(chunk_in[k], 16)
                sp.dma_start(dw[:, k * TPC:(k + 1) * TPC, :].bitcast(F32), d["dw"][h, k]).then_inc(chunk_in[k], 16)

            def load_gate(r, h):
                c, hh = NCH - 1 - r, (slice(h * SD, (h + 1) * SD) if isinstance(h, int) else bass.ds(h * SD, SD))
                sp.dma_start(gate[:, r % 2], d["sbz"][hh, c * CH:(c + 1) * CH]).then_inc(gate_in[r % 2], 16)

            for tile, row in ((fg, MH), (ig, 0)):
                sp.dma_start(tile[:], d["gates"][row:row + MH, :].rearrange("h (c t) -> (h c) t", t=P)).then_inc(g_in, 16)
            sp.dma_start(vrow[:], d["sbv"][1:S + 1, :].rearrange("(b r) e -> r b e", r=P)[P - 1]).then_inc(v_in, 16)
            load_chunk(NCH - 1, 0)
            load_gate(0, 0)
            load_gate(1, 0)
            for k in range(NCH - 2, -1, -1):
                load_chunk(k, 0)
            sp.dma_start(wout_raw[:], w_out[0:P, :]).then_inc(wout_in, 16)
            sp.wait_ge(g_dve, 14)
            sp.dma_start(d["m"].rearrange("h (c t) -> (h c) t", t=P), m[:]).then_inc(m_out, 16)

            def head(h, last):
                for r in range(NCH):
                    c = NCH - 1 - r
                    if not last:
                        sp.wait_ge(sum_done, NCH * h + (r + 1 + SUM0))
                        sp.sem_inc(held_sp, 1)
                        load_chunk(c, h + 1)
                    sp.wait_ge(gated, NCH * h + (r + 1))
                    sp.sem_inc(held_sp, 1)
                    hh = slice(h * SD, (h + 1) * SD) if isinstance(h, int) else bass.ds(h * SD, SD)
                    sp.dma_start(d["hsb"][c * TPC:(c + 1) * TPC, hh, :].rearrange("j e t -> e j t"),
                                 osum[:, r % 2].rearrange("e (j t) -> e j t", j=TPC)).then_inc(o_st[r % 2], 16)
                    if r + 2 < NCH:
                        load_gate(r + 2, h)
                    elif not last:
                        load_gate(r + 2 - NCH, h + 1)
                if not last:
                    sp.wait_ge(wout_step, 8 * h + 8)
                    sp.sem_inc(held_sp, 1)
                    sp.dma_start(wout_raw[:], w_out[bass.ds((h + 1) * P, P), :]).then_inc(wout_in, 16)

            with sp.Fori(0, SH - 1) as h:
                head(h, False)
            head(SH - 1, True)
            for p in range(2):
                sp.wait_ge(o_st[p], 16 * (SH * NCH // 2 + 1))
            sp.wait_ge(m_out, 16)

        @block.gpsimd
        def _(pool):
            identity(pool, ident[:], const, 0)
            pool.memset(zeros[:], 0.0).then_inc(const, 1)
            pool.memset(maskb[:], 0.0).then_inc(const, 1)
            pool.wait_ge(const, 4)
            pool.affine_select(out=maskb[:], in_=maskb[:], compare_op=ALU.is_gt, fill=-BIG, base=0,
                               pattern=[[-1, P]], channel_multiplier=1).then_inc(const, 1)
            pool.tensor_copy(identb[:], ident[:]).then_inc(const, 1)
            pool.memset(ones[:], 1.0).then_inc(g_const, 1)
            pool.memset(b_before[:], 0.0).then_inc(g_const, 1)
            pool.memset(mprev_row[:], 0.0).then_inc(g_const, 1)
            pool.wait_ge(ve_done, 1)
            with pool.Fori(0, SH) as h:
                def split_w_out(part):
                    cc = slice(part * (D // 4), (part + 1) * (D // 4))
                    whi, wlo = wout_hi[:, bass.ds(h, 1), cc], wout_lo[:, bass.ds(h, 1), cc]
                    raw = wout_raw[:, cc].unsqueeze(1)
                    pool.tensor_copy(whi, raw).then_inc(wout_step, 1)
                    pool.wait_ge(wout_step, 8 * h + (2 * part + 1))
                    pool.sem_inc(held, 1)
                    pool.tensor_tensor(wlo, raw, whi.bitcast(F32), ALU.subtract).then_inc(wout_step, 1)

                def finish_row(r):
                    c = NCH - 1 - r
                    o = osum[:, r % 2].rearrange("e (j t) -> e j t", j=TPC)
                    pool.wait_ge(sum_done, NCH * h + (r + 1 + SUM0))
                    pool.sem_inc(held, 1)
                    pool.tensor_tensor(o, o, v_e[:, bass.ds(h * NT + c * TPC, TPC)].unsqueeze(2).to_broadcast([SD, TPC, P]),
                                       ALU.add).then_inc(add_done, 1)
                    pool.wait_ge(add_done, NCH * h + (r + 1))
                    pool.sem_inc(held, 1)
                    pool.wait_ge(gate_in[r % 2], h * (16 * NCH // 2) + 16 * (r // 2 + 1))
                    pool.tensor_tensor(osum[:, r % 2], osum[:, r % 2], gate[:, r % 2], ALU.mult).then_inc(gated, 1)

                for k in range(N):
                    if by_pool(k):
                        t = lo_col(k)
                        pool.wait_ge(tile_done, NP * h + (pool_lows(k + 1) + TILE0))
                        pool.tensor_tensor(lo[:, k % 4, t:], tile[:, t:], hi[:, k % 4, t:].bitcast(F32), ALU.subtract).then_inc(pool_lo_done, 1)
                    for r in range(NCH):
                        if row_last[r] + 7 == k:
                            finish_row(r)
                    if k % (N // 4) == N // 4 - 5:
                        if k < N // 4:
                            pool.wait_ge(wout_in, 16 * h + 16)
                            pool.sem_inc(held, 1)
                        split_w_out(k // (N // 4))
                for r in range(NCH):
                    if row_last[r] + 7 >= N:
                        finish_row(r)

        @block.tensor
        def _(pe):
            pe.wait_ge(const, 6)
            pe.wait_ge(v_in, 16)
            for h in range(SH):
                last = pe.transpose(z[0][0:SD, h * NT:(h + 1) * NT], vrow[:, h * SD:(h + 1) * SD], ident[0:NT, 0:NT])
            last.then_inc(ve_tr, 1)
            pe.wait_ge(g_dve, 4)
            pe.transpose(acc[0][0:1, 0:P], b[:, P - 1:P], ident[:])
            pe.transpose(acc[0][0:1, P:2 * P], top[:, P - 1:P], ident[:]).then_inc(g_pe, 1)
            pe.transpose(rt[0][:, 0:P], u[:], ident[:])
            pe.transpose(rt[2][:, 0:P], b[:], ident[:]).then_inc(g_pe, 1)
            pe.wait_ge(g_dve, 11)
            row = lambda t: t[:].rearrange("a h c -> a (h c)")
            pe.matmul(acc[1][:, 2 * P:2 * P + 1], row(mprev_row), ones[0:1, 0:1], start=True, stop=True)
            pe.matmul(acc[1][:, 0:P], ones[0:1, :], row(mprev_row), start=True, stop=True)
            pe.matmul(acc[1][:, P:2 * P], ones[0:1, :], row(mlast_row), start=True, stop=True).then_inc(g_pe, 1)
            pe.wait_ge(g_dve, 14)
            pe.transpose(rt[1][:, 0:P], m[:], ident[:]).then_inc(g_pe, 1)
            pe.wait_ge(ve_done, 1)
            pe.wait_ge(g_dve, 20)
            pe.sem_inc(rt_done, RT0)
            pe.sem_inc(av_done, AV0)
            with pe.Fori(0, SH) as h:
                def scores(k):
                    n, r, c, j, q = STEPS[k]
                    if q == 0:
                        pe.wait_ge(chunk_in[j], h * 112 + 112)
                    pe.wait_ge(keep_done, N * h + (k + 1))
                    w, bank = width(k), z[k % ZB]
                    t, s = c * CH + q * P, slice(j * CH, j * CH + w)
                    pe.matmul(bank[:, 0:w], q_sb[:, t:t + P], khi[:, s], start=True, stop=False)
                    last = pe.matmul(bank[:, 0:w], q_sb[:, t:t + P], klo[:, s], start=False, stop=c != j)
                    if c == j:
                        last = pe.matmul(bank[:, q * P:w], identb[:], maskb[:], start=False, stop=True)
                    last.then_inc(z_done, 1)

                def turn(k):
                    n, r, c, j, q = STEPS[k]
                    if q == 0:
                        pe.wait_ge(scan_done, N * h + (4 * n + 4 + SCAN0))
                    before = k - RB
                    if by_pool(before):
                        pe.wait_ge(tile_done, NP * h + (pool_lows(before + 1) + TILE0))
                    else:
                        pe.wait_ge(lo_done, ND * h + (dve_lows(before + 1) + LO0))
                    for i in range(q if c == j else 0, TPC):
                        last = pe.transpose(rt[k % RB][:, i * P:(i + 1) * P], prod[:, n % PB, i, q * P:(q + 1) * P], ident[:])
                    last.then_inc(rt_done, 1)

                def weigh(k):
                    n, r, c, j, q = STEPS[k]
                    if c == j and q == 0:
                        pe.wait_ge(sum_done, NCH * h + (r + 1))
                    if by_pool(k):
                        pe.wait_ge(pool_lo_done, NP * h + pool_lows(k + 1))
                    else:
                        pe.wait_ge(lo_done, ND * h + (dve_lows(k + 1) + LO0))
                    t = lo_col(k)
                    w = dw[:, j * TPC + q, :]
                    pe.matmul(acc[r % 2][:, t:], w, hi[:, k % 4, t:], start=(c == j and q == 0), stop=False)
                    pe.matmul(acc[r % 2][:, t:], w, lo[:, k % 4, t:], start=False, stop=k == row_last[r]).then_inc(av_done, 1)

                for k in range(LEAD):
                    scores(k)
                for k in range(N + 3):
                    if k + LEAD < N:
                        scores(k + LEAD)
                    if k < N:
                        turn(k)
                    if k >= 3:
                        weigh(k - 3)

        @block.scalar
        def _(act):
            act.sem_inc(keep_done, KEEP0)
            act.sem_inc(tile_done, TILE0)
            act.preload_act_table_set("natural_log_exp_and_others")
            act.wait_ge(g_in, 32)
            act.activation(soft[:], fg[:], ACT.Abs).then_inc(g_act, 1)
            act.wait_ge(g_act, 1)
            act.activation(soft[:], soft[:], ACT.Exp, scale=-1.0).then_inc(g_act, 1)
            act.wait_ge(g_act, 2)
            act.activation(soft[:], soft[:], ACT.Ln, bias=1.0).then_inc(g_act, 1)
            act.wait_ge(ve_tr, 1)
            act.copy(v_e[:], z[0][0:SD, 0:SH * NT]).then_inc(ve_done, 1)
            act.wait_ge(g_dve, 20)
            act.activation(cols["wk"][:], xw[:], ACT.Exp).then_inc(g_act, 1)
            act.activation(cols["decay"][:], xs[:], ACT.Exp).then_inc(g_act, 1)
            act.activation(cols["floor"][:], xe[:], ACT.Exp, scale=-1.0).then_inc(g_act, 1)
            with act.Fori(0, SH) as h:
                def gate_of(k):
                    w = width(k)
                    act.wait_ge(z_done, N * h + (k + 1))
                    act.wait_ge(scan_done, N * h + (k + 1))
                    act.activation(keep[:, k % KB, 0:w], z[k % ZB][:, 0:w], ACT.Sigmoid, scale=-Z_SCALE).then_inc(keep_done, 1)

                def row_out(r):
                    act.wait_ge(av_done, N * h + (row_last[r] + 1 + AV0))
                    act.wait_ge(sum_done, NCH * h + (r + SUM0))
                    act.copy(lowsum[:], acc[r % 2][SD:P, :]).then_inc(low_done, 1)

                for k in range(LEAD):
                    gate_of(k)
                for k in range(N):
                    if k + LEAD < N:
                        gate_of(k + LEAD)
                    t = lo_col(k)
                    act.wait_ge(rt_done, N * h + (k + 1 + RT0))
                    act.wait_ge(av_done, N * h + (k + 1))
                    act.copy(hi[:, k % 4, t:], rt[k % RB][:, t:]).then_inc(hi_done, 1)
                    if by_pool(k):
                        act.copy(tile[:, t:], rt[k % RB][:, t:]).then_inc(tile_done, 1)
                    for r in range(NCH):
                        if row_last[r] + 4 == k:
                            row_out(r)
                row_out(NCH - 1)

        @block.vector
        def _(dve):
            dve.sem_inc(scan_done, SCAN0)
            dve.sem_inc(lo_done, LO0)
            dve.sem_inc(sum_done, SUM0)
            for p in range(2):
                dve.sem_inc(o_st[p], 16)
            dve.wait_ge(const, 6)
            dve.wait_ge(g_const, 3)
            dve.wait_ge(g_act, 3)
            dve.scalar_tensor_tensor(out=soft[:], in0=fg[:], scalar=0.0, in1=soft[:],
                                     op0=ALU.min, op1=ALU.subtract).then_inc(g_dve, 1)
            dve.wait_ge(g_dve, 1)
            dve.tensor_tensor_scan(b[:], ones[:], soft[:], 0.0, ALU.mult, ALU.add).then_inc(g_dve, 1)
            dve.wait_ge(g_dve, 2)
            dve.tensor_tensor(u[:], ig[:], b[:], ALU.subtract).then_inc(g_dve, 1)
            dve.wait_ge(g_dve, 3)
            dve.tensor_tensor_scan(top[:], zeros[:, 0:P], u[:], -3.0e38, ALU.add, ALU.max).then_inc(g_dve, 1)
            dve.wait_ge(g_pe, 1)
            sums, maxima = (acc[0][0:1, q * P:(q + 1) * P].rearrange("a (h c) -> a h c", h=MH) for q in range(2))
            dve.tensor_copy(b_before[:, :, 1:NT], sums[:, :, 0:NT - 1]).then_inc(g_dve, 1)
            dve.tensor_copy(tops[:], maxima).then_inc(g_dve, 1)
            dve.wait_ge(g_dve, 6)
            for h in range(MH):
                dve.tensor_tensor_scan(mlast_row[:, h], b_before[:, h], tops[:, h], 0.0, ALU.add, ALU.max).then_inc(g_dve, 1)
            dve.wait_ge(g_dve, 10)
            dve.tensor_tensor(mprev_row[:, :, 1:NT], mlast_row[:, :, 0:NT - 1], b_before[:, :, 1:NT], ALU.add).then_inc(g_dve, 1)
            dve.wait_ge(g_pe, 3)
            dve.tensor_copy(mcol_in[:], acc[1][:, 2 * P:2 * P + 1]).then_inc(g_dve, 1)
            dve.tensor_copy(cols["mprev"][:], acc[1][:, 0:P].rearrange("p (h c) -> p h c", h=MH)).then_inc(g_dve, 1)
            dve.wait_ge(g_dve, 12)
            dve.tensor_scalar(m[:], top[:], mcol_in[:], None, ALU.max).then_inc(g_dve, 1)
            by_chunk = lambda t: t.rearrange("p (h c) -> p c h", h=MH)
            dve.tensor_copy(mlast[:], acc[1][:, P:2 * P].rearrange("p (h c) -> p h c", h=MH)).then_inc(g_dve, 1)
            dve.tensor_copy(cols["u"][:], by_chunk(rt[0][:, 0:P])).then_inc(g_dve, 1)
            dve.wait_ge(g_dve, 15)
            dve.tensor_tensor(xw[:], by_chunk(rt[0][:, 0:P]), mlast[:].rearrange("p h c -> p c h"), ALU.subtract).then_inc(g_dve, 1)
            dve.tensor_tensor(xs[:].rearrange("p c h -> p h c"), cols["mprev"][:], mlast[:], ALU.subtract).then_inc(g_dve, 1)
            dve.wait_ge(g_pe, 4)
            dve.tensor_copy(mcol[:], by_chunk(rt[1][:, 0:P])).then_inc(g_dve, 1)
            dve.wait_ge(g_dve, 19)
            dve.tensor_tensor(xe[:], by_chunk(rt[2][:, 0:P]), mcol[:], ALU.add).then_inc(g_dve, 1)
            with dve.Fori(0, SH) as h:
                def scan(k):
                    n, r, c, j, q = STEPS[k]
                    w = width(k)
                    dve.wait_ge(keep_done, N * h + (k + 1 + KEEP0))
                    dve.wait_ge(rt_done, N * h + (TPC * (n - PB + 1) + RT0))
                    first = 1.0
                    if c != j:
                        dve.wait_ge(scan_done, N * h + (k - 4 + 1 + SCAN0))
                        first = prod[:, (n - 1) % PB, q, 0:1]
                    dve.tensor_tensor_scan(prod[:, n % PB, q, 0:w][:, ::-1], keep[:, k % KB, 0:w][:, ::-1], zeros[:, 0:w],
                                           first, ALU.mult, ALU.add).then_inc(scan_done, 1)

                def row_out(r):
                    dve.wait_ge(low_done, NCH * h + (r + 1))
                    dve.wait_ge(o_st[r % 2], h * (16 * NCH // 2) + 16 * (r // 2 + 1))
                    dve.tensor_tensor(osum[:, r % 2], acc[r % 2][0:SD, :], lowsum[:], ALU.add).then_inc(sum_done, 1)

                for k in range(LEAD):
                    scan(k)
                for k in range(N):
                    if k + LEAD < N:
                        scan(k + LEAD)
                    t = lo_col(k)
                    if not by_pool(k):
                        dve.wait_ge(hi_done, N * h + (k + 1))
                        dve.tensor_tensor(lo[:, k % 4, t:], rt[k % RB][:, t:], hi[:, k % 4, t:].bitcast(F32), ALU.subtract).then_inc(lo_done, 1)
                    for r in range(NCH):
                        if row_last[r] + 4 == k:
                            row_out(r)
                row_out(NCH - 1)


def stage_mix(nc, d, cols, x, whi, wlo, gg_d, y):
    VW = MD + 1
    with ExitStack() as ctx:
        sb = lambda n, s, dt=F32: ctx.enter_context(nc.sbuf_tensor("m_" + n, s, dt))
        ps = lambda n, s, dt=F32: ctx.enter_context(nc.psum_tensor("mp_" + n, s, dt))
        sem = lambda n: ctx.enter_context(nc.semaphore("m_" + n))
        ggb = sb("ggb", [P, D])
        ident, maskb = sb("ident", [P, P]), sb("maskb", [P, P])
        qT, kT, mb = (sb(n, [P, 2, MH, P]) for n in ("qT", "kT", "mb"))
        v = sb("v", [P, 2, MH, VW])
        so, szg = sb("so", [P, 2, MH, MD]), sb("szg", [P, 2, MH, MD])
        sbt, xt, ot = sb("sbt", [P, 2, MH, P]), sb("xt", [P, 2, D]), sb("ot", [P, 2, D])
        gap, dwt = sb("gap", [P, MH, P]), sb("dwt", [P, MH, P])
        wq, qs, pm, kn = (sb(n, [P, MH, P]) for n in ("wq", "qs", "pm", "kn"))
        state = sb("state", [P, MH, VW])
        dneg, den, rden = (sb(n, [P, MH]) for n in ("dneg", "den", "rden"))
        hp, hf = sb("hp", [P, MH, MD]), sb("hf", [P, MH, MD])
        sq, sqy = sb("sq", [P, MH, MD], BF16), sb("sqy", [P, 2, CH], BF16)
        yt = sb("yt", [P, 2, CH])
        ss, sv, sl, s0, s1, s2, s3 = (sb(n, [P, MH]) for n in ("ss", "sv", "sl", "s0", "s1", "s2", "s3"))
        ys, yv, yl, y0, y1, y2, y3 = (sb(n, [P, 2]) for n in ("ys", "yv", "yl", "y0", "y1", "y2", "y3"))
        shi, slo = sb("shi", [P, 2, MH, P], F32R), sb("slo", [P, 2, MH, P], F32R)
        mhi, mlo = sb("mhi", [P, MH, P], F32R), sb("mlo", [P, MH, P], F32R)
        t_ps, s_ps = ps("t", [P, MH, P]), ps("s", [P, MH, P])
        n_ps = [ps(f"n{k}", [P, 2, VW]) for k in range(2)]
        u_ps = [ps(f"u{k}", [P, 2, VW]) for k in range(2)]
        y_ps = [ps(f"y{k}", [P, CH]) for k in range(2)]

        names = ("const c_in k_tr s_done gap_done dwt_done wq_done qs_done pm_done kn_done n_done u_done "
                 "state_done den_step hp_done sq_done sv_done sr_done s_step hf_done h_tr mhi_done mlo_done shi_done slo_done "
                 "held y_done yc_done ysq_done yv_done yr_done y_step o_done fin_done").split()
        e = {n: sem(n) for n in names}
        ch_in, x_in, out_st = ([sem(f"{n}{p}") for p in range(2)] for n in ("ch_in", "x_in", "out_st"))
        act_held = sem("act_held")
        block = ctx.enter_context(nc.Block())

        def after(eng, semaphore, value):
            if not isinstance(value, int) or value > 0:
                eng.wait_ge(semaphore, value)

        def over_chunks(eng, body, ahead):
            body(0, 0, 0)
            body(1, 0, 1)
            pairs = (NT - 2 - ahead) // 2
            with eng.Fori(0, pairs) as i:
                for p in range(2):
                    body(2 * i + (2 + p), i + 1, p)
            for c in range(2 + 2 * pairs, NT):
                body(c, c // 2, c % 2)

        @block.sync
        def _(sp):
            def load(c, p):
                dst = [(qT, d["mlq"][c]), (kT, d["mlk"][c])]
                for tile, src in dst:
                    sp.dma_start(tile[:, p], src).then_inc(ch_in[p], 16)
                rows = slice(c * P, (c + 1) * P) if isinstance(c, int) else bass.ds(c * P, P)
                sp.dma_start(v[:, p, :, 0:MD], d["v"][rows, :].rearrange("t (h e) -> t h e", h=MH)).then_inc(ch_in[p], 16)
                sp.dma_start(so[:, p], d["so"][rows, :].rearrange("t (h e) -> t h e", h=MH)).then_inc(ch_in[p], 16)
                sp.dma_start(szg[:, p], d["szg"][rows, :].rearrange("t (h e) -> t h e", h=MH)).then_inc(ch_in[p], 16)
                sp.dma_start(mb[:, p], d["m"][:, rows].unsqueeze(0).to_broadcast([P, MH, P])).then_inc(ch_in[p], 16)
                sp.dma_start(sbt[:, p], d["hsb"][c].rearrange("(k p) t -> p k t", p=P)).then_inc(ch_in[p], 16)

            def load_x(c, p):
                rows = slice(c * P, (c + 1) * P) if isinstance(c, int) else bass.ds(c * P, P)
                sp.dma_start(xt[:, p], x[0, rows, :]).then_inc(x_in[p], 16)

            load(0, 0)
            load_x(0, 0)
            sp.dma_start(ggb[:], gg_d.to_broadcast([P, D])).then_inc(e["c_in"], 16)

            def store(c, p):
                after(sp, e["fin_done"], c + 1)
                rows = slice(c * P, (c + 1) * P) if isinstance(c, int) else bass.ds(c * P, P)
                sp.sem_inc(e["held"], 1)
                sp.dma_start(y[0, rows, :], ot[:, p]).then_inc(out_st[p], 16)

            def body(c, half, p):
                first, last = isinstance(c, int) and c == 0, isinstance(c, int) and c == NT - 1
                if not last:
                    after(sp, e["hf_done"], MH * c)
                    after(sp, e["slo_done"], c)
                    after(sp, e["state_done"], MH * (c + 1))
                    sp.sem_inc(e["held"], 1)
                    load(c + 1, 1 - p)
                if not first:
                    store(c - 1, 1 - p)
                if not last:
                    load_x(c + 1, 1 - p)

            over_chunks(sp, body, 2)
            store(NT - 1, (NT - 1) % 2)
            for p in range(2):
                sp.wait_ge(out_st[p], 16 * (NT // 2 + 1))

        @block.gpsimd
        def _(pool):
            identity(pool, ident[:], e["const"], 0)
            pool.memset(maskb[:], 0.0).then_inc(e["const"], 1)
            pool.wait_ge(e["const"], 3)
            pool.affine_select(out=maskb[:], in_=maskb[:], compare_op=ALU.is_ge, fill=BIG, base=0,
                               pattern=[[1, P]], channel_multiplier=-1).then_inc(e["const"], 1)
            pool.memset(v[:, :, :, MD:VW], 1.0).then_inc(e["const"], 1)
            pool.memset(state[:], 0.0).then_inc(e["state_done"], MH)

            def body(c, half, p):
                after(pool, ch_in[p], 112 * half + 112)
                after(pool, e["wq_done"], MH * (c + 1))
                after(pool, e["n_done"], c)
                pool.tensor_tensor(qs[:], qT[:, p], wq[:], ALU.mult).then_inc(e["qs_done"], 1)
                after(pool, e["shi_done"], c + 1)
                pool.tensor_tensor(slo[:, p], sbt[:, p], shi[:, p].bitcast(F32), ALU.subtract).then_inc(e["slo_done"], 1)
                if not (isinstance(c, int) and c == 0):
                    pool.wait_ge(x_in[1 - p], 16 * (half + p))
                    pool.wait_ge(e["o_done"], 2 * c)
                    pool.tensor_tensor(ot[:, 1 - p], ot[:, 1 - p], xt[:, 1 - p], ALU.add).then_inc(e["fin_done"], 1)

            over_chunks(pool, body, 0)
            pool.wait_ge(x_in[1], 16 * (NT // 2))
            pool.wait_ge(e["o_done"], 2 * NT)
            pool.tensor_tensor(ot[:, 1], ot[:, 1], xt[:, 1], ALU.add).then_inc(e["fin_done"], 1)

        @block.tensor
        def _(pe):
            pe.wait_ge(e["const"], 5)

            def turn_and_score(c, half, p):
                after(pe, ch_in[p], 112 * half + 112)
                after(pe, e["mlo_done"], c - 1)
                for h in range(MH):
                    last = pe.transpose(t_ps[:, h], kT[:, p, h], ident[:])
                last.then_inc(e["k_tr"], 1)
                after(pe, e["pm_done"], c)
                for h in range(MH):
                    last = pe.matmul(s_ps[:, h], kT[:, p, h], qT[:, p, h], start=True, stop=True)
                last.then_inc(e["s_done"], 1)

            def project(ks, parts, nb):
                for k in ks:
                    hi, lo = parts[0][:, k % MH], parts[1][:, k % MH]
                    cc = slice(nb * CH, (nb + 1) * CH)
                    for q, (a, b) in enumerate(((hi, whi), (hi, wlo), (lo, whi))):
                        last = pe.matmul(y_ps[nb][:], a, b[:, k, cc], start=(k == MH and q == 0), stop=(k == MH - 1 and q == 2))
                return last

            def project_sb(c, p):
                after(pe, e["slo_done"], c + 1)
                for nb in range(2):
                    after(pe, e["yc_done"], 2 * c - 1 + nb)
                    project(range(MH, KT), (shi[:, p], slo[:, p]), nb)

            def turn_h(c):
                after(pe, e["hf_done"], MH * (c + 1))
                after(pe, e["kn_done"], MH * (c + 2 if not (isinstance(c, int) and c == NT - 1) else c + 1))
                for h in range(MH):
                    last = pe.transpose(t_ps[:, h], hf[:, h], ident[:])
                last.then_inc(e["h_tr"], 1)

            def project_ml(c, p):
                after(pe, e["mlo_done"], c + 1)
                for nb in range(2):
                    project(range(MH), (mhi, mlo), nb).then_inc(e["y_done"], 1)

            def recur(c, p):
                after(pe, e["pm_done"], c + 1)
                after(pe, e["qs_done"], c + 1)
                after(pe, e["state_done"], MH * (c + 1))
                after(pe, e["hp_done"], MH * c)
                for h in range(MH):
                    dst = n_ps[h // 2][:, h % 2]
                    pe.matmul(dst, pm[:, h], v[:, p, h], start=(h % 2 == 0), stop=False, skip_group_check=True)
                    last = pe.matmul(dst, qs[:, h], state[:, h], start=False, stop=(h % 2 == 1), skip_group_check=True)
                last.then_inc(e["n_done"], 1)
                after(pe, e["kn_done"], MH * (c + 1))
                for h in range(MH):
                    last = pe.matmul(u_ps[h // 2][:, h % 2], kn[:, h], v[:, p, h], start=True, stop=True)
                last.then_inc(e["u_done"], 1)

            def body(c, half, p):
                turn_and_score(c, half, p)
                first = isinstance(c, int) and c == 0
                if not first:
                    project_sb(c - 1, 1 - p)
                    turn_h(c - 1)
                recur(c, p)
                if not first:
                    project_ml(c - 1, 1 - p)

            body(0, 0, 0)
            body(1, 0, 1)
            with pe.Fori(0, NT // 2 - 1) as i:
                for p in range(2):
                    body(2 * i + (2 + p), i + 1, p)
            project_sb(NT - 1, 1)
            turn_h(NT - 1)
            project_ml(NT - 1, 1)

        @block.scalar
        def _(act):
            def split_h(c):
                after(act, e["h_tr"], c + 1)
                after(act, e["y_done"], 2 * c)
                act.copy(mhi[:], t_ps[:]).then_inc(e["mhi_done"], 1)

            def out_y(c):
                after(act, e["o_done"], 2 * c)
                for nb in range(2):
                    after(act, e["y_done"], 2 * c + 1 + nb)
                    act.copy(yt[:, nb], y_ps[nb][:]).then_inc(e["yc_done"], 1)
                after(act, e["yv_done"], c)
                for nb in range(2):
                    after(act, e["yc_done"], 2 * c + 1 + nb)
                    act.activation(sqy[:, nb], yt[:, nb], ACT.Square, accum_out=ys[:, nb:nb + 1]).then_inc(e["ysq_done"], 1)
                after(act, e["yv_done"], c + 1)
                act.activation(yl[:, 0:1], yv[:, 0:1], ACT.Ln).then_inc(e["yr_done"], 1)
                after(act, e["yr_done"], 2 * c + 1)
                act.activation(y0[:, 0:1], yl[:, 0:1], ACT.Exp, scale=-0.5).then_inc(e["yr_done"], 1)

            def body(c, half, p):
                dyn = (lambda t, h: t[:, c, h:h + 1]) if isinstance(c, int) else (lambda t, h: t[:, bass.ds(c, 1), h])
                dynm = (lambda t, h: t[:, h, c:c + 1]) if isinstance(c, int) else (lambda t, h: t[:, h, bass.ds(c, 1)])
                after(act, ch_in[p], 112 * half + 112)
                after(act, e["qs_done"], c)
                act.sem_inc(act_held, 1)
                for h in range(MH):
                    act.activation(wq[:, h], mb[:, p, h], ACT.Exp, scale=-1.0, bias=dynm(cols["mprev"], h)).then_inc(e["wq_done"], 1)
                after(act, e["gap_done"], MH * (c + 1))
                after(act, e["pm_done"], c)
                act.activation(dwt[:], gap[:], ACT.Exp, scale=-1.0).then_inc(e["dwt_done"], 1)
                after(act, e["k_tr"], c + 1)
                after(act, e["u_done"], c)
                act.sem_inc(act_held, 1)
                for h in range(MH):
                    act.activation(kn[:, h], t_ps[:, h], ACT.Copy, scale=dyn(cols["wk"], h)).then_inc(e["kn_done"], 1)
                after(act, e["y_done"], 2 * (c - 1))
                act.copy(shi[:, p], sbt[:, p]).then_inc(e["shi_done"], 1)
                first = isinstance(c, int) and c == 0
                if not first:
                    split_h(c - 1)
                after(act, e["hp_done"], MH * (c + 1))
                after(act, e["sv_done"], c)
                for h in range(MH):
                    act.activation(sq[:, h], hp[:, h], ACT.Square, accum_out=ss[:, h:h + 1]).then_inc(e["sq_done"], 1)
                after(act, e["sv_done"], c + 1)
                act.activation(sl[:], sv[:], ACT.Ln).then_inc(e["sr_done"], 1)
                after(act, e["sr_done"], 2 * c + 1)
                act.activation(s0[:], sl[:], ACT.Exp, scale=-0.5).then_inc(e["sr_done"], 1)
                if not first:
                    out_y(c - 1)

            act.preload_act_table_set("natural_log_exp_and_others")
            body(0, 0, 0)
            body(1, 0, 1)
            with act.Fori(0, NT // 2 - 1) as i:
                for p in range(2):
                    body(2 * i + (2 + p), i + 1, p)
            split_h(NT - 1)
            out_y(NT - 1)

        @block.vector
        def _(dve):
            for p in range(2):
                dve.sem_inc(out_st[p], 16)
            dve.wait_ge(e["c_in"], 16)
            dve.wait_ge(e["const"], 4)

            def newton(step, base, r0, var, t1, t2, r, n):
                dve.tensor_tensor(t1[:, 0:n], r0[:, 0:n], r0[:, 0:n], ALU.mult).then_inc(step, 1)
                dve.wait_ge(step, base + 1)
                dve.tensor_tensor(t2[:, 0:n], t1[:, 0:n], var[:, 0:n], ALU.mult).then_inc(step, 1)
                dve.wait_ge(step, base + 2)
                dve.tensor_scalar(t1[:, 0:n], t2[:, 0:n], -0.5, 1.5, ALU.mult, ALU.add).then_inc(step, 1)
                dve.wait_ge(step, base + 3)
                dve.tensor_tensor(r[:, 0:n], r0[:, 0:n], t1[:, 0:n], ALU.mult).then_inc(step, 1)
                dve.wait_ge(step, base + 4)

            def low_h(c):
                after(dve, e["mhi_done"], c + 1)
                dve.tensor_tensor(mlo[:], t_ps[:], mhi[:].bitcast(F32), ALU.subtract).then_inc(e["mlo_done"], 1)

            def norm_y(c, p, stored):
                after(dve, e["ysq_done"], 2 * c + 2)
                dve.tensor_tensor(y1[:, 0:1], ys[:, 0:1], ys[:, 1:2], ALU.add).then_inc(e["y_step"], 1)
                dve.wait_ge(e["y_step"], 5 * c + 1)
                dve.tensor_scalar(yv[:, 0:1], y1[:, 0:1], 1.0 / D, EPS, ALU.mult, ALU.add).then_inc(e["yv_done"], 1)
                after(dve, e["yr_done"], 2 * c + 2)
                newton(e["y_step"], 5 * c + 1, y0, yv, y1, y2, y3, 1)
                after(dve, out_st[p], stored)
                for nb in range(2):
                    cc = slice(nb * CH, (nb + 1) * CH)
                    dve.scalar_tensor_tensor(out=ot[:, p, cc], in0=yt[:, nb], scalar=y3[:, 0:1], in1=ggb[:, cc],
                                             op0=ALU.mult, op1=ALU.mult).then_inc(e["o_done"], 1)

            def body(c, half, p):
                dyn = (lambda t, h: t[:, c, h:h + 1]) if isinstance(c, int) else (lambda t, h: t[:, bass.ds(c, 1), h])
                first = isinstance(c, int) and c == 0
                after(dve, ch_in[p], 112 * half + 112)
                after(dve, e["dwt_done"], c)
                for h in range(MH):
                    dve.scalar_tensor_tensor(out=gap[:, h], in0=mb[:, p, h], scalar=dyn(cols["u"], h), in1=maskb[:],
                                             op0=ALU.subtract, op1=ALU.max).then_inc(e["gap_done"], 1)
                after(dve, e["dwt_done"], c + 1)
                after(dve, e["s_done"], c + 1)
                after(dve, e["n_done"], c)
                dve.tensor_tensor(pm[:], s_ps[:], dwt[:], ALU.mult).then_inc(e["pm_done"], 1)
                if not first:
                    low_h(c - 1)
                after(dve, e["n_done"], c + 1)
                for b in range(2):
                    fl = cols["floor"][:, c, 2 * b:2 * b + 2] if isinstance(c, int) else cols["floor"][:, bass.ds(c, 1), 2 * b:2 * b + 2].rearrange("p a h -> p (a h)")
                    dve.scalar_tensor_tensor(out=dneg[:, 2 * b:2 * b + 2], in0=n_ps[b][:, :, MD], scalar=-1.0, in1=fl,
                                             op0=ALU.mult, op1=ALU.max).then_inc(e["den_step"], 1)
                dve.wait_ge(e["den_step"], 5 * c + 2)
                for b in range(2):
                    dve.tensor_tensor(den[:, 2 * b:2 * b + 2], n_ps[b][:, :, MD], dneg[:, 2 * b:2 * b + 2],
                                      ALU.max).then_inc(e["den_step"], 1)
                dve.wait_ge(e["den_step"], 5 * c + 4)
                dve.reciprocal(rden[:], den[:]).then_inc(e["den_step"], 1)
                dve.wait_ge(e["den_step"], 5 * c + 5)
                for h in range(MH):
                    dve.scalar_tensor_tensor(out=hp[:, h], in0=n_ps[h // 2][:, h % 2, 0:MD], scalar=rden[:, h:h + 1], in1=so[:, p, h],
                                             op0=ALU.mult, op1=ALU.mult).then_inc(e["hp_done"], 1)
                after(dve, e["u_done"], c + 1)
                for h in range(MH):
                    dve.scalar_tensor_tensor(out=state[:, h], in0=state[:, h], scalar=dyn(cols["decay"], h), in1=u_ps[h // 2][:, h % 2],
                                             op0=ALU.mult, op1=ALU.add).then_inc(e["state_done"], 1)
                after(dve, e["sq_done"], MH * (c + 1))
                dve.tensor_scalar(sv[:], ss[:], 1.0 / MD, EPS, ALU.mult, ALU.add).then_inc(e["sv_done"], 1)
                after(dve, e["sr_done"], 2 * c + 2)
                newton(e["s_step"], 4 * c, s0, sv, s1, s2, s3, MH)
                after(dve, e["h_tr"], c)
                for h in range(MH):
                    dve.scalar_tensor_tensor(out=hf[:, h], in0=hp[:, h], scalar=s3[:, h:h + 1], in1=szg[:, p, h],
                                             op0=ALU.mult, op1=ALU.mult).then_inc(e["hf_done"], 1)
                if not first:
                    norm_y(c - 1, 1 - p, 16 * half + 16 * p)

            body(0, 0, 0)
            body(1, 0, 1)
            with dve.Fori(0, NT // 2 - 1) as i:
                for p in range(2):
                    body(2 * i + (2 + p), i + 1, p)
            low_h(NT - 1)
            norm_y(NT - 1, 1, 16 * NT // 2)


def program(nc, x, c, w_ada, b_ada, g_pre, w_in, b_igate, b_fgate, conv_w, conv_b, g_ml_head, w_out, g_post, y):
    def scratch(name, *shape):
        return nc.dram_tensor("scratch_" + name, shape, F32, kind="Internal").ap()

    hT_d = scratch("hT", NCH + 2, P, KT * CH)
    gg_d = scratch("gg", 1, D)
    d = dict(mlq=scratch("mlq", NT, P, MH, P), mlk=scratch("mlk", NT, P, MH, P),
             v=scratch("v", S, 512), so=scratch("so", S, 512), szg=scratch("szg", S, 512),
             sbv=scratch("sbv", S + 1, 512), sbz=scratch("sbz", 512, S), gates=scratch("gates", 8, S),
             sqh=scratch("sqh", 512, S), sql=scratch("sql", 512, S), skh=scratch("skh", 512, S), skl=scratch("skl", 512, S),
             dw=scratch("dw", SH, NCH, P, TPC, P), hsb=scratch("hsb", NT, 512, P), m=scratch("m", MH, S))
    stage_norm(nc, x, c, w_ada, b_ada, g_pre, g_post, hT_d, gg_d)
    stage_project(nc, w_in, b_igate, b_fgate, conv_w, conv_b, g_ml_head, hT_d, d)
    with ExitStack() as ctx:
        cols = {k: ctx.enter_context(nc.sbuf_tensor("c_" + k, [P, NT, MH], F32)) for k in ("u", "wk", "decay", "floor")}
        cols["mprev"] = ctx.enter_context(nc.sbuf_tensor("c_mprev", [P, MH, NT], F32))
        wout_hi, wout_lo = (ctx.enter_context(nc.sbuf_tensor("c_" + k, [P, KT, D], F32R)) for k in ("wout_hi", "wout_lo"))
        stage_attend(nc, d, cols, wout_hi, wout_lo, w_out)
        stage_mix(nc, d, cols, x, wout_hi, wout_lo, gg_d, y)


def kernel(x, c, w_ada, b_ada, g_pre, w_in, b_igate, b_fgate, conv_w, conv_b, g_ml_head, w_out, g_post):
    import numpy as np
    import concourse.bacc as bacc
    from concourse.bass_utils import run_bass_kernel_spmd as run

    nc = bacc.Bacc("TRN2", target_bir_lowering=False, num_devices=1)
    given = dict(x=x, c=c, w_ada=w_ada, b_ada=b_ada, g_pre=g_pre, w_in=w_in, b_igate=b_igate, b_fgate=b_fgate,
                 conv_w=conv_w, conv_b=conv_b, g_ml_head=g_ml_head, w_out=w_out, g_post=g_post)
    arrays = {"in_" + k: np.ascontiguousarray(a) for k, a in given.items()}
    aps = [nc.dram_tensor(k, a.shape, F32, kind="ExternalInput").ap() for k, a in arrays.items()]
    y = nc.dram_tensor("out_y", (1, S, D), F32, kind="ExternalOutput").ap()
    program(nc, *aps, y)
    return run(nc, [arrays], core_ids=[0]).results[0]["out_y"]
```

```python
import concourse.bass as bass
from concourse import mybir
from contextlib import ExitStack

F32 = mybir.dt.float32
F32R = mybir.dt.float32r
BF16 = mybir.dt.bfloat16
ALU = mybir.AluOpType
ACT = mybir.ActivationFunctionType

P = 128
D = 1024
S = 4096
KT = D // P
CH = 512
NCH = S // CH
TPC = CH // P
NT = S // P
MH, MD = 4, 128
SH, SD = 8, 64
EPS = 1e-6
K_SCALE = float(MD) ** -0.5
Z_SCALE = float(SD) ** -0.5
BIG = 1.0e30

C_QK, C_V, C_O, C_Z, C_G = 0, 1024, 1536, 2048, 2560
C_SQ, C_SK, C_SV, C_SZ = 2568, 3080, 3592, 4104


class Count:

    def __init__(self, start=0):
        self.now, self.reg, self.per = start, None, 0

    def enter(self, reg, per):
        self.first, self.reg, self.per = self.now, reg, per

    def leave(self, trips):
        assert self.now - self.first == self.per, (self.now - self.first, self.per)
        self.now, self.reg = self.first + self.per * trips, None

    def value(self, more=0):
        if self.reg is None or not self.per:
            return self.now + more
        return self.reg * self.per + (self.now + more)

    def up(self, k=1):
        self.now += k
        return self.value()


def identity(pool, tile, sem, n):
    pool.memset(tile, 0.0).then_inc(sem, 1)
    pool.wait_ge(sem, n + 1)
    pool.affine_select(out=tile, in_=tile, compare_op=ALU.not_equal, fill=1.0, base=0,
                       pattern=[[-1, P]], channel_multiplier=1).then_inc(sem, 1)


def norm_tiles(nc, ctx):
    sb = lambda n, s: ctx.enter_context(nc.sbuf_tensor("n_" + n, s, F32, side="right"))
    kept = {n: sb(n, [P, KT]) for n in ("csil", "acol", "shcol")}
    kept["xt"] = sb("xt", [P, 2, TPC, D])
    kept["x_in"] = [ctx.enter_context(nc.semaphore(f"n_x_in{p}")) for p in range(2)]
    return kept


def chunks_of_x(x):
    return x.rearrange("b (n i p) d -> (b n) p i d", i=TPC, p=P)


def modulation_row(pe, row, csil, w):
    for k in range(KT):
        last = pe.matmul(row, csil[:, k:k + 1], w[:, k], start=(k == 0), stop=(k == KT - 1))
    return last


def stage_modulate(nc, x, c, w_ada, b_ada, g_pre, kept):
    NB = 2 * D // CH
    csil, acol, shcol, xt, x_in = (kept[k] for k in ("csil", "acol", "shcol", "xt", "x_in"))
    with ExitStack() as ctx:
        sb = lambda n, s, d=F32: ctx.enter_context(nc.sbuf_tensor("n_" + n, s, d))
        sem = lambda n: ctx.enter_context(nc.semaphore("n_" + n))
        wada = sb("wada", [P, NB, KT, CH])
        ccol, csig, gcol = sb("ccol", [P, KT]), sb("csig", [P, KT]), sb("gcol", [P, KT])
        brow, mrow, one = sb("brow", [1, 2 * D]), sb("mrow", [1, 2 * D]), sb("one", [1, 1])
        bank = [ctx.enter_context(nc.psum_tensor(f"n_row{k}", [P, CH], F32)) for k in range(NB + 1)]
        small_in, w_in = sem("small_in"), [sem(f"w_in{b}") for b in range(NB)]
        csig_ready, csil_ready = sem("csig_ready"), sem("csil_ready")
        row_done, mrow_ready, col_done, col_ready = sem("row_done"), sem("mrow_ready"), sem("col_done"), sem("col_ready")
        block = ctx.enter_context(nc.Block())

        @block.sync
        def _(sp):
            sp.dma_start(ccol[:], c.rearrange("b (k p) -> p (b k)", p=P), allow_slow_non_contiguous=True).then_inc(small_in, 16)
            sp.dma_start(gcol[:], g_pre.rearrange("(k p) -> p k", p=P), allow_slow_non_contiguous=True).then_inc(small_in, 16)
            sp.dma_start(brow[:], b_ada[0:2 * D].rearrange("(a n) -> a n", a=1)).then_inc(small_in, 16)
            for b in range(NB):
                sp.dma_start(wada[:, b], w_ada[:, b * CH:(b + 1) * CH].rearrange("(k p) n -> p k n", p=P)).then_inc(w_in[b], 16)
            for p in range(2):
                sp.dma_start(xt[:, p], chunks_of_x(x)[p]).then_inc(x_in[p], 16)

        @block.gpsimd
        def _(pool):
            pool.memset(one[:], 1.0).then_inc(csil_ready, 1)

        @block.scalar
        def _(act):
            act.wait_ge(small_in, 48)
            act.activation(csig[:], ccol[:], ACT.Sigmoid).then_inc(csig_ready, 1)

        @block.vector
        def _(dve):
            dve.wait_ge(small_in, 48)
            dve.wait_ge(csig_ready, 1)
            dve.tensor_tensor(csil[:], csig[:], ccol[:], ALU.mult).then_inc(csil_ready, 1)
            for b in range(NB):
                dve.wait_ge(row_done, b + 1)
                dve.tensor_tensor(mrow[0:1, b * CH:(b + 1) * CH], bank[b][0:1, :], brow[0:1, b * CH:(b + 1) * CH],
                                  ALU.add).then_inc(mrow_ready, 1)
            dve.wait_ge(col_done, 1)
            dve.tensor_copy(shcol[:], bank[NB][:, 0:KT]).then_inc(col_ready, 1)
            dve.scalar_tensor_tensor(out=acol[:], in0=bank[NB][:, KT:2 * KT], scalar=1.0, in1=gcol[:],
                                     op0=ALU.add, op1=ALU.mult).then_inc(col_ready, 1)
            dve.wait_ge(col_ready, 2)

        @block.tensor
        def _(pe):
            pe.wait_ge(csil_ready, 2)
            for b in range(NB):
                pe.wait_ge(w_in[b], 16)
                modulation_row(pe, bank[b][0:1, :], csil, wada[:, b]).then_inc(row_done, 1)
            for b in range(NB):
                pe.wait_ge(mrow_ready, b + 1)
                for k in range(b * CH // P, (b + 1) * CH // P):
                    last = pe.matmul(bank[NB][:, k:k + 1], mrow[0:1, k * P:(k + 1) * P], one[:], start=True, stop=True)
            last.then_inc(col_done, 1)


def stage_norm(nc, x, w_ada, b_ada, g_post, w_in, kept, weights, hT_d, gg_d):
    csil, acol, shcol, xt, x_in = (kept[k] for k in ("csil", "acol", "shcol", "xt", "x_in"))
    wraw, whi, wlo = weights
    W = whi.shape[2]
    with ExitStack() as ctx:
        sb = lambda n, s, d=F32: ctx.enter_context(nc.sbuf_tensor("n_" + n, s, d, side="right"))
        sem = lambda n: ctx.enter_context(nc.semaphore("n_" + n))
        wgate = sb("wgate", [P, KT, CH])
        grow, gprow = sb("grow", [1, D]), sb("gprow", [1, D])
        ident = sb("ident", [P, P])
        xn = sb("xn", [P, TPC, D])
        sq = sb("sq", [P, 2, D], BF16)
        ss = sb("ss", [P, 2, TPC])
        var, rt, r0, r1, r2, rr = (sb(n, [P, TPC]) for n in ("var", "rt", "r0", "r1", "r2", "rr"))
        hout = sb("hout", [P, 2, KT, CH])
        bank = [ctx.enter_context(nc.psum_tensor(f"n_bank{k}", [P, CH], F32)) for k in range(8)]

        small_in, gate_in, gate_in2 = sem("gsmall_in"), sem("gate_in"), sem("gate_in2")
        id_ready, gate_row, gate_done = sem("id_ready"), sem("gate_row"), sem("gate_done")
        tail_out = sem("tail_out")
        ss_ready, var_ready, rt_ready, r_step, xn_ready = sem("ss_ready"), sem("var_ready"), sem("rt_ready"), sem("r_step"), sem("xn_ready")
        tr_done, a_evac, v_evac = sem("tr_done"), sem("a_evac"), sem("v_evac")
        h_out = [sem("h_out0"), sem("h_out1")]
        wk_in, wk_step, wk_held = [sem("wk_in0"), sem("wk_in1")], sem("wk_step"), sem("wk_held")
        block = ctx.enter_context(nc.Block())
        x_v = chunks_of_x(x)

        @block.sync
        def _(sp):
            sp.dma_start(wgate[:], w_ada[:, 2 * D:2 * D + CH].rearrange("(k p) n -> p k n", p=P)).then_inc(gate_in, 16)
            sp.dma_start(grow[:], b_ada[2 * D:3 * D].rearrange("(a n) -> a n", a=1)).then_inc(small_in, 16)
            sp.dma_start(gprow[:], g_post.rearrange("(a n) -> a n", a=1)).then_inc(small_in, 16)

            def pair(i, ahead):
                for p in range(2):
                    sp.wait_ge(wk_step, 4 * i + 2 * p + 1)
                    rows = slice((2 * i + p) * P, (2 * i + p + 1) * P) if isinstance(i, int) else bass.ds((2 * i + p) * P, P)
                    sp.dma_start(wraw[:, p], w_in[rows, C_QK:C_QK + W]).then_inc(wk_in[p], 16)
                    if ahead:
                        sp.wait_ge(xn_ready, 2 * TPC * i + TPC * (p + 1))
                        sp.dma_start(xt[:, p], x_v[2 * i + (2 + p)]).then_inc(x_in[p], 16)
                    sp.wait_ge(a_evac, KT * i + KT // 2 * (p + 2))
                    sp.wait_ge(v_evac, KT * i + KT // 2 * (p + 2))
                    sp.dma_start(hT_d[2 * i + p], hout[:, p]).then_inc(h_out[p], 16)

            with sp.Fori(0, NCH // 2 - 1) as i:
                pair(i, True)
            pair(NCH // 2 - 1, False)
            sp.wait_ge(gate_done, 3)
            sp.dma_start(gg_d, grow[:]).then_inc(tail_out, 16)
            sp.wait_ge(tail_out, 16)
            for p in range(2):
                sp.wait_ge(h_out[p], 16 * (NCH // 2 + 1))

        @block.gpsimd
        def _(pool):
            identity(pool, ident[:], id_ready, 0)
            pool.sem_inc(wk_step, 3)
            pool.wait_ge(gate_row, 1)
            pool.dma_start(wgate[:], w_ada[:, 2 * D + CH:3 * D].rearrange("(k p) n -> p k n", p=P)).then_inc(gate_in2, 16)
            with pool.Fori(0, NCH // 2) as i:
                for p in range(2):
                    whi_k, wlo_k = whi[:, bass.ds(2 * i + p, 1)], wlo[:, bass.ds(2 * i + p, 1)]
                    pool.wait_ge(wk_in[p], 16 * i + 16)
                    pool.sem_inc(wk_held, 1)
                    pool.tensor_copy(whi_k, wraw[:, p:p + 1]).then_inc(wk_step, 1)
                    pool.wait_ge(wk_step, 4 * i + 2 * p + 4)
                    pool.sem_inc(wk_held, 1)
                    pool.tensor_tensor(wlo_k, wraw[:, p:p + 1], whi_k.bitcast(F32), ALU.subtract).then_inc(wk_step, 1)

        @block.scalar
        def _(act):
            act.sem_inc(a_evac, KT // 2)

            def measure(half, p):
                n = 2 * half + p
                act.wait_ge(x_in[p], 16 * half + 16)
                for t in range(TPC):
                    if t >= 2:
                        act.wait_ge(ss_ready, TPC * n + t - 1)
                    act.activation(sq[:, t % 2], xt[:, p, t], ACT.Square, accum_out=ss[:, p, t:t + 1]).then_inc(ss_ready, 1)
                act.wait_ge(var_ready, n + 1)
                act.activation(rt[:], var[:], ACT.Sqrt).then_inc(rt_ready, 1)

            def pair(i, last):
                for p in range(2):
                    if not (last and p):
                        measure(i + p, 1 - p)
                    for k in range(0, KT, 2):
                        act.wait_ge(tr_done, 2 * KT * i + KT * (p + 1) + k + 1)
                        if k == 0:
                            act.wait_ge(h_out[p], 16 * i + 16)
                        act.activation(hout[:, p, k], bank[k][:], ACT.Identity, bias=shcol[:, k:k + 1],
                                       scale=acol[:, k:k + 1]).then_inc(a_evac, 1)

            measure(0, 0)
            with act.Fori(0, NCH // 2 - 1) as i:
                pair(i, False)
            pair(NCH // 2 - 1, True)

        @block.vector
        def _(dve):
            for p in range(2):
                dve.sem_inc(h_out[p], 16)
            dve.sem_inc(v_evac, KT // 2)

            def gate_block(b):
                dve.wait_ge(gate_row, b + 1)
                dve.tensor_tensor(grow[0:1, b * CH:(b + 1) * CH], bank[0][0:1, :], grow[0:1, b * CH:(b + 1) * CH],
                                  ALU.add).then_inc(gate_done, 1)

            def root(half, p):
                n = 2 * half + p
                dve.wait_ge(ss_ready, TPC * n + TPC)
                dve.tensor_scalar(var[:], ss[:, p], 1.0 / D, EPS, ALU.mult, ALU.add).then_inc(var_ready, 1)
                dve.wait_ge(rt_ready, n + 1)
                dve.reciprocal(r0[:], rt[:]).then_inc(r_step, 1)
                dve.wait_ge(r_step, 5 * n + 1)
                dve.tensor_tensor(r1[:], r0[:], r0[:], ALU.mult).then_inc(r_step, 1)
                dve.wait_ge(r_step, 5 * n + 2)
                dve.tensor_tensor(r2[:], r1[:], var[:], ALU.mult).then_inc(r_step, 1)
                dve.wait_ge(r_step, 5 * n + 3)
                dve.tensor_scalar(r1[:], r2[:], -0.5, 1.5, ALU.mult, ALU.add).then_inc(r_step, 1)
                dve.wait_ge(r_step, 5 * n + 4)
                dve.tensor_tensor(rr[:], r0[:], r1[:], ALU.mult).then_inc(r_step, 1)
                dve.wait_ge(r_step, 5 * n + 5)

            def pair(i, last):
                for p in range(2):
                    dve.wait_ge(tr_done, 2 * KT * i + KT * (p + 1))
                    for t in range(TPC):
                        dve.tensor_scalar(xn[:, t], xt[:, p, t], rr[:, t:t + 1], None, ALU.mult).then_inc(xn_ready, 1)
                    if not (last and p):
                        root(i + p, 1 - p)
                    for k in range(1, KT, 2):
                        dve.wait_ge(tr_done, 2 * KT * i + KT * (p + 1) + k + 1)
                        if k == 1:
                            dve.wait_ge(h_out[p], 16 * i + 16)
                        dve.tensor_scalar(hout[:, p, k], bank[k][:], acol[:, k:k + 1], shcol[:, k:k + 1],
                                          ALU.mult, ALU.add).then_inc(v_evac, 1)

            dve.wait_ge(small_in, 32)
            root(0, 0)
            gate_block(0)
            pair(0, False)
            gate_block(1)
            dve.wait_ge(gate_done, 2)
            dve.tensor_tensor(grow[:], grow[:], gprow[:], ALU.mult).then_inc(gate_done, 1)
            with dve.Fori(1, NCH // 2 - 1) as i:
                pair(i, False)
            pair(NCH // 2 - 1, True)

        @block.tensor
        def _(pe):
            pe.wait_ge(gate_in, 16)
            modulation_row(pe, bank[0][0:1, :], csil, wgate).then_inc(gate_row, 1)
            pe.wait_ge(id_ready, 2)
            pe.wait_ge(gate_done, 1)
            pe.sem_inc(tr_done, KT)

            def pair(i):
                for p in range(2):
                    pe.wait_ge(xn_ready, 2 * TPC * i + TPC * (p + 1))
                    for k in range(KT):
                        pe.wait_ge(a_evac if k % 2 == 0 else v_evac, KT * i + KT // 2 * p + k // 2 + 1)
                        for t in range(TPC):
                            last = pe.transpose(bank[k][:, t * P:(t + 1) * P], xn[:, t, k * P:(k + 1) * P], ident[:])
                        last.then_inc(tr_done, 1)

            pair(0)
            pe.wait_ge(gate_in2, 16)
            pe.wait_ge(a_evac, KT + 1)
            modulation_row(pe, bank[0][0:1, :], csil, wgate).then_inc(gate_row, 1)
            pe.wait_ge(gate_done, 2)
            with pe.Fori(1, NCH // 2) as i:
                pair(i)


CONV, SPLIT, VO, ZV, GATED = range(5)
GROUPS = [
    (CONV, [(C_QK, 1024)]),
    (ZV, [(C_Z, 512), (C_SV, 512)]),
    (SPLIT, [(C_SQ, 1024)]),
    (VO, [(C_V, 1024)]),
    (GATED, [(C_SZ, 512), (C_G, 8)]),
]


def stage_project(nc, w_in, b_igate, b_fgate, conv_w, conv_b, g_ml, weights, hT_d, out):
    NG = len(GROUPS)
    W = 1024
    with ExitStack() as ctx:
        sb = lambda n, s, d=F32: ctx.enter_context(nc.sbuf_tensor("p_" + n, s, d))
        ps = lambda n, s, d=F32: ctx.enter_context(nc.psum_tensor("p_" + n, s, d))
        sem = lambda n: ctx.enter_context(nc.semaphore("p_" + n))
        wraw, whi, wlo = weights
        hraw = sb("hraw", [P, KT, CH])
        hhi, hlo = sb("hhi", [P, 2, KT, CH], F32R), sb("hlo", [P, 2, KT, CH], F32R)
        oa, ob = sb("oa", [P, 4, CH]), sb("ob", [P, 4, CH])
        u, y = sb("u", [P, 2, CH + 3]), sb("y", [P, 2, CH])
        tail = sb("tail", [P, 8, 3])
        cw, cb = sb("cw", [P, 4, 8]), sb("cb", [P, 8])
        gml = sb("gml", [P, CH])
        gbias = sb("gbias", [8, 1])
        bank = [ps(f"bank{k}", [P, CH]) for k in range(8)]

        small_in, h_in, w_ld = sem("small_in"), sem("h_in"), sem("w_ld")
        h_hi, h_lo, w_hi, w_lo = sem("h_hi"), sem("h_lo"), sem("w_hi"), sem("w_lo")
        full = [sem(f"full{b}") for b in range(8)]
        free = [sem(f"free{b}") for b in range(8)]
        ready = [sem(f"ready{s}") for s in range(4)]
        st_a, st_b = [sem(f"st_a{s}") for s in range(4)], [sem(f"st_b{s}") for s in range(4)]
        sig_step, conv_step, u_ready, conv_done = sem("sig_step"), sem("conv_step"), sem("u_ready"), sem("conv_done")
        zero_out, again = sem("zero_out"), sem("again")
        dv_in, dv_step, dv_out = sem("dv_in"), sem("dv_step"), sem("dv_out")
        pool_held = sem("pool_held")
        va, vb, vh = (sb(n, [P, CH // 2]) for n in ("va", "vb", "vh"))
        block = ctx.enter_context(nc.Block())

        def banks(kind):
            return 5 if kind == GATED else 8

        def uses(kind, s):
            return sum(b % 4 == s for b in range(banks(kind)))

        def by_ready(kind, b):
            return kind in (CONV, SPLIT) or (kind == ZV and b % 2 == 0)

        def ready_uses(kind, s):
            return sum(b % 4 == s and by_ready(kind, b) for b in range(banks(kind)))

        def split_after(kind):
            return {CONV: 2, GATED: 0}.get(kind, 1)

        def low_uses(kind, s):
            return uses(kind, s) if kind == SPLIT else 0

        def enter(cs, i, pers):
            for c, per in zip(cs, pers):
                c.enter(i, per)

        def leave(cs):
            for c in cs:
                c.leave(NCH // 2)

        @block.sync
        def _(sp):
            sp.dma_start(cw[:], conv_w.rearrange("j (m p) -> p j m", p=P), allow_slow_non_contiguous=True).then_inc(small_in, 16)
            sp.dma_start(cb[:], conv_b.rearrange("(m p) -> p m", p=P), allow_slow_non_contiguous=True).then_inc(small_in, 16)
            sp.dma_start(gbias[0:4], b_igate.rearrange("(p a) -> p a", a=1), allow_slow_non_contiguous=True).then_inc(small_in, 16)
            sp.dma_start(gbias[4:8], b_fgate.rearrange("(p a) -> p a", a=1), allow_slow_non_contiguous=True).then_inc(small_in, 16)
            sp.dma_start(gml[:], g_ml.rearrange("(a h) d -> a (h d)", a=1).to_broadcast([P, CH])).then_inc(small_in, 16)
            h_v = hT_d.rearrange("n p (k t) -> n p k t", k=KT)

            def load_w(cols):
                at = 0
                for c0, w in cols:
                    sp.dma_start(wraw[:, :, at:at + w], w_in[:, c0:c0 + w].rearrange("(k p) n -> p k n", p=P)).then_inc(w_ld, 16)
                    at += w

            qk_v = [out[k].rearrange("(n j) p h t -> n p j h t", j=TPC) for k in ("mlq", "mlk")]
            nat_v = {k: out[k].rearrange("(n i p) d -> n i p d", i=TPC, p=P) for k in ("v", "so", "szg")}
            nat_v["sbv"] = out["sbv"][1:S + 1, :].rearrange("(n i p) d -> n i p d", i=TPC, p=P)
            ch_v = {k: out[k].rearrange("(m p) (n t) -> n m p t", p=P, t=CH) for k in ("sqh", "sql", "skh", "skl", "sbz")}
            g_v = out["gates"].rearrange("g (n t) -> n g t", t=CH)

            def place(kind, b, n, low=False):
                if kind == CONV:
                    return qk_v[b // 4][n, :, :, b % 4, :]
                if kind == SPLIT:
                    return ch_v[("sq", "sk")[b // 4] + ("l" if low else "h")][n, b % 4]
                if kind in (VO, ZV):
                    return nat_v[(("v", "so") if kind == VO else ("szg", "sbv"))[b % 2]][n, b // 2]
                return ch_v["sbz"][n, b] if b < 4 else g_v[n]

            sp.dma_start(hraw[:], h_v[0]).then_inc(h_in, 16)
            sp.wait_ge(h_lo, 1)
            sp.dma_start(hraw[:], h_v[1]).then_inc(h_in, 16)
            sp.dma_start(hT_d[NCH:NCH + 2], hT_d[0:2]).then_inc(again, 16)
            sp.wait_ge(again, 16)
            rdy, freed, stored, stored_low = ([Count() for _ in range(4)], [Count(1) for _ in range(8)],
                                              [Count(1) for _ in range(4)], [Count(1) for _ in range(4)])
            h_split = Count(1)
            for g, (kind, _) in enumerate(GROUPS):
                if g + 1 < NG:
                    if g:
                        sp.wait_ge(w_hi, KT * (g + 1))
                        sp.wait_ge(w_lo, KT * (g + 1))
                    load_w(GROUPS[g + 1][1])
                with sp.Fori(0, NCH // 2) as i:
                    enter(rdy, i, [2 * ready_uses(kind, s) for s in range(4)])
                    enter(freed, i, [2 * (b < banks(kind)) for b in range(8)])
                    enter(stored, i, [2 * uses(kind, s) for s in range(4)])
                    enter(stored_low, i, [2 * low_uses(kind, s) for s in range(4)])
                    h_split.enter(i, 2)
                    for p in range(2):
                        for b in range(banks(kind)):
                            s = b % 4
                            rows = 8 if b >= 4 and kind == GATED else P
                            tile = oa[0:rows, s]
                            if kind == CONV:
                                tile = tile.rearrange("p (j t) -> p j t", j=TPC)
                            stored[s].up()
                            freed[b].up()
                            if by_ready(kind, b):
                                sp.wait_ge(ready[s], rdy[s].up())
                            else:
                                sp.wait_ge(free[b], freed[b].value())
                            sp.dma_start(place(kind, b, 2 * i + p), tile).then_inc(st_a[s], 16)
                            if kind == SPLIT:
                                stored_low[s].up()
                                sp.wait_ge(free[b], freed[b].value())
                                sp.dma_start(place(kind, b, 2 * i + p, True), ob[:, s]).then_inc(st_b[s], 16)
                        sp.wait_ge(h_lo, h_split.up())
                        sp.dma_start(hraw[:], h_v[2 * i + (p + 2)]).then_inc(h_in, 16)
                    leave(rdy + freed + stored + stored_low + [h_split])
            sp.wait_ge(h_in, 16 * (NCH * NG + 2))
            for s in range(4):
                sp.wait_ge(st_a[s], 16 * stored[s].now)
                sp.wait_ge(st_b[s], 16 * stored_low[s].now)

        @block.tensor
        def _(pe):
            for b in range(8):
                pe.sem_inc(full[b], 1)
            got = Count()
            bank_free = [Count() for _ in range(8)]
            for g, (kind, _) in enumerate(GROUPS):
                with pe.Fori(0, NCH // 2) as i:
                    got.enter(i, 2)
                    enter(bank_free, i, [2 * (b < banks(kind)) for b in range(8)])
                    for p in range(2):
                        n = got.up()
                        pe.wait_ge(h_hi, n)
                        pe.wait_ge(h_lo, n)
                        for b in range(banks(kind)):
                            pe.wait_ge(free[b], bank_free[b].up())
                            for k in range(KT):
                                if p == 0 and b == 0:
                                    pe.wait_ge(w_hi, KT * g + k + 1)
                                    pe.wait_ge(w_lo, KT * g + k + 1)
                                if kind in (VO, ZV):
                                    t, c = slice((b // 2) * P, (b // 2 + 1) * P), slice((b % 2) * CH, (b % 2 + 1) * CH)
                                    dst = bank[b][:]
                                    hl = [(hhi[:, p, k, t], whi[:, k, c]), (hhi[:, p, k, t], wlo[:, k, c]), (hlo[:, p, k, t], whi[:, k, c])]
                                else:
                                    m = 8 if b >= 4 and kind == GATED else P
                                    c = slice(b * P, b * P + m)
                                    dst = bank[b][0:m, :]
                                    hl = [(whi[:, k, c], hhi[:, p, k]), (whi[:, k, c], hlo[:, p, k]), (wlo[:, k, c], hhi[:, p, k])]
                                for q, (stationary, moving) in enumerate(hl):
                                    last = pe.matmul(dst, stationary, moving, start=(k == 0 and q == 0), stop=(k == KT - 1 and q == 2))
                            last.then_inc(full[b], 1)
                    leave(bank_free + [got])

        @block.gpsimd
        def _(pool):
            pool.memset(vh[:], 0.0).then_inc(pool_held, 1)
            pool.wait_ge(pool_held, 1)
            for q in range(2):
                pool.dma_start(out["sbv"][0:1, q * 256:(q + 1) * 256], vh[0:1, :]).then_inc(zero_out, 16)
            pool.wait_ge(zero_out, 32)
            got, vin, vstep, vout = Count(1), Count(), Count(), Count()

            def hold(semaphore, value):
                pool.wait_ge(semaphore, value)
                pool.sem_inc(pool_held, 1)

            for g, (kind, _) in enumerate(GROUPS):
                dv = g in (2, 3)
                if g == 2:
                    for s in range(4):
                        pool.wait_ge(st_a[s], 16 * (2 * 2 * NCH + 1))
                with pool.Fori(0, NCH // 2) as i:
                    enter([got, vin, vstep, vout], i, [2 * (g == 0), 256 * dv, 24 * dv, 256 * dv])
                    for p in range(2):
                        if g == 0:
                            pool.wait_ge(h_hi, got.up())
                            pool.tensor_tensor(hlo[:, 1 - p], hraw[:], hhi[:, 1 - p].bitcast(F32), ALU.subtract).then_inc(h_lo, 1)
                        if not dv:
                            continue
                        for e in range(2):
                            row = 16 * P * (g - 2) + (4 * i + (2 * p + e)) * P
                            for q in range(2):
                                cols = slice(q * 256, (q + 1) * 256)
                                pool.dma_start(va[:], out["sbv"][bass.ds(row, P), cols]).then_inc(dv_in, 16)
                                pool.dma_start(vb[:], out["sbv"][bass.ds(row + 1, P), cols]).then_inc(dv_in, 16)
                                pool.wait_ge(dv_in, vin.up(32))
                                pool.tensor_tensor(va[:], va[:], vb[:], ALU.subtract).then_inc(dv_step, 1)
                                hold(dv_step, vstep.up())
                                pool.tensor_copy(vh[:].bitcast(F32R), va[:]).then_inc(dv_step, 1)
                                pool.wait_ge(dv_step, vstep.up())
                                pool.tensor_tensor(vb[:].bitcast(F32R), va[:], vh[:], ALU.subtract).then_inc(dv_step, 1)
                                hold(dv_step, vstep.up())
                                dst = out["dw"][4 * q:4 * q + 4, 4 * (g - 2) + i, :, 2 * p + e, :].rearrange("h p e -> p h e")
                                pool.dma_start(dst[:, :, 0:SD], vh[:].rearrange("p (h e) -> p h e", h=4)).then_inc(dv_out, 16)
                                pool.dma_start(dst[:, :, SD:P], vb[:].rearrange("p (h e) -> p h e", h=4)).then_inc(dv_out, 16)
                                hold(dv_out, vout.up(32))
                    leave([got, vin, vstep, vout])
            pool.wait_ge(dv_out, vout.now)

        @block.scalar
        def _(act):
            act.wait_ge(h_in, 16)
            act.copy(hhi[:, 0], hraw[:]).then_inc(h_hi, 1)
            for b in range(8):
                act.sem_inc(free[b], 1)
            act.sem_inc(w_hi, KT)
            act.sem_inc(w_lo, KT)
            got, wl = Count(1), Count()
            fulls, slot = [Count(1) for _ in range(8)], [Count() for _ in range(4)]
            cdone, freed = Count(), [Count(1) for _ in range(8)]
            for g, (kind, cols) in enumerate(GROUPS):
                width = sum(w for _, w in cols)
                if g:
                    act.wait_ge(w_ld, wl.up(16 * len(cols)))
                    last_bank = banks(GROUPS[g - 1][0]) - 1
                    act.wait_ge(full[last_bank], fulls[last_bank].value())
                    for k in range(KT):
                        act.copy(whi[:, k, 0:width], wraw[:, k, 0:width]).then_inc(w_hi, 1)
                with act.Fori(0, NCH // 2) as i:
                    conv = kind == CONV
                    enter([got, cdone], i, [2, 16 * conv])
                    enter(fulls, i, [2 * (b < banks(kind)) for b in range(8)])
                    enter(slot, i, [2 * uses(kind, s) for s in range(4)])
                    enter(freed, i, [2 * (b < banks(kind)) for b in range(8)])
                    for p in range(2):
                        def high_h():
                            act.wait_ge(h_in, 16 * got.up())
                            last_bank = banks(kind) - 1
                            act.wait_ge(full[last_bank], fulls[last_bank].value())
                            act.copy(hhi[:, 1 - p], hraw[:]).then_inc(h_hi, 1)

                        def conv_gate(b):
                            act.wait_ge(conv_done, cdone.up())
                            act.activation(ob[:, b % 4], y[:, b % 2], ACT.Sigmoid).then_inc(sig_step, 1)

                        for b in range(banks(kind)):
                            s = b % 4
                            act.wait_ge(full[b], fulls[b].up())
                            if kind == CONV:
                                act.copy(u[:, b % 2, 3:], bank[b][:]).then_inc(u_ready, 1)
                                if b:
                                    conv_gate(b - 1)
                            elif kind == SPLIT:
                                other = (b + 4) % 8
                                act.wait_ge(free[other], freed[other].value())
                                act.wait_ge(st_a[s], 16 * slot[s].up())
                                act.copy(oa[:, s].bitcast(F32R), bank[b][:]).then_inc(ready[s], 1)
                            elif kind == VO and b % 2:
                                act.wait_ge(st_a[s], 16 * slot[s].up())
                                act.activation(oa[:, s], bank[b][:], ACT.Sigmoid).then_inc(free[b], 1)
                            elif (kind == ZV and b % 2 == 0) or (kind == GATED and b < 4):
                                act.wait_ge(st_a[s], 16 * slot[s].up())
                                act.activation(ob[:, s], bank[b][:], ACT.Sigmoid).then_inc(sig_step, 1)
                            else:
                                slot[s].up()
                            freed[b].up()
                            if b == split_after(kind):
                                high_h()
                        if kind == CONV:
                            conv_gate(7)
                            for b in range(8):
                                slot[b % 4].up()
                    leave([got, cdone] + fulls + slot + freed)

        @block.vector
        def _(dve):
            for s in range(4):
                dve.sem_inc(st_a[s], 16)
                dve.sem_inc(st_b[s], 16)
            dve.wait_ge(h_hi, 1)
            dve.tensor_tensor(hlo[:, 0], hraw[:], hhi[:, 0].bitcast(F32), ALU.subtract).then_inc(h_lo, 1)
            dve.memset(tail[:], 0.0).then_inc(conv_step, 1)
            dve.wait_ge(conv_step, 1)
            dve.wait_ge(small_in, 80)
            fulls, slot, slot_b = [Count(1) for _ in range(8)], [Count() for _ in range(4)], [Count() for _ in range(4)]
            got, rdy, freed, ur, cs, sg = Count(1 + NCH), [Count() for _ in range(4)], [Count(1) for _ in range(8)], Count(), Count(1), Count()
            for g, (kind, cols) in enumerate(GROUPS):
                width = sum(w for _, w in cols)
                for k in range(KT if g else 0):
                    dve.wait_ge(w_hi, KT * g + k + 1)
                    dve.tensor_tensor(wlo[:, k, 0:width], wraw[:, k, 0:width], whi[:, k, 0:width].bitcast(F32),
                                      ALU.subtract).then_inc(w_lo, 1)
                with dve.Fori(0, NCH // 2) as i:
                    conv = kind == CONV
                    gated = {CONV: 8, ZV: 4, GATED: 4}.get(kind, 0)
                    enter([got, ur, cs, sg], i, [2 * (not conv), 16 * conv, 64 * conv, 2 * gated])
                    enter(freed, i, [2 * (b < banks(kind)) for b in range(8)])
                    enter(fulls, i, [2 * (b < banks(kind)) for b in range(8)])
                    enter(slot, i, [2 * uses(kind, s) for s in range(4)])
                    enter(slot_b, i, [2 * low_uses(kind, s) for s in range(4)])
                    enter(rdy, i, [2 * ready_uses(kind, s) for s in range(4)])
                    for p in range(2):
                        def conv_out(b):
                            s = b % 4
                            dve.wait_ge(sig_step, sg.up())
                            dve.wait_ge(st_a[s], 16 * slot[s].up())
                            dve.scalar_tensor_tensor(out=oa[:, s], in0=y[:, b % 2], scalar=1.0 if b < 4 else K_SCALE,
                                                     in1=ob[:, s], op0=ALU.mult, op1=ALU.mult).then_inc(ready[s], 1)

                        for b in range(banks(kind)):
                            s = b % 4
                            if kind == CONV:
                                fulls[b].up()
                                rdy[s].up()
                                uu, yy = u[:, b % 2], y[:, b % 2]
                                dve.wait_ge(u_ready, ur.up())
                                dve.wait_ge(free[b], freed[b].value())
                                dve.tensor_copy(uu[:, 0:3], tail[:, b]).then_inc(conv_step, 1)
                                dve.wait_ge(conv_step, cs.up())
                                dve.tensor_copy(tail[:, b], uu[:, CH:CH + 3]).then_inc(free[b], 1)
                                freed[b].up()
                                dve.tensor_scalar(yy, uu[:, 0:CH], cw[:, 0, b:b + 1], cb[:, b:b + 1], ALU.mult, ALU.add).then_inc(conv_step, 1)
                                for j in range(1, 4):
                                    dve.wait_ge(conv_step, cs.up())
                                    dve.scalar_tensor_tensor(out=yy, in0=uu[:, j:j + CH], scalar=cw[:, j, b:b + 1], in1=yy,
                                                             op0=ALU.mult, op1=ALU.add).then_inc(conv_step if j < 3 else conv_done, 1)
                                if b:
                                    conv_out(b - 1)
                                continue
                            dve.wait_ge(full[b], fulls[b].up())
                            freed[b].up()
                            if by_ready(kind, b):
                                rdy[s].up()
                            if kind == SPLIT:
                                slot[s].up()
                                dve.wait_ge(ready[s], rdy[s].value())
                                dve.wait_ge(st_b[s], 16 * slot_b[s].up())
                                dve.tensor_tensor(ob[:, s].bitcast(F32R), bank[b][:], oa[:, s], ALU.subtract).then_inc(free[b], 1)
                            elif (kind == ZV and b % 2 == 0) or (kind == GATED and b < 4):
                                dve.wait_ge(sig_step, sg.up())
                                dve.wait_ge(st_a[s], 16 * slot[s].up())
                                if kind == ZV:
                                    dve.wait_ge(ready[(s + 2) % 4], rdy[(s + 2) % 4].value())
                                    dve.tensor_tensor(y[:, 0], bank[b][:], ob[:, s], ALU.mult).then_inc(free[b], 1)
                                    dve.wait_ge(free[b], freed[b].value())
                                    dve.tensor_tensor(oa[:, s], y[:, 0], gml[:], ALU.mult).then_inc(ready[s], 1)
                                else:
                                    dve.tensor_tensor(oa[:, s], bank[b][:], ob[:, s], ALU.mult).then_inc(free[b], 1)
                            elif kind == GATED:
                                dve.wait_ge(st_a[s], 16 * slot[s].up())
                                dve.tensor_scalar(oa[0:8, s], bank[b][0:8, :], gbias[:], None, ALU.add).then_inc(free[b], 1)
                            elif kind == VO and b % 2:
                                slot[s].up()
                            else:
                                dve.wait_ge(st_a[s], 16 * slot[s].up())
                                dve.tensor_copy(oa[:, s], bank[b][:]).then_inc(free[b], 1)
                            if b == split_after(kind):
                                dve.wait_ge(h_hi, got.up())
                                dve.tensor_tensor(hlo[:, 1 - p], hraw[:], hhi[:, 1 - p].bitcast(F32), ALU.subtract).then_inc(h_lo, 1)
                        if kind == CONV:
                            conv_out(7)
                    leave([got, ur, cs, sg] + fulls + freed + slot + slot_b + rdy)


def stage_attend(nc, d, cols, wout_hi, wout_lo, w_out):
    STEPS = []
    n = 0
    for r in range(NCH):
        for j in range(NCH - 1 - r, -1, -1):
            STEPS += [(n, r, NCH - 1 - r, j, q) for q in range(TPC)]
            n += 1
    N = len(STEPS)
    row_last = {r: max(k for k, s in enumerate(STEPS) if s[1] == r) for r in range(NCH)}
    ZB, RB = 3, 3
    KB, PB = 3, 3
    LEAD = 6
    with ExitStack() as ctx:
        sb = lambda n, s, dt=F32: ctx.enter_context(nc.sbuf_tensor("a_" + n, s, dt))
        ps = lambda n, s, dt=F32: ctx.enter_context(nc.psum_tensor("a_" + n, s, dt))
        sem = lambda n: ctx.enter_context(nc.semaphore("a_" + n))
        q_sb = sb("q", [P, S], F32R)
        khi, klo = sb("khi", [P, S], F32R), sb("klo", [P, S], F32R)
        dw = sb("dw", [P, NT, P], F32R)
        keep = sb("keep", [P, KB, CH])
        prod = sb("prod", [P, PB, TPC, CH])
        hi, lo = sb("hi", [P, 4, CH], F32R), sb("lo", [P, 4, CH], F32R)
        tile = sb("tile", [P, CH])
        zeros = sb("zeros", [P, CH])
        ident, identb, maskb = sb("ident", [P, P]), sb("identb", [P, P], BF16), sb("maskb", [P, P], BF16)
        lowsum, osum, gate = sb("lowsum", [SD, CH]), sb("osum", [SD, 2, CH]), sb("gate", [SD, 2, CH])
        vrow, v_e = sb("vrow", [NT, SH * SD]), sb("v_e", [SD, SH * NT])
        ig, fg, soft, b, u, top, m = (sb(n, [P, P]) for n in ("ig", "fg", "soft", "b", "u", "top", "m"))
        ones, mcol_in = sb("ones", [P, P]), sb("mcol_in", [P, 1])
        b_before, tops, mlast_row, mprev_row = (sb(n, [1, MH, NT]) for n in ("b_before", "tops", "mlast_row", "mprev_row"))
        mlast, (xw, xs, xe, mcol) = sb("mlast", [P, MH, NT]), (sb(n, [P, NT, MH]) for n in ("xw", "xs", "xe", "mcol"))
        wout_raw = sb("wout_raw", [P, D])
        z = [ps(f"z{k}", [P, CH]) for k in range(ZB)]
        rt = [ps(f"rt{k}", [P, CH]) for k in range(RB)]
        acc = [ps(f"acc{k}", [P, CH]) for k in range(2)]

        const, v_in, ve_tr, ve_done = sem("const"), sem("v_in"), sem("ve_tr"), sem("ve_done")
        chunk_in = [sem(f"chunk_in{k}") for k in range(NCH)]
        z_done, keep_done, scan_done = sem("z_done"), sem("keep_done"), sem("scan_done")
        rt_done, hi_done, lo_done, av_done = sem("rt_done"), sem("hi_done"), sem("lo_done"), sem("av_done")
        tile_done, pool_lo_done = sem("tile_done"), sem("pool_lo_done")
        low_done, sum_done, add_done, gated = sem("low_done"), sem("sum_done"), sem("add_done"), sem("gated")
        gate_in, o_st = [sem("gate_in0"), sem("gate_in1")], [sem("o_st0"), sem("o_st1")]
        held = sem("held")
        g_in, g_const, g_act, g_dve, g_pe, m_out = (sem(n) for n in ("g_in", "g_const", "g_act", "g_dve", "g_pe", "m_out"))
        wout_in, wout_step = sem("wout_in"), sem("wout_step")
        block = ctx.enter_context(nc.Block())
        KEEP0, SCAN0, RT0, LO0, AV0, SUM0, TILE0 = ZB, KB, TPC * PB, RB - 1, 4, 2, 1

        def by_pool(k):
            return k % 4 == 2

        def pool_lows(k):
            return (k + 1) // 4

        def dve_lows(k):
            return k - pool_lows(k)

        NP, ND = pool_lows(N), dve_lows(N)

        def lo_col(k):
            _, _, c, j, q = STEPS[k]
            return q * P if c == j else 0

        def width(k):
            _, _, c, j, q = STEPS[k]
            return (q + 1) * P if c == j else CH

        @block.sync
        def _(sp):
            def load_chunk(k, h):
                t, hh = slice(k * CH, (k + 1) * CH), (slice(h * SD, (h + 1) * SD) if isinstance(h, int) else bass.ds(h * SD, SD))
                for tile, part, src in ((q_sb, 0, "sqh"), (q_sb, 1, "sql"), (khi, 0, "skh"), (khi, 1, "skh"), (klo, 0, "skl"), (klo, 1, "skl")):
                    sp.dma_start(tile[part * SD:(part + 1) * SD, t].bitcast(F32), d[src][hh, t]).then_inc(chunk_in[k], 16)
                sp.dma_start(dw[:, k * TPC:(k + 1) * TPC, :].bitcast(F32), d["dw"][h, k]).then_inc(chunk_in[k], 16)

            def load_gate(r, h):
                c, hh = NCH - 1 - r, (slice(h * SD, (h + 1) * SD) if isinstance(h, int) else bass.ds(h * SD, SD))
                sp.dma_start(gate[:, r % 2], d["sbz"][hh, c * CH:(c + 1) * CH]).then_inc(gate_in[r % 2], 16)

            for tile, row in ((fg, MH), (ig, 0)):
                sp.dma_start(tile[:], d["gates"][row:row + MH, :].rearrange("h (c t) -> (h c) t", t=P)).then_inc(g_in, 16)
            sp.dma_start(vrow[:], d["sbv"][1:S + 1, :].rearrange("(b r) e -> r b e", r=P)[P - 1]).then_inc(v_in, 16)
            load_chunk(NCH - 1, 0)
            load_gate(0, 0)
            load_gate(1, 0)
            for k in range(NCH - 2, -1, -1):
                load_chunk(k, 0)
            sp.dma_start(wout_raw[:], w_out[0:P, :]).then_inc(wout_in, 16)
            sp.wait_ge(g_dve, 14)
            sp.dma_start(d["m"].rearrange("h (c t) -> (h c) t", t=P), m[:]).then_inc(m_out, 16)

            def head(h, last):
                for r in range(NCH):
                    c = NCH - 1 - r
                    if not last:
                        sp.wait_ge(sum_done, NCH * h + (r + 1 + SUM0))
                        sp.sem_inc(held, 1)
                        load_chunk(c, h + 1)
                    sp.wait_ge(gated, NCH * h + (r + 1))
                    sp.sem_inc(held, 1)
                    hh = slice(h * SD, (h + 1) * SD) if isinstance(h, int) else bass.ds(h * SD, SD)
                    sp.dma_start(d["hsb"][c * TPC:(c + 1) * TPC, hh, :].rearrange("j e t -> e j t"),
                                 osum[:, r % 2].rearrange("e (j t) -> e j t", j=TPC)).then_inc(o_st[r % 2], 16)
                    if r + 2 < NCH:
                        load_gate(r + 2, h)
                    elif not last:
                        load_gate(r + 2 - NCH, h + 1)
                if not last:
                    sp.wait_ge(wout_step, 8 * h + 8)
                    sp.sem_inc(held, 1)
                    sp.dma_start(wout_raw[:], w_out[bass.ds((h + 1) * P, P), :]).then_inc(wout_in, 16)

            with sp.Fori(0, SH - 1) as h:
                head(h, False)
            head(SH - 1, True)
            for p in range(2):
                sp.wait_ge(o_st[p], 16 * (SH * NCH // 2 + 1))
            sp.wait_ge(m_out, 16)

        @block.gpsimd
        def _(pool):
            identity(pool, ident[:], const, 0)
            pool.memset(zeros[:], 0.0).then_inc(const, 1)
            pool.memset(maskb[:], 0.0).then_inc(const, 1)
            pool.wait_ge(const, 4)
            pool.affine_select(out=maskb[:], in_=maskb[:], compare_op=ALU.is_gt, fill=-BIG, base=0,
                               pattern=[[-1, P]], channel_multiplier=1).then_inc(const, 1)
            pool.tensor_copy(identb[:], ident[:]).then_inc(const, 1)
            pool.memset(ones[:], 1.0).then_inc(g_const, 1)
            pool.memset(b_before[:], 0.0).then_inc(g_const, 1)
            pool.memset(mprev_row[:], 0.0).then_inc(g_const, 1)
            pool.wait_ge(ve_done, 1)
            with pool.Fori(0, SH) as h:
                def split_w_out(part):
                    cc = slice(part * (D // 4), (part + 1) * (D // 4))
                    whi, wlo = wout_hi[:, bass.ds(h, 1), cc], wout_lo[:, bass.ds(h, 1), cc]
                    raw = wout_raw[:, cc].unsqueeze(1)
                    pool.tensor_copy(whi, raw).then_inc(wout_step, 1)
                    pool.wait_ge(wout_step, 8 * h + (2 * part + 1))
                    pool.sem_inc(held, 1)
                    pool.tensor_tensor(wlo, raw, whi.bitcast(F32), ALU.subtract).then_inc(wout_step, 1)

                def finish_row(r):
                    c = NCH - 1 - r
                    o = osum[:, r % 2].rearrange("e (j t) -> e j t", j=TPC)
                    pool.wait_ge(sum_done, NCH * h + (r + 1 + SUM0))
                    pool.sem_inc(held, 1)
                    pool.tensor_tensor(o, o, v_e[:, bass.ds(h * NT + c * TPC, TPC)].unsqueeze(2).to_broadcast([SD, TPC, P]),
                                       ALU.add).then_inc(add_done, 1)
                    pool.wait_ge(add_done, NCH * h + (r + 1))
                    pool.sem_inc(held, 1)
                    pool.wait_ge(gate_in[r % 2], h * (16 * NCH // 2) + 16 * (r // 2 + 1))
                    pool.tensor_tensor(osum[:, r % 2], osum[:, r % 2], gate[:, r % 2], ALU.mult).then_inc(gated, 1)

                for k in range(N):
                    if by_pool(k):
                        t = lo_col(k)
                        pool.wait_ge(tile_done, NP * h + (pool_lows(k + 1) + TILE0))
                        pool.tensor_tensor(lo[:, k % 4, t:], tile[:, t:], hi[:, k % 4, t:].bitcast(F32), ALU.subtract).then_inc(pool_lo_done, 1)
                    for r in range(NCH):
                        if row_last[r] + 7 == k:
                            finish_row(r)
                    if k % (N // 4) == N // 4 - 5:
                        if k < N // 4:
                            pool.wait_ge(wout_in, 16 * h + 16)
                            pool.sem_inc(held, 1)
                        split_w_out(k // (N // 4))
                for r in range(NCH):
                    if row_last[r] + 7 >= N:
                        finish_row(r)

        @block.tensor
        def _(pe):
            pe.wait_ge(const, 6)
            pe.wait_ge(v_in, 16)
            for h in range(SH):
                last = pe.transpose(z[0][0:SD, h * NT:(h + 1) * NT], vrow[:, h * SD:(h + 1) * SD], ident[0:NT, 0:NT])
            last.then_inc(ve_tr, 1)
            pe.wait_ge(g_dve, 4)
            pe.transpose(acc[0][0:1, 0:P], b[:, P - 1:P], ident[:])
            pe.transpose(acc[0][0:1, P:2 * P], top[:, P - 1:P], ident[:]).then_inc(g_pe, 1)
            pe.transpose(rt[0][:, 0:P], u[:], ident[:])
            pe.transpose(rt[2][:, 0:P], b[:], ident[:]).then_inc(g_pe, 1)
            pe.wait_ge(g_dve, 11)
            row = lambda t: t[:].rearrange("a h c -> a (h c)")
            pe.matmul(acc[1][:, 2 * P:2 * P + 1], row(mprev_row), ones[0:1, 0:1], start=True, stop=True)
            pe.matmul(acc[1][:, 0:P], ones[0:1, :], row(mprev_row), start=True, stop=True)
            pe.matmul(acc[1][:, P:2 * P], ones[0:1, :], row(mlast_row), start=True, stop=True).then_inc(g_pe, 1)
            pe.wait_ge(g_dve, 14)
            pe.transpose(rt[1][:, 0:P], m[:], ident[:]).then_inc(g_pe, 1)
            pe.wait_ge(ve_done, 1)
            pe.wait_ge(g_dve, 20)
            pe.sem_inc(rt_done, RT0)
            pe.sem_inc(av_done, AV0)
            with pe.Fori(0, SH) as h:
                def scores(k):
                    n, r, c, j, q = STEPS[k]
                    if q == 0:
                        pe.wait_ge(chunk_in[j], h * 112 + 112)
                    pe.wait_ge(keep_done, N * h + (k + 1))
                    w, bank = width(k), z[k % ZB]
                    t, s = c * CH + q * P, slice(j * CH, j * CH + w)
                    pe.matmul(bank[:, 0:w], q_sb[:, t:t + P], khi[:, s], start=True, stop=False)
                    last = pe.matmul(bank[:, 0:w], q_sb[:, t:t + P], klo[:, s], start=False, stop=c != j)
                    if c == j:
                        last = pe.matmul(bank[:, q * P:w], identb[:], maskb[:], start=False, stop=True)
                    last.then_inc(z_done, 1)

                def turn(k):
                    n, r, c, j, q = STEPS[k]
                    if q == 0:
                        pe.wait_ge(scan_done, N * h + (4 * n + 4 + SCAN0))
                    before = k - RB
                    if by_pool(before):
                        pe.wait_ge(tile_done, NP * h + (pool_lows(before + 1) + TILE0))
                    else:
                        pe.wait_ge(lo_done, ND * h + (dve_lows(before + 1) + LO0))
                    for i in range(q if c == j else 0, TPC):
                        last = pe.transpose(rt[k % RB][:, i * P:(i + 1) * P], prod[:, n % PB, i, q * P:(q + 1) * P], ident[:])
                    last.then_inc(rt_done, 1)

                def weigh(k):
                    n, r, c, j, q = STEPS[k]
                    if c == j and q == 0:
                        pe.wait_ge(sum_done, NCH * h + (r + 1))
                    if by_pool(k):
                        pe.wait_ge(pool_lo_done, NP * h + pool_lows(k + 1))
                    else:
                        pe.wait_ge(lo_done, ND * h + (dve_lows(k + 1) + LO0))
                    t = lo_col(k)
                    w = dw[:, j * TPC + q, :]
                    pe.matmul(acc[r % 2][:, t:], w, hi[:, k % 4, t:], start=(c == j and q == 0), stop=False)
                    pe.matmul(acc[r % 2][:, t:], w, lo[:, k % 4, t:], start=False, stop=k == row_last[r]).then_inc(av_done, 1)

                for k in range(LEAD):
                    scores(k)
                for k in range(N + 3):
                    if k + LEAD < N:
                        scores(k + LEAD)
                    if k < N:
                        turn(k)
                    if k >= 3:
                        weigh(k - 3)

        @block.scalar
        def _(act):
            act.sem_inc(keep_done, KEEP0)
            act.sem_inc(tile_done, TILE0)
            act.preload_act_table_set("natural_log_exp_and_others")
            act.wait_ge(g_in, 32)
            act.activation(soft[:], fg[:], ACT.Abs).then_inc(g_act, 1)
            act.wait_ge(g_act, 1)
            act.activation(soft[:], soft[:], ACT.Exp, scale=-1.0).then_inc(g_act, 1)
            act.wait_ge(g_act, 2)
            act.activation(soft[:], soft[:], ACT.Ln, bias=1.0).then_inc(g_act, 1)
            act.wait_ge(ve_tr, 1)
            act.copy(v_e[:], z[0][0:SD, 0:SH * NT]).then_inc(ve_done, 1)
            act.wait_ge(g_dve, 20)
            act.activation(cols["wk"][:], xw[:], ACT.Exp).then_inc(g_act, 1)
            act.activation(cols["decay"][:], xs[:], ACT.Exp).then_inc(g_act, 1)
            act.activation(cols["floor"][:], xe[:], ACT.Exp, scale=-1.0).then_inc(g_act, 1)
            with act.Fori(0, SH) as h:
                def gate_of(k):
                    w = width(k)
                    act.wait_ge(z_done, N * h + (k + 1))
                    act.wait_ge(scan_done, N * h + (k + 1))
                    act.activation(keep[:, k % KB, 0:w], z[k % ZB][:, 0:w], ACT.Sigmoid, scale=-Z_SCALE).then_inc(keep_done, 1)

                def row_out(r):
                    act.wait_ge(av_done, N * h + (row_last[r] + 1 + AV0))
                    act.wait_ge(sum_done, NCH * h + (r + SUM0))
                    act.copy(lowsum[:], acc[r % 2][SD:P, :]).then_inc(low_done, 1)

                for k in range(LEAD):
                    gate_of(k)
                for k in range(N):
                    if k + LEAD < N:
                        gate_of(k + LEAD)
                    t = lo_col(k)
                    act.wait_ge(rt_done, N * h + (k + 1 + RT0))
                    act.wait_ge(av_done, N * h + (k + 1))
                    act.copy(hi[:, k % 4, t:], rt[k % RB][:, t:]).then_inc(hi_done, 1)
                    if by_pool(k):
                        act.copy(tile[:, t:], rt[k % RB][:, t:]).then_inc(tile_done, 1)
                    for r in range(NCH):
                        if row_last[r] + 4 == k:
                            row_out(r)
                row_out(NCH - 1)

        @block.vector
        def _(dve):
            dve.sem_inc(scan_done, SCAN0)
            dve.sem_inc(lo_done, LO0)
            dve.sem_inc(sum_done, SUM0)
            for p in range(2):
                dve.sem_inc(o_st[p], 16)
            dve.wait_ge(const, 6)
            dve.wait_ge(g_const, 3)
            dve.wait_ge(g_act, 3)
            dve.scalar_tensor_tensor(out=soft[:], in0=fg[:], scalar=0.0, in1=soft[:],
                                     op0=ALU.min, op1=ALU.subtract).then_inc(g_dve, 1)
            dve.wait_ge(g_dve, 1)
            dve.tensor_tensor_scan(b[:], ones[:], soft[:], 0.0, ALU.mult, ALU.add).then_inc(g_dve, 1)
            dve.wait_ge(g_dve, 2)
            dve.tensor_tensor(u[:], ig[:], b[:], ALU.subtract).then_inc(g_dve, 1)
            dve.wait_ge(g_dve, 3)
            dve.tensor_tensor_scan(top[:], zeros[:, 0:P], u[:], -3.0e38, ALU.add, ALU.max).then_inc(g_dve, 1)
            dve.wait_ge(g_pe, 1)
            sums, maxima = (acc[0][0:1, q * P:(q + 1) * P].rearrange("a (h c) -> a h c", h=MH) for q in range(2))
            dve.tensor_copy(b_before[:, :, 1:NT], sums[:, :, 0:NT - 1]).then_inc(g_dve, 1)
            dve.tensor_copy(tops[:], maxima).then_inc(g_dve, 1)
            dve.wait_ge(g_dve, 6)
            for h in range(MH):
                dve.tensor_tensor_scan(mlast_row[:, h], b_before[:, h], tops[:, h], 0.0, ALU.add, ALU.max).then_inc(g_dve, 1)
            dve.wait_ge(g_dve, 10)
            dve.tensor_tensor(mprev_row[:, :, 1:NT], mlast_row[:, :, 0:NT - 1], b_before[:, :, 1:NT], ALU.add).then_inc(g_dve, 1)
            dve.wait_ge(g_pe, 3)
            dve.tensor_copy(mcol_in[:], acc[1][:, 2 * P:2 * P + 1]).then_inc(g_dve, 1)
            dve.tensor_copy(cols["mprev"][:], acc[1][:, 0:P].rearrange("p (h c) -> p h c", h=MH)).then_inc(g_dve, 1)
            dve.wait_ge(g_dve, 12)
            dve.tensor_scalar(m[:], top[:], mcol_in[:], None, ALU.max).then_inc(g_dve, 1)
            by_chunk = lambda t: t.rearrange("p (h c) -> p c h", h=MH)
            dve.tensor_copy(mlast[:], acc[1][:, P:2 * P].rearrange("p (h c) -> p h c", h=MH)).then_inc(g_dve, 1)
            dve.tensor_copy(cols["u"][:], by_chunk(rt[0][:, 0:P])).then_inc(g_dve, 1)
            dve.wait_ge(g_dve, 15)
            dve.tensor_tensor(xw[:], by_chunk(rt[0][:, 0:P]), mlast[:].rearrange("p h c -> p c h"), ALU.subtract).then_inc(g_dve, 1)
            dve.tensor_tensor(xs[:].rearrange("p c h -> p h c"), cols["mprev"][:], mlast[:], ALU.subtract).then_inc(g_dve, 1)
            dve.wait_ge(g_pe, 4)
            dve.tensor_copy(mcol[:], by_chunk(rt[1][:, 0:P])).then_inc(g_dve, 1)
            dve.wait_ge(g_dve, 19)
            dve.tensor_tensor(xe[:], by_chunk(rt[2][:, 0:P]), mcol[:], ALU.add).then_inc(g_dve, 1)
            with dve.Fori(0, SH) as h:
                def scan(k):
                    n, r, c, j, q = STEPS[k]
                    w = width(k)
                    dve.wait_ge(keep_done, N * h + (k + 1 + KEEP0))
                    dve.wait_ge(rt_done, N * h + (TPC * (n - PB + 1) + RT0))
                    first = 1.0
                    if c != j:
                        dve.wait_ge(scan_done, N * h + (k - 4 + 1 + SCAN0))
                        first = prod[:, (n - 1) % PB, q, 0:1]
                    dve.tensor_tensor_scan(prod[:, n % PB, q, 0:w][:, ::-1], keep[:, k % KB, 0:w][:, ::-1], zeros[:, 0:w],
                                           first, ALU.mult, ALU.add).then_inc(scan_done, 1)

                def row_out(r):
                    dve.wait_ge(low_done, NCH * h + (r + 1))
                    dve.wait_ge(o_st[r % 2], h * (16 * NCH // 2) + 16 * (r // 2 + 1))
                    dve.tensor_tensor(osum[:, r % 2], acc[r % 2][0:SD, :], lowsum[:], ALU.add).then_inc(sum_done, 1)

                for k in range(LEAD):
                    scan(k)
                for k in range(N):
                    if k + LEAD < N:
                        scan(k + LEAD)
                    t = lo_col(k)
                    if not by_pool(k):
                        dve.wait_ge(hi_done, N * h + (k + 1))
                        dve.tensor_tensor(lo[:, k % 4, t:], rt[k % RB][:, t:], hi[:, k % 4, t:].bitcast(F32), ALU.subtract).then_inc(lo_done, 1)
                    for r in range(NCH):
                        if row_last[r] + 4 == k:
                            row_out(r)
                row_out(NCH - 1)


def stage_mix(nc, d, cols, x, whi, wlo, gg_d, y):
    VW = MD + 1
    with ExitStack() as ctx:
        sb = lambda n, s, dt=F32: ctx.enter_context(nc.sbuf_tensor("m_" + n, s, dt))
        ps = lambda n, s, dt=F32: ctx.enter_context(nc.psum_tensor("mp_" + n, s, dt))
        sem = lambda n: ctx.enter_context(nc.semaphore("m_" + n))
        ggb = sb("ggb", [P, D])
        ident, maskb = sb("ident", [P, P]), sb("maskb", [P, P])
        qT, kT, mb = (sb(n, [P, 2, MH, P]) for n in ("qT", "kT", "mb"))
        v = sb("v", [P, 2, MH, VW])
        so, szg = sb("so", [P, 2, MH, MD]), sb("szg", [P, 2, MH, MD])
        sbt, xt, ot = sb("sbt", [P, 2, MH, P]), sb("xt", [P, 2, D]), sb("ot", [P, 2, D])
        gap, dwt = sb("gap", [P, MH, P]), sb("dwt", [P, MH, P])
        wq, qs, pm, kn = (sb(n, [P, MH, P]) for n in ("wq", "qs", "pm", "kn"))
        state = sb("state", [P, MH, VW])
        dneg, den, rden = (sb(n, [P, MH]) for n in ("dneg", "den", "rden"))
        hp, hf = sb("hp", [P, MH, MD]), sb("hf", [P, MH, MD])
        sq, sqy = sb("sq", [P, MH, MD], BF16), sb("sqy", [P, 2, CH], BF16)
        yt = sb("yt", [P, 2, CH])
        ss, sv, sl, s0, s1, s2, s3 = (sb(n, [P, MH]) for n in ("ss", "sv", "sl", "s0", "s1", "s2", "s3"))
        ys, yv, yl, y0, y1, y2, y3 = (sb(n, [P, 2]) for n in ("ys", "yv", "yl", "y0", "y1", "y2", "y3"))
        shi, slo = sb("shi", [P, 2, MH, P], F32R), sb("slo", [P, 2, MH, P], F32R)
        mhi, mlo = sb("mhi", [P, MH, P], F32R), sb("mlo", [P, MH, P], F32R)
        t_ps, s_ps = ps("t", [P, MH, P]), ps("s", [P, MH, P])
        n_ps = [ps(f"n{k}", [P, 2, VW]) for k in range(2)]
        u_ps = [ps(f"u{k}", [P, 2, VW]) for k in range(2)]
        y_ps = [ps(f"y{k}", [P, CH]) for k in range(2)]

        names = ("const c_in k_tr s_done gap_done dwt_done wq_done qs_done pm_done kn_done n_done u_done "
                 "state_done den_step hp_done sq_done sv_done sr_done s_step hf_done h_tr mhi_done mlo_done shi_done slo_done "
                 "held y_done yc_done ysq_done yv_done yr_done y_step o_done fin_done").split()
        e = {n: sem(n) for n in names}
        ch_in, x_in, out_st = ([sem(f"{n}{p}") for p in range(2)] for n in ("ch_in", "x_in", "out_st"))
        block = ctx.enter_context(nc.Block())

        def after(eng, semaphore, value):
            if not isinstance(value, int) or value > 0:
                eng.wait_ge(semaphore, value)

        def over_chunks(eng, body, ahead):
            body(0, 0, 0)
            body(1, 0, 1)
            pairs = (NT - 2 - ahead) // 2
            with eng.Fori(0, pairs) as i:
                for p in range(2):
                    body(2 * i + (2 + p), i + 1, p)
            for c in range(2 + 2 * pairs, NT):
                body(c, c // 2, c % 2)

        @block.sync
        def _(sp):
            def load(c, p):
                dst = [(qT, d["mlq"][c]), (kT, d["mlk"][c])]
                for tile, src in dst:
                    sp.dma_start(tile[:, p], src).then_inc(ch_in[p], 16)
                rows = slice(c * P, (c + 1) * P) if isinstance(c, int) else bass.ds(c * P, P)
                sp.dma_start(v[:, p, :, 0:MD], d["v"][rows, :].rearrange("t (h e) -> t h e", h=MH)).then_inc(ch_in[p], 16)
                sp.dma_start(so[:, p], d["so"][rows, :].rearrange("t (h e) -> t h e", h=MH)).then_inc(ch_in[p], 16)
                sp.dma_start(szg[:, p], d["szg"][rows, :].rearrange("t (h e) -> t h e", h=MH)).then_inc(ch_in[p], 16)
                sp.dma_start(mb[:, p], d["m"][:, rows].unsqueeze(0).to_broadcast([P, MH, P])).then_inc(ch_in[p], 16)
                sp.dma_start(sbt[:, p], d["hsb"][c].rearrange("(k p) t -> p k t", p=P)).then_inc(ch_in[p], 16)

            def load_x(c, p):
                rows = slice(c * P, (c + 1) * P) if isinstance(c, int) else bass.ds(c * P, P)
                sp.dma_start(xt[:, p], x[0, rows, :]).then_inc(x_in[p], 16)

            load(0, 0)
            load_x(0, 0)
            load_x(1, 1)
            sp.dma_start(ggb[:], gg_d.to_broadcast([P, D])).then_inc(e["c_in"], 16)

            def store(c, p):
                after(sp, e["fin_done"], c + 1)
                rows = slice(c * P, (c + 1) * P) if isinstance(c, int) else bass.ds(c * P, P)
                sp.sem_inc(e["held"], 1)
                sp.dma_start(y[0, rows, :], ot[:, p]).then_inc(out_st[p], 16)

            def body(c, half, p):
                last = isinstance(c, int) and c == NT - 1
                if not last:
                    after(sp, e["hf_done"], MH * c)
                    after(sp, e["slo_done"], c)
                    after(sp, e["state_done"], MH * (c + 1))
                    sp.sem_inc(e["held"], 1)
                    load(c + 1, 1 - p)
                if not isinstance(c, int) or c >= 2:
                    store(c - 2, p)
                    load_x(c, p)

            over_chunks(sp, body, 2)
            store(NT - 2, 0)
            store(NT - 1, 1)
            for p in range(2):
                sp.wait_ge(out_st[p], 16 * (NT // 2 + 1))

        @block.gpsimd
        def _(pool):
            identity(pool, ident[:], e["const"], 0)
            pool.memset(maskb[:], 0.0).then_inc(e["const"], 1)
            pool.wait_ge(e["const"], 3)
            pool.affine_select(out=maskb[:], in_=maskb[:], compare_op=ALU.is_ge, fill=BIG, base=0,
                               pattern=[[1, P]], channel_multiplier=-1).then_inc(e["const"], 1)
            pool.memset(v[:, :, :, MD:VW], 1.0).then_inc(e["const"], 1)
            pool.memset(state[:], 0.0).then_inc(e["state_done"], MH)

            def body(c, half, p):
                after(pool, ch_in[p], 112 * half + 112)
                after(pool, e["wq_done"], MH * (c + 1))
                after(pool, e["n_done"], c)
                pool.tensor_tensor(qs[:], qT[:, p], wq[:], ALU.mult).then_inc(e["qs_done"], 1)
                if not isinstance(c, int) or c >= 2:
                    add_x(c - 2, half, p)
                after(pool, e["shi_done"], c + 1)
                pool.tensor_tensor(slo[:, p], sbt[:, p], shi[:, p].bitcast(F32), ALU.subtract).then_inc(e["slo_done"], 1)

            def add_x(c, loads, p):
                pool.wait_ge(x_in[p], 16 * loads)
                pool.wait_ge(e["o_done"], 2 * c + 2)
                pool.tensor_tensor(ot[:, p], ot[:, p], xt[:, p], ALU.add).then_inc(e["fin_done"], 1)

            over_chunks(pool, body, 0)
            for c in (NT - 2, NT - 1):
                add_x(c, NT // 2, c % 2)

        @block.tensor
        def _(pe):
            pe.wait_ge(e["const"], 5)

            def turn_and_score(c, half, p):
                after(pe, ch_in[p], 112 * half + 112)
                after(pe, e["mlo_done"], c - 1)
                for h in range(MH):
                    last = pe.transpose(t_ps[:, h], kT[:, p, h], ident[:])
                last.then_inc(e["k_tr"], 1)
                after(pe, e["pm_done"], c)
                for h in range(MH):
                    last = pe.matmul(s_ps[:, h], kT[:, p, h], qT[:, p, h], start=True, stop=True)
                last.then_inc(e["s_done"], 1)

            def project(ks, parts, nb):
                for k in ks:
                    hi, lo = parts[0][:, k % MH], parts[1][:, k % MH]
                    cc = slice(nb * CH, (nb + 1) * CH)
                    for q, (a, b) in enumerate(((hi, whi), (hi, wlo), (lo, whi))):
                        last = pe.matmul(y_ps[nb][:], a, b[:, k, cc], start=(k == MH and q == 0), stop=(k == MH - 1 and q == 2))
                return last

            def project_sb(c, p):
                after(pe, e["slo_done"], c + 1)
                for nb in range(2):
                    after(pe, e["yc_done"], 2 * c - 1 + nb)
                    project(range(MH, KT), (shi[:, p], slo[:, p]), nb)

            def turn_h(c):
                after(pe, e["hf_done"], MH * (c + 1))
                after(pe, e["kn_done"], MH * (c + 2 if not (isinstance(c, int) and c == NT - 1) else c + 1))
                for h in range(MH):
                    last = pe.transpose(t_ps[:, h], hf[:, h], ident[:])
                last.then_inc(e["h_tr"], 1)

            def project_ml(c, p):
                after(pe, e["mlo_done"], c + 1)
                for nb in range(2):
                    project(range(MH), (mhi, mlo), nb).then_inc(e["y_done"], 1)

            def recur(c, p):
                after(pe, e["pm_done"], c + 1)
                after(pe, e["qs_done"], c + 1)
                after(pe, e["state_done"], MH * (c + 1))
                after(pe, e["hp_done"], MH * c)
                for h in range(MH):
                    dst = n_ps[h // 2][:, h % 2]
                    pe.matmul(dst, pm[:, h], v[:, p, h], start=(h % 2 == 0), stop=False, skip_group_check=True)
                    last = pe.matmul(dst, qs[:, h], state[:, h], start=False, stop=(h % 2 == 1), skip_group_check=True)
                last.then_inc(e["n_done"], 1)
                after(pe, e["kn_done"], MH * (c + 1))
                for h in range(MH):
                    last = pe.matmul(u_ps[h // 2][:, h % 2], kn[:, h], v[:, p, h], start=True, stop=True)
                last.then_inc(e["u_done"], 1)

            def body(c, half, p):
                turn_and_score(c, half, p)
                first = isinstance(c, int) and c == 0
                if not first:
                    project_sb(c - 1, 1 - p)
                    turn_h(c - 1)
                recur(c, p)
                if not first:
                    project_ml(c - 1, 1 - p)

            body(0, 0, 0)
            body(1, 0, 1)
            with pe.Fori(0, NT // 2 - 1) as i:
                for p in range(2):
                    body(2 * i + (2 + p), i + 1, p)
            project_sb(NT - 1, 1)
            turn_h(NT - 1)
            project_ml(NT - 1, 1)

        @block.scalar
        def _(act):
            def split_h(c):
                after(act, e["h_tr"], c + 1)
                after(act, e["y_done"], 2 * c)
                act.copy(mhi[:], t_ps[:]).then_inc(e["mhi_done"], 1)

            def out_y(c):
                after(act, e["o_done"], 2 * c)
                for nb in range(2):
                    after(act, e["y_done"], 2 * c + 1 + nb)
                    act.copy(yt[:, nb], y_ps[nb][:]).then_inc(e["yc_done"], 1)
                after(act, e["yv_done"], c)
                for nb in range(2):
                    after(act, e["yc_done"], 2 * c + 1 + nb)
                    act.activation(sqy[:, nb], yt[:, nb], ACT.Square, accum_out=ys[:, nb:nb + 1]).then_inc(e["ysq_done"], 1)
                after(act, e["yv_done"], c + 1)
                act.activation(yl[:, 0:1], yv[:, 0:1], ACT.Ln).then_inc(e["yr_done"], 1)
                after(act, e["yr_done"], 2 * c + 1)
                act.activation(y0[:, 0:1], yl[:, 0:1], ACT.Exp, scale=-0.5).then_inc(e["yr_done"], 1)

            def body(c, half, p):
                dyn = (lambda t, h: t[:, c, h:h + 1]) if isinstance(c, int) else (lambda t, h: t[:, bass.ds(c, 1), h])
                dynm = (lambda t, h: t[:, h, c:c + 1]) if isinstance(c, int) else (lambda t, h: t[:, h, bass.ds(c, 1)])
                after(act, e["k_tr"], c + 1)
                after(act, e["u_done"], c)
                act.sem_inc(e["held"], 1)
                for h in range(MH):
                    act.activation(kn[:, h], t_ps[:, h], ACT.Copy, scale=dyn(cols["wk"], h)).then_inc(e["kn_done"], 1)
                after(act, ch_in[p], 112 * half + 112)
                after(act, e["qs_done"], c)
                act.sem_inc(e["held"], 1)
                for h in range(MH):
                    act.activation(wq[:, h], mb[:, p, h], ACT.Exp, scale=-1.0, bias=dynm(cols["mprev"], h)).then_inc(e["wq_done"], 1)
                after(act, e["gap_done"], MH * (c + 1))
                after(act, e["pm_done"], c)
                act.activation(dwt[:], gap[:], ACT.Exp, scale=-1.0).then_inc(e["dwt_done"], 1)
                after(act, e["y_done"], 2 * (c - 1))
                act.copy(shi[:, p], sbt[:, p]).then_inc(e["shi_done"], 1)
                first = isinstance(c, int) and c == 0
                if not first:
                    split_h(c - 1)
                after(act, e["hp_done"], MH * (c + 1))
                after(act, e["sv_done"], c)
                for h in range(MH):
                    act.activation(sq[:, h], hp[:, h], ACT.Square, accum_out=ss[:, h:h + 1]).then_inc(e["sq_done"], 1)
                after(act, e["sv_done"], c + 1)
                act.activation(sl[:], sv[:], ACT.Ln).then_inc(e["sr_done"], 1)
                after(act, e["sr_done"], 2 * c + 1)
                act.activation(s0[:], sl[:], ACT.Exp, scale=-0.5).then_inc(e["sr_done"], 1)
                if not first:
                    out_y(c - 1)

            act.preload_act_table_set("natural_log_exp_and_others")
            body(0, 0, 0)
            body(1, 0, 1)
            with act.Fori(0, NT // 2 - 1) as i:
                for p in range(2):
                    body(2 * i + (2 + p), i + 1, p)
            split_h(NT - 1)
            out_y(NT - 1)

        @block.vector
        def _(dve):
            for p in range(2):
                dve.sem_inc(out_st[p], 16)
            dve.wait_ge(e["c_in"], 16)
            dve.wait_ge(e["const"], 4)

            def newton(step, base, r0, var, t1, t2, r, n):
                dve.tensor_tensor(t1[:, 0:n], r0[:, 0:n], r0[:, 0:n], ALU.mult).then_inc(step, 1)
                dve.wait_ge(step, base + 1)
                dve.tensor_tensor(t2[:, 0:n], t1[:, 0:n], var[:, 0:n], ALU.mult).then_inc(step, 1)
                dve.wait_ge(step, base + 2)
                dve.tensor_scalar(t1[:, 0:n], t2[:, 0:n], -0.5, 1.5, ALU.mult, ALU.add).then_inc(step, 1)
                dve.wait_ge(step, base + 3)
                dve.tensor_tensor(r[:, 0:n], r0[:, 0:n], t1[:, 0:n], ALU.mult).then_inc(step, 1)
                dve.wait_ge(step, base + 4)

            def low_h(c):
                after(dve, e["mhi_done"], c + 1)
                dve.tensor_tensor(mlo[:], t_ps[:], mhi[:].bitcast(F32), ALU.subtract).then_inc(e["mlo_done"], 1)

            def norm_y(c, p, stored):
                after(dve, e["ysq_done"], 2 * c + 2)
                dve.tensor_tensor(y1[:, 0:1], ys[:, 0:1], ys[:, 1:2], ALU.add).then_inc(e["y_step"], 1)
                dve.wait_ge(e["y_step"], 5 * c + 1)
                dve.tensor_scalar(yv[:, 0:1], y1[:, 0:1], 1.0 / D, EPS, ALU.mult, ALU.add).then_inc(e["yv_done"], 1)
                after(dve, e["yr_done"], 2 * c + 2)
                newton(e["y_step"], 5 * c + 1, y0, yv, y1, y2, y3, 1)
                after(dve, out_st[p], stored)
                for nb in range(2):
                    cc = slice(nb * CH, (nb + 1) * CH)
                    dve.scalar_tensor_tensor(out=ot[:, p, cc], in0=yt[:, nb], scalar=y3[:, 0:1], in1=ggb[:, cc],
                                             op0=ALU.mult, op1=ALU.mult).then_inc(e["o_done"], 1)

            def body(c, half, p):
                dyn = (lambda t, h: t[:, c, h:h + 1]) if isinstance(c, int) else (lambda t, h: t[:, bass.ds(c, 1), h])
                first = isinstance(c, int) and c == 0
                after(dve, ch_in[p], 112 * half + 112)
                after(dve, e["dwt_done"], c)
                for h in range(MH):
                    dve.scalar_tensor_tensor(out=gap[:, h], in0=mb[:, p, h], scalar=dyn(cols["u"], h), in1=maskb[:],
                                             op0=ALU.subtract, op1=ALU.max).then_inc(e["gap_done"], 1)
                if not isinstance(c, int) or c >= 2:
                    norm_y(c - 2, p, 16 * half)
                after(dve, e["dwt_done"], c + 1)
                after(dve, e["s_done"], c + 1)
                after(dve, e["n_done"], c)
                dve.tensor_tensor(pm[:], s_ps[:], dwt[:], ALU.mult).then_inc(e["pm_done"], 1)
                if not first:
                    low_h(c - 1)
                after(dve, e["n_done"], c + 1)
                for b in range(2):
                    fl = cols["floor"][:, c, 2 * b:2 * b + 2] if isinstance(c, int) else cols["floor"][:, bass.ds(c, 1), 2 * b:2 * b + 2].rearrange("p a h -> p (a h)")
                    dve.scalar_tensor_tensor(out=dneg[:, 2 * b:2 * b + 2], in0=n_ps[b][:, :, MD], scalar=-1.0, in1=fl,
                                             op0=ALU.mult, op1=ALU.max).then_inc(e["den_step"], 1)
                dve.wait_ge(e["den_step"], 5 * c + 2)
                for b in range(2):
                    dve.tensor_tensor(den[:, 2 * b:2 * b + 2], n_ps[b][:, :, MD], dneg[:, 2 * b:2 * b + 2],
                                      ALU.max).then_inc(e["den_step"], 1)
                dve.wait_ge(e["den_step"], 5 * c + 4)
                dve.reciprocal(rden[:], den[:]).then_inc(e["den_step"], 1)
                dve.wait_ge(e["den_step"], 5 * c + 5)
                for h in range(MH):
                    dve.scalar_tensor_tensor(out=hp[:, h], in0=n_ps[h // 2][:, h % 2, 0:MD], scalar=rden[:, h:h + 1], in1=so[:, p, h],
                                             op0=ALU.mult, op1=ALU.mult).then_inc(e["hp_done"], 1)
                after(dve, e["u_done"], c + 1)
                for h in range(MH):
                    dve.scalar_tensor_tensor(out=state[:, h], in0=state[:, h], scalar=dyn(cols["decay"], h), in1=u_ps[h // 2][:, h % 2],
                                             op0=ALU.mult, op1=ALU.add).then_inc(e["state_done"], 1)
                after(dve, e["sq_done"], MH * (c + 1))
                dve.tensor_scalar(sv[:], ss[:], 1.0 / MD, EPS, ALU.mult, ALU.add).then_inc(e["sv_done"], 1)
                after(dve, e["sr_done"], 2 * c + 2)
                newton(e["s_step"], 4 * c, s0, sv, s1, s2, s3, MH)
                after(dve, e["h_tr"], c)
                for h in range(MH):
                    dve.scalar_tensor_tensor(out=hf[:, h], in0=hp[:, h], scalar=s3[:, h:h + 1], in1=szg[:, p, h],
                                             op0=ALU.mult, op1=ALU.mult).then_inc(e["hf_done"], 1)

            body(0, 0, 0)
            body(1, 0, 1)
            with dve.Fori(0, NT // 2 - 1) as i:
                for p in range(2):
                    body(2 * i + (2 + p), i + 1, p)
            norm_y(NT - 2, 0, 16 * NT // 2)
            low_h(NT - 1)
            norm_y(NT - 1, 1, 16 * NT // 2)


def program(nc, x, c, w_ada, b_ada, g_pre, w_in, b_igate, b_fgate, conv_w, conv_b, g_ml_head, w_out, g_post, y):
    def scratch(name, *shape):
        return nc.dram_tensor("scratch_" + name, shape, F32, kind="Internal").ap()

    hT_d = scratch("hT", NCH + 2, P, KT * CH)
    gg_d = scratch("gg", 1, D)
    d = dict(mlq=scratch("mlq", NT, P, MH, P), mlk=scratch("mlk", NT, P, MH, P),
             v=scratch("v", S, 512), so=scratch("so", S, 512), szg=scratch("szg", S, 512),
             sbv=scratch("sbv", S + 1, 512), sbz=scratch("sbz", 512, S), gates=scratch("gates", 8, S),
             sqh=scratch("sqh", 512, S), sql=scratch("sql", 512, S), skh=scratch("skh", 512, S), skl=scratch("skl", 512, S),
             dw=scratch("dw", SH, NCH, P, TPC, P), hsb=scratch("hsb", NT, 512, P), m=scratch("m", MH, S))
    with ExitStack() as ctx:
        with ExitStack() as first:
            kept = norm_tiles(nc, first)
            stage_modulate(nc, x, c, w_ada, b_ada, g_pre, kept)
            weights = [ctx.enter_context(nc.sbuf_tensor("p_" + n, [P, KT, D], dt)) for n, dt in (("wraw", F32), ("whi", F32R), ("wlo", F32R))]
            stage_norm(nc, x, w_ada, b_ada, g_post, w_in, kept, weights, hT_d, gg_d)
        stage_project(nc, w_in, b_igate, b_fgate, conv_w, conv_b, g_ml_head, weights, hT_d, d)
    with ExitStack() as ctx:
        cols = {k: ctx.enter_context(nc.sbuf_tensor("c_" + k, [P, NT, MH], F32)) for k in ("u", "wk", "decay", "floor")}
        cols["mprev"] = ctx.enter_context(nc.sbuf_tensor("c_mprev", [P, MH, NT], F32))
        wout_hi, wout_lo = (ctx.enter_context(nc.sbuf_tensor("c_" + k, [P, KT, D], F32R)) for k in ("wout_hi", "wout_lo"))
        stage_attend(nc, d, cols, wout_hi, wout_lo, w_out)
        stage_mix(nc, d, cols, x, wout_hi, wout_lo, gg_d, y)


def kernel(x, c, w_ada, b_ada, g_pre, w_in, b_igate, b_fgate, conv_w, conv_b, g_ml_head, w_out, g_post):
    import numpy as np
    import concourse.bacc as bacc
    from concourse.bass_utils import run_bass_kernel_spmd as run

    nc = bacc.Bacc("TRN2", target_bir_lowering=False, num_devices=1)
    given = dict(x=x, c=c, w_ada=w_ada, b_ada=b_ada, g_pre=g_pre, w_in=w_in, b_igate=b_igate, b_fgate=b_fgate,
                 conv_w=conv_w, conv_b=conv_b, g_ml_head=g_ml_head, w_out=w_out, g_post=g_post)
    arrays = {"in_" + k: np.ascontiguousarray(a) for k, a in given.items()}
    aps = [nc.dram_tensor(k, a.shape, F32, kind="ExternalInput").ap() for k, a in arrays.items()]
    y = nc.dram_tensor("out_y", (1, S, D), F32, kind="ExternalOutput").ap()
    program(nc, *aps, y)
    return run(nc, [arrays], core_ids=[0]).results[0]["out_y"]
```
